# Optimizing a Trainium2 kernel written in Bass

```python
import numpy as np
import jax, jax.numpy as jnp
from jax import lax

D_MODEL = 2048
BATCH = 1
SEQ = 256
DEPTH = 1

EPS = 1e-6
N_BRANCHES = 3
DSA_HEADS = 16
DSA_HEAD_DIM = 128
DSA_KV_RANK = 512
DSA_SCALE = DSA_HEAD_DIM ** -0.5
IDX_HEADS = 16
IDX_HEAD_DIM = 128
IDX_SCALE = IDX_HEAD_DIM ** -0.5
IDX_W_SCALE = IDX_HEADS ** -0.5
DSA_TOPK_MAX = 256
Q_BLOCK = 128
SSD_EXPAND = 2
SSD_INNER = SSD_EXPAND * D_MODEL
SSD_HEAD_DIM = 64
SSD_HEADS = SSD_INNER // SSD_HEAD_DIM
SSD_GROUPS = 8
SSD_STATE = 128
SSD_CONV = 4
SSD_CHUNK = 128
MEM_LEN = 256
MEM_HEADS = 4
MEM_HEAD_DIM = 512
FFN_DIM = 5632
FFN_CONV = 3

DSA_Q_COLS = DSA_HEADS * DSA_HEAD_DIM
IDX_Q_COLS = IDX_HEADS * IDX_HEAD_DIM
SSD_BC_COLS = SSD_GROUPS * SSD_STATE
SSD_XBC_COLS = SSD_INNER + 2 * SSD_BC_COLS
MEM_COLS = MEM_HEADS * MEM_HEAD_DIM
GATE_COLS = N_BRANCHES * D_MODEL
IN_SPLITS = (DSA_Q_COLS, DSA_KV_RANK, IDX_Q_COLS, IDX_HEAD_DIM, IDX_HEADS,
             SSD_INNER, SSD_XBC_COLS, SSD_HEADS, MEM_COLS, GATE_COLS)
IN_COLS = sum(IN_SPLITS)

kernel_name = 'hybrid_dsa_ssd_memxattn_convffn_layer'

def rmsnorm(x, g):
    xf = x.astype(jnp.float32)
    y = xf * lax.rsqrt(jnp.mean(xf * xf, axis=-1, keepdims=True) + EPS)
    return (y * g.astype(jnp.float32)).astype(x.dtype)

def split_cols(a, sizes):
    offs = np.cumsum(sizes)[:-1].tolist()
    return jnp.split(a, offs, axis=-1)

def causal_dwconv(x, w, b):
    K, C = w.shape
    y = lax.conv_general_dilated(x, w[:, None, :].astype(x.dtype), window_strides=(1,),
                                 padding=[(K - 1, 0)], dimension_numbers=('NWC', 'WIO', 'NWC'),
                                 feature_group_count=C)
    return y + b.astype(x.dtype)

def dsa_attention(q, c_kv, q_idx, k_idx, w_idx, w_uk, w_uv):
    B, S = q.shape[0], q.shape[1]
    topk = min(DSA_TOPK_MAX, S // 4)
    nb = S // Q_BLOCK
    key_pos = jnp.arange(S)

    def to_blocks(a):
        return jnp.moveaxis(a.reshape((B, nb, Q_BLOCK) + a.shape[2:]), 1, 0)

    def block(args):
        qb, qib, wb, start = args
        qpos = start + jnp.arange(Q_BLOCK)
        causal = key_pos[None, :] <= qpos[:, None]
        logits = jnp.einsum('bqhd,bsd->bqhs', qib, k_idx).astype(jnp.float32) * IDX_SCALE
        score = jnp.einsum('bqhs,bqh->bqs', jax.nn.relu(logits),
                           wb.astype(jnp.float32) * IDX_W_SCALE)
        score = jnp.where(causal[None], score, -jnp.inf)
        _, sel = lax.top_k(score, topk)
        valid = sel <= qpos[None, :, None]
        c_sel = jax.vmap(lambda c, i: c[i])(c_kv, sel)
        q_lat = jnp.einsum('bqhd,hdr->bqhr', qb, w_uk)
        s = jnp.einsum('bqhr,bqkr->bqhk', q_lat, c_sel).astype(jnp.float32) * DSA_SCALE
        s = jnp.where(valid[:, :, None, :], s, -jnp.inf)
        p = jax.nn.softmax(s, axis=-1).astype(qb.dtype)
        o_lat = jnp.einsum('bqhk,bqkr->bqhr', p, c_sel)
        return jnp.einsum('bqhr,hrd->bqhd', o_lat, w_uv)

    starts = jnp.arange(nb, dtype=jnp.int32) * Q_BLOCK
    out = lax.map(block, (to_blocks(q), to_blocks(q_idx), to_blocks(w_idx), starts))
    return jnp.moveaxis(out, 0, 1).reshape(B, S, -1)

def ssd_scan(x, dt, A, Bm, Cm):
    Bsz, L, H, P = x.shape
    G, N = Bm.shape[2], Bm.shape[3]
    K = H // G
    Q = SSD_CHUNK
    nc = L // Q
    xc = (x * dt[..., None]).reshape(Bsz, nc, Q, G, K, P)
    a = jnp.moveaxis((dt * A).reshape(Bsz, nc, Q, G, K), 2, -1)
    a_cum = jnp.cumsum(a, axis=-1)
    Bc = Bm.reshape(Bsz, nc, Q, G, N)
    Cc = Cm.reshape(Bsz, nc, Q, G, N)
    tri = jnp.tril(jnp.ones((Q, Q), dtype=bool))
    seg = a_cum[..., :, None] - a_cum[..., None, :]
    decay = jnp.exp(jnp.where(tri, seg, -jnp.inf))
    cb = jnp.einsum('bclgn,bcsgn->bcgls', Cc, Bc)
    y_diag = jnp.einsum('bcgls,bcgkls,bcsgkp->bclgkp', cb, decay, xc)
    decay_states = jnp.exp(a_cum[..., -1:] - a_cum)
    states = jnp.einsum('bcsgn,bcgks,bcsgkp->bcgkpn', Bc, decay_states, xc)
    chunk_decay = jnp.exp(a_cum[..., -1])

    def step(h, inp):
        s_c, d_c = inp
        return h * d_c[..., None, None] + s_c, h

    h0 = jnp.zeros((Bsz, G, K, P, N), dtype=x.dtype)
    _, prev = lax.scan(step, h0, (jnp.moveaxis(states, 1, 0), jnp.moveaxis(chunk_decay, 1, 0)))
    prev = jnp.moveaxis(prev, 0, 1)
    y_off = jnp.einsum('bclgn,bcgkpn,bcgkl->bclgkp', Cc, prev, jnp.exp(a_cum))
    return (y_diag + y_off).reshape(Bsz, L, H, P)

def ssd_mixer(z, xbc, dt_raw, conv_w, conv_b, dt_bias, a_log, d_skip, norm_g):
    B, L = z.shape[0], z.shape[1]
    dtype = z.dtype
    xbc = jax.nn.silu(causal_dwconv(xbc, conv_w, conv_b))
    xs, Bm, Cm = split_cols(xbc, (SSD_INNER, SSD_BC_COLS, SSD_BC_COLS))
    xh = xs.reshape(B, L, SSD_HEADS, SSD_HEAD_DIM).astype(jnp.float32)
    Bm = Bm.reshape(B, L, SSD_GROUPS, SSD_STATE).astype(jnp.float32)
    Cm = Cm.reshape(B, L, SSD_GROUPS, SSD_STATE).astype(jnp.float32)
    dt = jax.nn.softplus(dt_raw.astype(jnp.float32) + dt_bias.astype(jnp.float32))
    A = -jnp.exp(a_log.astype(jnp.float32))
    y = ssd_scan(xh, dt, A, Bm, Cm) + d_skip.astype(jnp.float32)[:, None] * xh
    y = y.reshape(B, L, SSD_INNER) * jax.nn.silu(z.astype(jnp.float32))
    yg = y.reshape(B, L, SSD_GROUPS, SSD_INNER // SSD_GROUPS)
    yg = yg * lax.rsqrt(jnp.mean(yg * yg, axis=-1, keepdims=True) + EPS)
    return (yg.reshape(B, L, SSD_INNER) * norm_g.astype(jnp.float32)).astype(dtype)

def memory_cross_attention(q, mem, mem_norm_g, w_mem_k, w_mem_v):
    B, S = q.shape[0], q.shape[1]
    M = mem.shape[1]
    mem_n = rmsnorm(mem, mem_norm_g)
    qh = q.reshape(B, S, MEM_HEADS, MEM_HEAD_DIM)
    km = (mem_n @ w_mem_k).reshape(B, M, MEM_HEADS, MEM_HEAD_DIM)
    vm = (mem_n @ w_mem_v).reshape(B, M, MEM_HEADS, MEM_HEAD_DIM)
    s = jnp.einsum('bshd,bmhd->bhsm', qh, km).astype(jnp.float32) * (MEM_HEAD_DIM ** -0.5)
    p = jax.nn.softmax(s, axis=-1).astype(q.dtype)
    return jnp.einsum('bhsm,bmhd->bshd', p, vm).reshape(B, S, MEM_COLS)

def setup_inputs(seed: int = 0) -> dict:
    key = jax.random.key(seed)
    ks = jax.random.split(key, 32)
    f32 = jnp.float32
    L = DEPTH

    def nrm(k, shape, scale):
        return jax.random.normal(k, shape, f32) * scale

    def gain(k, n):
        return 1.0 + 0.05 * jax.random.normal(k, (L, n), f32)

    dt = jnp.exp(jax.random.uniform(ks[9], (L, SSD_HEADS), f32) * (np.log(0.1) - np.log(1e-3)) + np.log(1e-3))
    dt_bias = dt + jnp.log(-jnp.expm1(-dt))
    a_log = jnp.log(jax.random.uniform(ks[10], (L, SSD_HEADS), f32, minval=1.0, maxval=16.0))
    return {
        'x': jax.random.normal(ks[0], (BATCH, SEQ, D_MODEL), f32),
        'mem': jax.random.normal(ks[1], (BATCH, MEM_LEN, D_MODEL), f32),
        'pre_mix_g': gain(ks[2], D_MODEL),
        'w_in': nrm(ks[3], (L, D_MODEL, IN_COLS), D_MODEL ** -0.5),
        'kv_norm_g': gain(ks[4], DSA_KV_RANK),
        'w_uk': nrm(ks[5], (L, DSA_HEADS, DSA_HEAD_DIM, DSA_KV_RANK), DSA_KV_RANK ** -0.5),
        'w_uv': nrm(ks[6], (L, DSA_HEADS, DSA_KV_RANK, DSA_HEAD_DIM), DSA_KV_RANK ** -0.5),
        'ssd_conv_w': nrm(ks[7], (L, SSD_CONV, SSD_XBC_COLS), SSD_CONV ** -0.5),
        'ssd_conv_b': nrm(ks[8], (L, SSD_XBC_COLS), 0.02),
        'dt_bias': dt_bias,
        'a_log': a_log,
        'd_skip': 1.0 + 0.1 * jax.random.normal(ks[11], (L, SSD_HEADS), f32),
        'ssd_norm_g': gain(ks[12], SSD_INNER),
        'mem_norm_g': gain(ks[13], D_MODEL),
        'w_mem_k': nrm(ks[14], (L, D_MODEL, MEM_COLS), D_MODEL ** -0.5),
        'w_mem_v': nrm(ks[15], (L, D_MODEL, MEM_COLS), D_MODEL ** -0.5),
        'w_br_a': nrm(ks[16], (L, DSA_Q_COLS, D_MODEL), DSA_Q_COLS ** -0.5),
        'w_br_b': nrm(ks[17], (L, SSD_INNER, D_MODEL), SSD_INNER ** -0.5),
        'w_br_c': nrm(ks[18], (L, MEM_COLS, D_MODEL), MEM_COLS ** -0.5),
        'w_out': nrm(ks[19], (L, D_MODEL, D_MODEL), D_MODEL ** -0.5),
        'post_mix_g': gain(ks[20], D_MODEL),
        'pre_ffn_g': gain(ks[21], D_MODEL),
        'w_up': nrm(ks[22], (L, D_MODEL, 2 * FFN_DIM), D_MODEL ** -0.5),
        'ffn_conv_w': nrm(ks[23], (L, FFN_CONV, 2 * FFN_DIM), FFN_CONV ** -0.5),
        'ffn_conv_b': nrm(ks[24], (L, 2 * FFN_DIM), 0.02),
        'w_down': nrm(ks[25], (L, FFN_DIM, D_MODEL), FFN_DIM ** -0.5),
        'post_ffn_g': gain(ks[26], D_MODEL),
    }

def reference(x, mem, pre_mix_g, w_in, kv_norm_g, w_uk, w_uv, ssd_conv_w, ssd_conv_b,
              dt_bias, a_log, d_skip, ssd_norm_g, mem_norm_g, w_mem_k, w_mem_v,
              w_br_a, w_br_b, w_br_c, w_out, post_mix_g, pre_ffn_g, w_up,
              ffn_conv_w, ffn_conv_b, w_down, post_ffn_g):
    B, S = x.shape[0], x.shape[1]
    for l in range(DEPTH):
        h = rmsnorm(x, pre_mix_g[l])
        proj = h @ w_in[l]
        q_a, c_kv, q_i, k_i, w_i, z, xbc, dt_raw, q_m, gate_raw = split_cols(proj, IN_SPLITS)
        c_kv = rmsnorm(c_kv, kv_norm_g[l])
        o_a = dsa_attention(q_a.reshape(B, S, DSA_HEADS, DSA_HEAD_DIM), c_kv,
                            q_i.reshape(B, S, IDX_HEADS, IDX_HEAD_DIM), k_i, w_i,
                            w_uk[l], w_uv[l])
        o_b = ssd_mixer(z, xbc, dt_raw, ssd_conv_w[l], ssd_conv_b[l], dt_bias[l],
                        a_log[l], d_skip[l], ssd_norm_g[l])
        o_c = memory_cross_attention(q_m, mem, mem_norm_g[l], w_mem_k[l], w_mem_v[l])
        g = jax.nn.sigmoid(gate_raw).reshape(B, S, N_BRANCHES, D_MODEL)
        merged = (g[:, :, 0] * (o_a @ w_br_a[l]) + g[:, :, 1] * (o_b @ w_br_b[l])
                  + g[:, :, 2] * (o_c @ w_br_c[l]))
        x = x + rmsnorm(merged @ w_out[l], post_mix_g[l])
        h = rmsnorm(x, pre_ffn_g[l])
        u = causal_dwconv(h @ w_up[l], ffn_conv_w[l], ffn_conv_b[l])
        a, v = jnp.split(u, 2, axis=-1)
        f = (jax.nn.gelu(a, approximate=True) * v) @ w_down[l]
        x = x + rmsnorm(f, post_ffn_g[l])
    return x


_drawn_inputs = setup_inputs


def setup_inputs(seed=0):
    import zlib

    import numpy as np

    out = dict(_drawn_inputs(seed))
    spreads = {}
    factors = {'kv_norm_g': 4.423,
     'mem_norm_g': 8.0,
     'ffn_conv_b': 3.408,
     'ssd_conv_b': 8.0,
     'd_skip': 7.371,
     'ssd_norm_g': 8.0}
    for name, (base, spread) in spreads.items():
        noise = np.random.default_rng([zlib.crc32(name.encode()), seed]).standard_normal(out[name].shape)
        drawn = base * np.exp(spread * noise) if base else spread * noise
        out[name] = __import__('jax').numpy.asarray(drawn.astype(out[name].dtype))
    for name, factor in factors.items():
        out[name] = (out[name] * factor).astype(out[name].dtype)
    return out
```

```python
from contextlib import ExitStack

import concourse.bass as bass
from concourse import mybir

F32 = mybir.dt.float32
F32R = mybir.dt.float32r
I32 = mybir.dt.int32
ALU = mybir.AluOpType
ACT = mybir.ActivationFunctionType
AX_X = mybir.AxisListType.X

P = 128
S = 256
D = 2048
NT = S // P
KT = D // P
CH = 512
EPS = 1e-6
GELU_CUBE, GELU_SCALE = 0.044715, (2 / 3.141592653589793) ** 0.5

HEADS, HD, RANK = 16, 128, 512
TOPK = S // 4
SCALE = HD ** -0.5
IDX_SCALE, IDX_W_SCALE = HD ** -0.5, 16 ** -0.5
MEM_HEADS, MEM_HD = 4, 512
MEM_SCALE = MEM_HD ** -0.5
GROUPS, STATE, SSD_HEADS, SHD = 8, 128, 64, 64
INNER = 4096
HPG = SSD_HEADS // GROUPS
FFN = 5632
FB = FFN // P
XBLK = INNER // P
UP0, UP1 = 6, 5
CONV_BLK = 48

Q_A = 0
C_KV = Q_A + 2048
Q_I = C_KV + 512
K_I = Q_I + 2048
W_I = K_I + 128
Z = W_I + 16
XBC = Z + 4096
DT_C = XBC + 6144
Q_M = DT_C + 64
GATE = Q_M + 2048
IN_COLS = GATE + 3 * D
SMALL = 128 + 16 + 64

NEG = -3.0e38
MARK = -3.4e38
TAKEN = -3.2e38
MASKED = -1.0e30


def hybrid_layer(nc, t, out):
    ctx = ExitStack()
    with ctx:
        def sem(name):
            return ctx.enter_context(nc.semaphore(name))

        BASE = 16512
        RAW_AT = BASE
        WHI_AT = RAW_AT + 2 * 8192
        WLO_AT = WHI_AT + 4 * 8192
        HT_AT = WLO_AT + 4 * 8192
        OT_AT = HT_AT + 32768
        MERGED_AT = OT_AT + 32768
        PAR_AT = MERGED_AT + 16384
        WORK_AT = PAR_AT + 8192
        END = 229368

        def at(name, shape, dtype, offset):
            return nc.alloc_sbuf_tensor_at(name, [P] + shape, dtype, offset=offset)

        raw = at("raw", [2, 2048], F32, RAW_AT)
        whi = at("whi", [4, 2048], F32R, WHI_AT)
        wlo = at("wlo", [4, 2048], F32R, WLO_AT)
        ht_hi = at("ht_hi", [KT, S], F32R, HT_AT)
        ht_lo = at("ht_lo", [KT, S], F32R, HT_AT + 16384)
        ot_hi = at("ot_hi", [KT, S], F32R, OT_AT)
        ot_lo = at("ot_lo", [KT, S], F32R, OT_AT + 16384)
        merged = at("merged", [NT, D], F32, MERGED_AT)

        par = at("par", [672], F32, PAR_AT)
        ident = at("ident", [P], F32, PAR_AT + 2688)
        ones = at("ones", [P], F32, PAR_AT + 3200)
        tri = at("tri", [P], F32, PAR_AT + 3712)
        causneg = at("causneg", [P], F32, PAR_AT + 4224)
        rows = at("rows", [3, 64], F32, PAR_AT + 4736)
        dt = at("dt", [NT, 64], F32, PAR_AT + 5504)
        da = at("da", [NT, 64], F32, PAR_AT + 6016)
        acum = at("acum", [NT, 64], F32, PAR_AT + 6528)
        eacum = at("eacum", [64], F32, PAR_AT + 7040)
        edec = at("edec", [64], F32, PAR_AT + 7296)
        stat = at("stat", [32], F32, PAR_AT + 7552)
        widx = at("widx", [NT, 16], F32, PAR_AT + 7680)
        scr = at("scr", [32], F32, PAR_AT + 7808)
        PRE_MIX, MEM_G, PRE_FFN, SSD_G, CONV_B, CONV_W, FFN_W, FFN_B = 0, 16, 32, 48, 80, 128, 320, 584

        xin = at("xin", [NT, D], F32, OT_AT)
        memin = at("memin", [NT, D], F32, OT_AT + 16384)
        stage = at("stage", [7, P], F32, WORK_AT + 16384)
        junk_a = at("junk_a", [D], F32, WORK_AT + 24576)
        memn_hi = at("memn_hi", [KT, S], F32R, MERGED_AT)
        memn_lo = at("memn_lo", [KT, S], F32R, WORK_AT)

        kmem = at("kmem", [4, S], F32, WORK_AT + 16384)
        vmem = at("vmem", [NT, CH], F32, WORK_AT + 20480)
        qmem = at("qmem", [4, S], F32, WORK_AT + 24576)
        pmem = at("pmem", [NT, S], F32, WORK_AT + 28672)
        pmemT = at("pmemT", [NT, S], F32, WORK_AT + 30720)
        tgate = at("tgate", [NT, CH], F32, WORK_AT + 32768)

        kvg = at("kvg", [RANK], F32, WORK_AT)
        mask = at("mask", [384], F32, WORK_AT)
        ckv_hi = at("ckv_hi", [NT, RANK], F32R, WORK_AT + 2048)
        ckv_lo = at("ckv_lo", [NT, RANK], F32R, WORK_AT + 6144)
        ckvT_hi = at("ckvT_hi", [4, S], F32R, WORK_AT + 10240)
        ckvT_lo = at("ckvT_lo", [4, S], F32R, WORK_AT + 14336)
        ql_hi = at("ql_hi", [4, S], F32R, WORK_AT + 18432)
        ql_lo = at("ql_lo", [4, S], F32R, WORK_AT + 22528)
        ol_hi = at("ol_hi", [4, S], F32R, WORK_AT + 26624)
        ol_lo = at("ol_lo", [4, S], F32R, WORK_AT + 30720)
        pT_hi = at("pT_hi", [384], F32R, WORK_AT + 34816)
        pT_lo = at("pT_lo", [384], F32R, WORK_AT + 36352)
        prob = at("prob", [384], F32, WORK_AT + 37888)
        scored = at("scored", [384], F32, WORK_AT + 37888)
        qi_hi = [ql_hi, ol_hi]
        qi_lo = [ql_lo, ol_lo]
        ckv = at("ckv", [NT, RANK], F32, WORK_AT + 26624)
        junk_q = at("junk_q", [RANK], F32, OT_AT + 12 * 1024)
        relu = at("relu", [2, 384], F32, OT_AT + 12 * 1024)
        ki_hi = at("ki_hi", [S], F32R, OT_AT + 16384 + 12 * 1024)
        ki_lo = at("ki_lo", [S], F32R, OT_AT + 16384 + 13 * 1024)
        score = at("score", [384], F32, OT_AT + 16384 + 14 * 1024)

        xv = at("xv", [4, S], F32, WORK_AT)
        xT = at("xT", [4, S], F32, WORK_AT + 4096)
        bcv = at("bcv", [2, S], F32, WORK_AT + 8192)
        bcT = at("bcT", [2, S], F32, WORK_AT + 10240)
        xdt = at("xdt", [NT, CH], F32, WORK_AT + 12288)
        y = at("y", [NT, CH], F32, WORK_AT + 16384)
        xdd = at("xdd", [CH], F32, WORK_AT + 20480)
        atri = at("atri", [HPG, P], F32, WORK_AT + 22528)
        dec = at("dec", [HPG, P], F32, WORK_AT + 26624)
        cb = at("cb", [NT, P], F32, WORK_AT + 30720)
        btok = at("btok", [P], F32, WORK_AT + 31744)
        hst = at("hst", [CH], F32, WORK_AT + 32256)
        zs = at("zs", [NT, CH], F32, WORK_AT + 34304)
        assert WORK_AT + 34304 + 4096 <= END

        tmp = at("tmp", [8, P], F32, WORK_AT + 12288)
        tgate_b = at("tgate_b", [NT, CH], F32, WORK_AT)
        gprod = at("gprod", [NT, CH], F32, WORK_AT + 12288)

        mix = at("mix", [NT, D], F32, WORK_AT)
        grow = at("grow", [D], F32, WORK_AT + 16384)
        diag = at("diag", [NT, P], F32, WORK_AT + 24576)
        junk_o = at("junk_o", [D], F32, OT_AT)
        x1 = at("x1", [NT, D], F32, MERGED_AT)

        ft_hi = at("ft_hi", [24, S], F32R, OT_AT)
        ft_lo = at("ft_lo", [24, S], F32R, OT_AT + 24576)
        acc = at("acc", [NT, D], F32, WORK_AT)
        va = at("va", [4, S], F32, WORK_AT + 16384)
        ta = at("ta", [4, S], F32, WORK_AT + 20480)
        vv = at("vv", [4, S], F32, WORK_AT + 24576)
        tb = at("tb", [4, S], F32, WORK_AT + 28672)
        x1b = at("x1b", [NT, D], F32, HT_AT)
        frow = at("frow", [D], F32, HT_AT + 16384)
        junk_f = at("junk_f", [CH], F32, HT_AT + 24576)

        x1_dram = nc.dram_tensor("x1_scratch", (S, D), F32, kind="Internal").ap()

        gate_dram = nc.dram_tensor("gate_scratch", (4, P, NT * CH), F32, kind="Internal").ap()

        bank = [ctx.enter_context(nc.psum_tensor(f"bank{i}", [P, CH], F32)) for i in range(8)]

        kvg_in = sem("kvg_in")
        pre_n, pre_u, pre_w, pre_ln, pre_da, pre_cum, pre_dec, pre_done = (
            sem(n) for n in ("pre_n", "pre_u", "pre_w", "pre_ln", "pre_da", "pre_cum", "pre_dec", "pre_done"))
        x_tap, x_conv, x_tanh, x_ready, bc_tap, bc_conv, bc_tanh, bc_ready, z_tanh = (
            sem(n) for n in ("x_tap", "x_conv", "x_tanh", "x_ready", "bc_tap", "bc_conv", "bc_tanh", "bc_ready", "z_tanh"))
        core_in, core_btok, core_x, core_cb, atri_done, cum_done, seg_done, dec_done, m_ready, yd_done = (
            sem(n) for n in ("core_in", "core_btok", "core_x", "core_cb", "atri_done", "cum_done", "seg_done", "dec_done", "m_ready", "yd_done"))
        y0_done, st_done, st_ready, yoff_done, y_ready, yT_done, yT_hi, yT_lo = (
            sem(n) for n in ("y0_done", "st_done", "st_ready", "yoff_done", "y_ready", "yT_done", "yT_hi", "yT_lo"))
        gate_saved, gate_back = sem("gate_saved"), sem("gate_back")
        x_in, mem_in, par_in, row_in = sem("x_in"), sem("mem_in"), sem("par_in"), sem("row_in")
        late_in, x_again, x1_out, x1_in, out_done = (sem(n) for n in ("late_in", "x_again", "x1_out", "x1_in", "out_done"))
        mix_sq, x1_ready, x1_sq, diag_ready = (sem(n) for n in ("mix_sq", "x1_ready", "x1_sq", "diag_ready"))
        a_tap, a_conv, a_sq, a_arg, a_tanh, v_tap, f_ready, f_hi, f_lo, down_sq, y_out = (
            sem(n) for n in ("a_tap", "a_conv", "a_sq", "a_arg", "a_tanh", "v_tap", "f_ready", "f_hi", "f_lo", "down_sq", "y_out"))
        consts = sem("consts")
        raw_in = [sem("raw_in0"), sem("raw_in1")]
        dtw_in = sem("dtw_in")
        hi_done = sem("hi_done")
        lo_done = sem("lo_done")
        unit_used = sem("unit_used")
        evac = [sem("evac0"), sem("evac1"), sem("evac2"), sem("evac3")]
        tp_done, tp_hi, tp_lo = sem("tp_done"), sem("tp_hi"), sem("tp_lo")
        par_tp, par_done = sem("par_tp"), sem("par_done")
        sq_done, norm_done = sem("sq_done"), sem("norm_done")
        ms_done, mnb, mexp, mprob, mt_done, mpT, mo_done, mo_hi, mo_lo = (
            sem(n) for n in ("ms_done", "mnb", "mexp", "mprob", "mt_done", "mpT", "mo_done", "mo_hi", "mo_lo"))
        small_hi, ck_sq, ck_hi, ck_lo, ckT_done, ckT_hi, ckT_lo = (
            sem(n) for n in ("small_hi", "ck_sq", "ck_hi", "ck_lo", "ckT_done", "ckT_hi", "ckT_lo"))
        q_hi = sem("q_hi")
        idx_done, relu_done, relu_used, mask_done = (sem(n) for n in ("idx_done", "relu_done", "relu_used", "mask_done"))
        at_ql, at_ql_hi, at_ql_lo, at_s, at_nb, at_exp, at_p, at_t = (
            sem(n) for n in ("at_ql", "at_ql_hi", "at_ql_lo", "at_s", "at_nb", "at_exp", "at_p", "at_t"))
        at_t_hi, at_t_lo, at_ol, at_ol_hi, at_ol_lo, at_o, at_o_hi, at_o_lo = (
            sem(n) for n in ("at_t_hi", "at_t_lo", "at_ol", "at_ol_hi", "at_ol_lo", "at_o", "at_o_hi", "at_o_lo"))
        gate_used = sem("gate_used")

        U_MEM = 0
        U_GC = U_MEM + 12 * MEM_HEADS
        U_SMALL = U_GC + 32
        U_CKV = U_SMALL + 4
        U_QI = U_CKV + 4
        U_QA = U_QI + 16
        U_ATT = U_QA + 16
        U_GA = U_ATT + 16
        U_S0 = U_GA + 32
        U_GB = U_S0 + 5 * 12
        U_S5 = U_GB + 32
        U_B2 = U_S5 + 3 * 12
        U_OUT = U_B2 + 16
        U_UP0 = U_OUT + 16
        U_DOWN0 = U_UP0 + 8 * UP0
        U_UP1 = U_DOWN0 + 4 * UP0
        U_DOWN1 = U_UP1 + 8 * UP1
        U_END = U_DOWN1 + 4 * UP1

        w_in = t["w_in"][0]

        def cols(w, j, c0, n):
            return w[j * 512:(j + 1) * 512, c0:c0 + n].rearrange("(k p) c -> p k c", p=P)

        def dcols(w, j, c0, n):
            return w[j * 512:(j + 1) * 512, bass.ds(c0, n)].rearrange("(k p) c -> p k c", p=P)

        def gates_from(n, i):
            return E0_GATE[n] + i

        def tp_bank(n):
            return bank[n] if n < 8 else bank[2 + (n - 8) % 6] if n < 16 else bank[4 + n % 4] if n < 24 else bank[n - 24]

        E0_GATE = {0: 9, 1: 10, 4: 19, 5: 20, 8: 28, 9: 29}

        def key_unit(pair):
            return max(2 * pair - 1, 0)

        def value_unit(pair):
            return 2 * pair + 2 if pair < HEADS // 2 - 1 else 2 * pair + 1

        block = ctx.enter_context(nc.Block())

        @block.sync
        def _(sp):
            sp.dma_start(memin[:], t["mem"][0].rearrange("(a p) d -> p a d", p=P)).then_inc(mem_in, 16)
            sp.dma_start(xin[:], t["x"][0].rearrange("(a p) d -> p a d", p=P)).then_inc(x_in, 16)

            def load(u, src, width, i=0, per=0):
                if not isinstance(i, int) or u >= 2:
                    sp.wait_ge(lo_done, u - 1 + per * i)
                dst = raw[:, u % 2, 0:width]
                if len(src.shape) == 3:
                    dst = dst.rearrange("p (k c) -> p k c", k=src.shape[1])
                if len(src.shape) == 4:
                    dst = dst.rearrange("p (k a c) -> p k a c", k=src.shape[1], a=src.shape[2])
                return sp.dma_start(dst, src).then_inc(raw_in[u % 2], 16)

            wk, wv = t["w_mem_k"][0], t["w_mem_v"][0]

            def mem_head(u, c0, i=0):
                for n, (w, off) in enumerate(((wk, 0), (wv, 0), (w_in, Q_M))):
                    for j in range(4):
                        load(u + 4 * n + j, dcols(w, j, c0 + off, CH), 2048, i, 12)

            mem_head(0, 0)
            with sp.Fori(0, MEM_HEADS - 1) as i:
                mem_head(12, 512 + 512 * i, i)

            def gated(u, branch, w, j0, c0, i=0):
                for j in range(4):
                    load(u + j, dcols(w_in, j, GATE + branch * D + c0, CH), 2048, i, 8)
                for j in range(4):
                    load(u + 4 + j, dcols(w, j0 + j, c0, CH), 2048, i, 8)

            gated(U_GC, 2, t["w_br_c"][0], 0, 0)
            with sp.Fori(0, 3) as i:
                gated(U_GC + 8, 2, t["w_br_c"][0], 0, 512 + 512 * i, i)

            sp.wait_ge(unit_used, U_GC)
            sp.dma_start(kvg[:], t["kv_norm_g"].to_broadcast([P, RANK])).then_inc(kvg_in, 16)
            for j in range(4):
                c0, n = (K_I, 144) if j < 2 else (DT_C, 64)
                r = 1024 * (j % 2)
                load(U_SMALL + j, w_in[r:r + 1024, c0:c0 + n].rearrange("(k p) c -> p k c", p=P), 8 * n)
            for j in range(4):
                load(U_CKV + j, cols(w_in, j, C_KV, CH), 2048)
            for u, c0 in ((U_QI, Q_I), (U_QA, Q_A)):
                for j in range(4):
                    load(u + j, cols(w_in, j, c0, CH), 2048)
                with sp.Fori(0, 3) as i:
                    for j in range(4):
                        load(u + 4 + j, dcols(w_in, j, c0 + 512 + 512 * i, CH), 2048, i, 4)
            uk = t["w_uk"][0].rearrange("(g h) d r -> g d h r", h=2)
            uv = t["w_uv"][0].rearrange("h r d -> (h r) d").rearrange("(g x p) d -> g p x d", p=P, x=8)
            for n in range(16):
                if n == 0 or n % 2 and n < 15:
                    load(U_ATT + n, uk[(n + 1) // 2], 1024)
                else:
                    load(U_ATT + n, uv[7 if n == 15 else n // 2 - 1], 1024)
            gated(U_GA, 0, t["w_br_a"][0], 0, 0)
            with sp.Fori(0, 3) as i:
                gated(U_GA + 8, 0, t["w_br_a"][0], 0, 512 + 512 * i, i)

            def group(u, g, i=0):
                for j in range(4):
                    load(u + j, dcols(w_in, j, XBC + CH * g, CH), 2048, i, 12)
                for j in range(4):
                    c0 = XBC + INNER + 1024 * (j // 2) + P * g
                    r = 1024 * (j % 2)
                    load(u + 4 + j, w_in[r:r + 1024, bass.ds(c0, P)].rearrange("(k p) c -> p k c", p=P), 1024, i, 12)
                for j in range(4):
                    load(u + 8 + j, dcols(w_in, j, Z + CH * g, CH), 2048, i, 12)

            group(U_S0, 0)
            with sp.Fori(0, 4) as i:
                group(U_S0 + 12, 1 + i, i)
            gated(U_GB, 1, t["w_br_b"][0], 0, 0)
            with sp.Fori(0, 3) as i:
                gated(U_GB + 8, 1, t["w_br_b"][0], 0, 512 + 512 * i, i)
            with sp.Fori(0, 3) as i:
                group(U_S5, 5 + i, i)
            with sp.Fori(0, 4) as i:
                for j in range(4):
                    load(U_B2 + j, dcols(t["w_br_b"][0], 4 + j, 512 * i, CH), 2048, i, 4)
            with sp.Fori(0, 4) as i:
                for j in range(4):
                    load(U_OUT + j, dcols(t["w_out"][0], j, 512 * i, CH), 2048, i, 4)

            def up(u, c0, chunks):
                with sp.Fori(0, chunks) as i:
                    for n in range(2):
                        for j in range(4):
                            load(u + 4 * n + j, dcols(t["w_up"][0], j, c0 + n * FFN + 512 * i, CH), 2048, i, 8)

            up(U_UP0, 0, UP0)
            with sp.Fori(0, 2) as i:
                for n in range(2):
                    for k in range(UP0):
                        load(U_DOWN0 + UP0 * n + k, dcols(t["w_down"][0], k, 1024 * i + 512 * n, CH), 2048, i, 2 * UP0)
            up(U_UP1, 512 * UP0, UP1)
            for n in range(4):
                for k in range(UP1):
                    load(U_DOWN1 + UP1 * n + k, cols(t["w_down"][0], UP0 + k, 512 * n, CH), 2048)
            y = out[0].rearrange("(q p) d -> q p d", p=P)
            for n in range(4):
                sp.wait_ge(y_out, n + 1)
                c = slice(n % 2 * 1024, n % 2 * 1024 + 1024)
                sp.dma_start(y[n // 2][:, c], acc[:, n // 2, c]).then_inc(out_done, 16)
            sp.wait_ge(out_done, 64)

        @block.gpsimd
        def _(pool):
            nc.gpsimd.memset(ones[:], 1.0)
            nc.gpsimd.memset(ident[:], 0.0)
            nc.gpsimd.memset(causneg[:], 0.0)
            pool.drain()
            nc.gpsimd.affine_select(out=ident[:], in_=ident[:], compare_op=ALU.not_equal, fill=1.0, base=0,
                                    pattern=[[-1, P]], channel_multiplier=1)
            nc.gpsimd.affine_select(out=tri[:], in_=ones[:], compare_op=ALU.is_ge, fill=0.0, base=0,
                                    pattern=[[1, P]], channel_multiplier=-1)
            nc.gpsimd.affine_select(out=causneg[:], in_=causneg[:], compare_op=ALU.is_ge, fill=NEG, base=0,
                                    pattern=[[-1, P]], channel_multiplier=1).then_inc(consts, 1)

            pool.wait_ge(pre_da, 1)

            def running(g, c):
                nc.gpsimd.tensor_tensor(atri[:], tri[:].unsqueeze(1).to_broadcast([P, HPG, P]),
                                        da[:, c, bass.ds(HPG * g, HPG)].unsqueeze(2).to_broadcast([P, HPG, P]), ALU.mult).then_inc(atri_done, 1)
                pool.wait_ge(cum_done, 2 * g + c + 1)

            with pool.Fori(0, GROUPS) as g:
                for c in range(NT):
                    running(g, c)
            pool.wait_ge(gate_saved, 64)
            pool.wait_ge(x_ready, GROUPS)
            for n in range(4):
                if n:
                    pool.wait_ge(gate_used, 12 + n)
                nc.gpsimd.dma_start(tgate_b[:].rearrange("p a c -> p (a c)"), gate_dram[n]).then_inc(gate_back, 16)
            nc.gpsimd.dma_start(grow[:], t["post_mix_g"].to_broadcast([P, D])).then_inc(late_in, 16)
            pool.wait_ge(tp_done, 24)
            nc.gpsimd.dma_start(x1[:], t["x"][0].rearrange("(a p) d -> p a d", p=P)).then_inc(x_again, 16)
            pool.wait_ge(x1_ready, 2)
            nc.gpsimd.dma_start(x1_dram.rearrange("(a p) d -> p a d", p=P), x1[:]).then_inc(x1_out, 16)
            pool.wait_ge(x1_out, 16)
            pool.wait_ge(unit_used, U_DOWN1)
            nc.gpsimd.dma_start(x1b[:], x1_dram.rearrange("(a p) d -> p a d", p=P)).then_inc(x1_in, 16)
            nc.gpsimd.dma_start(frow[:], t["post_ffn_g"].to_broadcast([P, D])).then_inc(x1_in, 16)

        @block.scalar
        def _(act):
            for n, (name, r0, k) in enumerate((("pre_mix_g", 0, 16), ("mem_norm_g", 16, 16), ("pre_ffn_g", 32, 16),
                                               ("ssd_norm_g", 48, 32), ("ssd_conv_b", 80, 48))):
                act.dma_start(stage[r0:r0 + k, 0, :], t[name][0].rearrange("(b c) -> b c", c=P)).then_inc(par_in, 16)
            cw = t["ssd_conv_w"][0].rearrange("k (b c) -> (k b) c", c=P)
            fw = t["ffn_conv_w"][0].rearrange("k (b c) -> (k b) c", c=P)
            for n in range(2):
                act.dma_start(stage[0:96, 1 + n, :], cw[96 * n:96 * n + 96]).then_inc(par_in, 16)
            for n in range(3):
                act.dma_start(stage[0:88, 3 + n, :], fw[88 * n:88 * n + 88]).then_inc(par_in, 16)
            act.dma_start(stage[0:88, 6, :], t["ffn_conv_b"][0].rearrange("(b c) -> b c", c=P)).then_inc(par_in, 16)
            for n, name in enumerate(("dt_bias", "a_log", "d_skip")):
                act.dma_start(rows[:, n, :], t[name].to_broadcast([P, 64])).then_inc(row_in, 16)

            def split(u, width=2048, i=0, per=0):
                act.wait_ge(raw_in[u % 2], 16 * (u // 2 + 1) + 8 * per * i)
                if not isinstance(i, int) or u >= 4:
                    act.wait_ge(unit_used, u - 3 + per * i)
                nc.scalar.copy(whi[:, u % 4, 0:width], raw[:, u % 2, 0:width]).then_inc(hi_done, 1)

            def transposed_hi(n0, dst, gain, scale=1.0, groups=range(8)):
                for g in groups:
                    b = tp_bank(n0 + g)
                    act.wait_ge(tp_done, n0 + g + 1)
                    for k in range(2):
                        last = nc.scalar.activation(dst[:, 2 * g + k, :], b[:, k * S:(k + 1) * S], ACT.Copy,
                                                    scale=par[:, gain + 2 * g + k:gain + 2 * g + k + 1] if gain is not None else scale)
                    last.then_inc(tp_hi, 1)

            def mem_exp(h):
                act.wait_ge(mnb, h + 1)
                for q in range(NT):
                    last = nc.scalar.activation(pmem[:, q, :], bank[6][:, q * S:(q + 1) * S], ACT.Exp, scale=MEM_SCALE,
                                                bias=stat[:, 2 + q:3 + q], accum_out=stat[:, 4 + q:5 + q])
                last.then_inc(mexp, 1)

            def mem_out_hi(h):
                act.wait_ge(mo_done, h + 1)
                for n in range(2):
                    last = nc.scalar.copy(ot_hi[:, bass.ds(4 * h + 2 * n, 2), :], bank[6 + n][:].rearrange("p (b s) -> p b s", b=2))
                last.then_inc(mo_hi, 1)

            def mem_head(u, h, i=0, first=False):
                split(u + 4, i=i, per=12)
                if not first:
                    mem_exp(h - 1)
                for j in range(1, 4):
                    split(u + 4 + j, i=i, per=12)
                act.wait_ge(unit_used, u + 4 + 12 * i)
                nc.scalar.copy(kmem[:, 0:2, :], bank[0][:].rearrange("p (b s) -> p b s", b=2)).then_inc(evac[0], 1)
                if first:
                    transposed_hi(8, ht_hi, PRE_MIX)
                for j in range(4):
                    split(u + 8 + j, i=i, per=12)
                    if j == 1 and not first:
                        mem_out_hi(h - 1)
                act.wait_ge(unit_used, u + 8 + 12 * i)
                nc.scalar.copy(vmem[:, 0, :], bank[2][:]).then_inc(evac[1], 1)
                for j in range(4):
                    split(u + 12 + j, i=i, per=12)
                act.wait_ge(unit_used, u + 12 + 12 * i)
                nc.scalar.copy(qmem[:, 0:2, :], bank[4][:].rearrange("p (b s) -> p b s", b=2)).then_inc(evac[2], 1)

            for n, (src, ready) in enumerate(((memin, mem_in), (xin, x_in))):
                act.wait_ge(ready, 16)
                for q in range(NT):
                    last = nc.scalar.activation(junk_a[:], src[:, q, :], ACT.Square, accum_out=stat[:, 8 + 2 * n + q:9 + 2 * n + q])
                    act.drain()
                last.then_inc(sq_done, 1)
            act.wait_ge(par_tp, 1)
            nc.scalar.copy(par[:, 0:80], bank[0][:, 0:80])
            nc.scalar.mul(par[:, 80:320], bank[0][:, 80:320], 0.5)
            nc.scalar.copy(par[:, 320:672], bank[1][:, 0:352]).then_inc(par_done, 1)
            act.drain()
            transposed_hi(0, memn_hi, MEM_G)
            for j in range(4):
                split(j)
            mem_head(0, 0, first=True)
            with act.Fori(0, MEM_HEADS - 1) as i:
                mem_head(12, 1 + i, i)

            def gate_tanh(u, n, i=0):
                act.wait_ge(unit_used, u + 4 + 8 * i)
                if n > 0:
                    act.wait_ge(gate_used, n + i)
                for q in range(NT):
                    last = nc.scalar.activation(tgate[:, q, :], bank[q][:], ACT.Tanh, scale=0.5)
                last.then_inc(evac[0], 1)

            def gated(u, n, i=0, side=(None, None, None, None)):
                for j in range(4):
                    split(u + 4 + j, i=i, per=8)
                    if side[j]:
                        side[j]()
                gate_tanh(u, n, i)
                for j in range(4):
                    split(u + 8 + j, i=i, per=8)

            gated(U_GC, 0, side=(lambda: mem_exp(3), None, None, lambda: mem_out_hi(3)))
            with act.Fori(0, 3) as i:
                gated(U_GC + 8, 1, i)

            for j in range(4):
                split(U_CKV + j)
            act.wait_ge(unit_used, U_SMALL + 4)
            nc.scalar.copy(ki_hi[:], bank[0][:, 0:S]).then_inc(small_hi, 1)
            nc.scalar.copy(dt[:], bank[1][:, 0:160].rearrange("p (q c) -> p q c", q=NT)[:, :, 16:80]).then_inc(evac[0], 1)
            for j in range(4):
                split(U_QI + j)
            act.wait_ge(unit_used, U_CKV + 4)
            for q in range(NT):
                last = nc.scalar.activation(junk_q[:], bank[2 + q][:], ACT.Square, accum_out=stat[:, 16 + q:17 + q])
                act.drain()
            last.then_inc(ck_sq, 1)
            act.wait_ge(evac[1], 13)
            nc.scalar.copy(ckv_hi[:], ckv[:]).then_inc(ck_hi, 1)

            def queries_hi(n):
                u = U_QI + 4 * n
                for j in range(4):
                    split(u + 4 + j, 1024 if n == 7 else 2048)
                    if n == 0 and j == 2:
                        act.wait_ge(ckT_done, 1)
                        for b in range(2):
                            last = nc.scalar.copy(ckvT_hi[:, 2 * b:2 * b + 2, :], bank[6 + b][:].rearrange("p (b s) -> p b s", b=2))
                        last.then_inc(ckT_hi, 1)
                    if 1 <= n <= 4:
                        h = 4 * (n - 1) + j
                        act.wait_ge(idx_done, h + 1)
                        if h >= 2:
                            act.wait_ge(relu_used, h - 1)
                        nc.scalar.activation(relu[:, h % 2, :], bank[6 + h % 2][:, 0:384], ACT.Relu, scale=IDX_SCALE).then_inc(relu_done, 1)
                act.wait_ge(unit_used, u + 4)
                for b in range(2):
                    dst = qi_hi[n % 2][:, 2 * b:2 * b + 2, :] if n < 4 else ot_hi[:, 4 * (n - 4) + 2 * b:4 * (n - 4) + 2 * b + 2, :]
                    last = nc.scalar.copy(dst, bank[2 * (n % 2) + b][:].rearrange("p (b s) -> p b s", b=2))
                last.then_inc(q_hi, 1)

            for n in range(8):
                queries_hi(n)

            def two_banks(dst, n):
                for b in range(2):
                    last = nc.scalar.copy(dst[:, 2 * b:2 * b + 2, :], bank[n + b][:].rearrange("p (b s) -> p b s", b=2))
                return last

            def key_hi(h):
                act.wait_ge(at_ql, h + 1)
                two_banks(ql_hi, 0).then_inc(at_ql_hi, 1)

            def out_latent_hi(h):
                act.wait_ge(at_ol, h + 1)
                two_banks(ol_hi, 4).then_inc(at_ol_hi, 1)

            def out_hi(h):
                act.wait_ge(at_o, h + 1)
                nc.scalar.copy(ot_hi[:, bass.ds(h, 1), :].rearrange("p a s -> p (a s)"), bank[6][:, 0:S]).then_inc(at_o_hi, 1)

            def attention(h, first=False, last_head=False):
                act.wait_ge(at_nb, h + 1)
                nc.scalar.activation(prob[:, 0:P], prob[:, 0:P], ACT.Exp, bias=stat[:, 18:19], accum_out=stat[:, 20:21])
                nc.scalar.activation(prob[:, P:384], prob[:, P:384], ACT.Exp, bias=stat[:, 19:20], accum_out=stat[:, 21:22]).then_inc(at_exp, 1)
                if not first:
                    out_latent_hi(h - 1)
                if not last_head:
                    key_hi(h + 1)
                act.wait_ge(at_t, h + 1)
                nc.scalar.copy(pT_hi[:], bank[3][:, 0:384]).then_inc(at_t_hi, 1)
                if not first:
                    out_hi(h - 1)

            key_hi(0)
            attention(0, first=True)
            attention(1)
            with act.Fori(0, 3) as i:
                for k in range(4):
                    attention(2 + k + 4 * i)
                    if k % 2 == 0:
                        split(U_ATT + 4 + k, 1024, i, 4)
                        split(U_ATT + 5 + k, 1024, i, 4)
            attention(14)
            for j in range(3):
                split(U_GA + j)
            attention(15, last_head=True)
            out_latent_hi(15)
            out_hi(15)
            split(U_GA + 3)

            gated(U_GA, 4)
            with act.Fori(0, 3) as i:
                gated(U_GA + 8, 5, i)

            def conv_tap(first_block, dst, banks, blocks, done, n, u, i):
                act.wait_ge(unit_used, u + 12 * i)
                for b in range(blocks):
                    k = first_block[b]
                    last = nc.scalar.activation(dst[:, b, :], banks[b // 2][:, (b % 2) * S:(b % 2 + 1) * S], ACT.Identity,
                                                scale=par[:, bass.ds(CONV_W + 3 * CONV_BLK + k, 1)], bias=par[:, bass.ds(CONV_B + k, 1)])
                last.then_inc(done, 1)

            def decay_exp(g, c):
                act.wait_ge(seg_done, 2 * g + c + 1)
                nc.scalar.activation(dec[:], dec[:], ACT.Exp).then_inc(dec_done, 1)

            def b_token(g):
                act.wait_ge(core_in, g + 1)
                nc.scalar.copy(btok[:], bank[7][:, 0:P]).then_inc(core_btok, 1)

            def state(g):
                act.wait_ge(st_done, g + 1)
                nc.scalar.copy(hst[:], bank[7][:]).then_inc(st_ready, 1)

            def y_hi(g, kt):
                act.wait_ge(yT_done, g + 1)
                for b in range(4):
                    src = bank[7 if b < 2 else 5][:, (b % 2) * S:(b % 2 + 1) * S]
                    last = nc.scalar.activation(ot_hi[:, bass.ds(kt + b, 1), :].rearrange("p a s -> p (a s)"), src, ACT.Copy,
                                                scale=par[:, bass.ds(SSD_G + 4 * g + b, 1)])
                last.then_inc(yT_hi, 1)

            def group(u, g, kt, i=0, core=True):
                split(u + 4, 1024, i, 12)
                if core:
                    b_token(g - 1)
                split(u + 5, 1024, i, 12)
                split(u + 6, 1024, i, 12)
                if core:
                    decay_exp(g - 1, 0)
                split(u + 7, 1024, i, 12)
                conv_tap([4 * g + b for b in range(4)], xv, bank[0:2], 4, x_tap, 0, u + 4, i)
                split(u + 8, 2048, i, 12)
                act.wait_ge(x_conv, g + 1)
                nc.scalar.activation(xT[:], xv[:], ACT.Tanh).then_inc(x_tanh, 1)
                if core:
                    decay_exp(g - 1, 1)
                split(u + 9, 2048, i, 12)
                if core:
                    state(g - 1)
                split(u + 10, 2048, i, 12)
                split(u + 11, 2048, i, 12)
                conv_tap([XBLK + g, XBLK + GROUPS + g], bcv, bank[2:3], 2, bc_tap, 0, u + 8, i)
                split(u + 12, 2048, i, 12)
                act.wait_ge(bc_conv, g + 1)
                nc.scalar.activation(bcT[:], bcv[:], ACT.Tanh).then_inc(bc_tanh, 1)
                split(u + 13, 2048, i, 12)
                split(u + 14, 2048, i, 12)
                if core:
                    y_hi(g - 1, kt)
                split(u + 15, 2048, i, 12)
                act.wait_ge(unit_used, u + 12 + 12 * i)
                if core:
                    act.wait_ge(y_ready, g)
                for q in range(NT):
                    last = nc.scalar.activation(zs[:, q, :], bank[3 + q][:], ACT.Tanh, scale=0.5)
                last.then_inc(z_tanh, 1)

            act.wait_ge(row_in, 48)
            nc.scalar.activation(rows[:, 1, :], rows[:, 1, :], ACT.Exp)
            act.wait_ge(pre_n, 1)
            nc.scalar.activation(tmp[:, 3, :], tmp[:, 2, :], ACT.Exp).then_inc(pre_u, 1)
            act.wait_ge(pre_w, 1)
            nc.scalar.activation(tmp[:, 5, :], tmp[:, 4, :], ACT.Ln).then_inc(pre_ln, 1)
            act.wait_ge(pre_dec, 1)
            nc.scalar.activation(eacum[:], acum[:, 1, :], ACT.Exp)
            nc.scalar.activation(edec[:], edec[:], ACT.Exp).then_inc(pre_done, 1)

            group(U_S0, 0, 0, core=False)
            with act.Fori(0, 4) as i:
                group(U_S0 + 12, 1 + i, 4 * i, i)

            def gate_b(u, n, i=0):
                for j in range(4):
                    split(u + 4 + j, i=i, per=8)
                act.wait_ge(unit_used, u + 4 + 8 * i)
                if n > 8:
                    act.wait_ge(gate_used, n + i)
                    act.wait_ge(gate_saved, 16 * (n - 8) + 16 * i)
                for q in range(NT):
                    last = nc.scalar.activation(tgate_b[:, q, :], bank[q][:], ACT.Tanh, scale=0.5)
                last.then_inc(evac[0], 1)
                act.wait_ge(evac[0], gates_from(n, i))
                act.dma_start(gate_dram[bass.ds(n - 8 + i, 1), :, :].rearrange("a p c -> (a p) c"), tgate_b[:].rearrange("p a c -> p (a c)")).then_inc(gate_saved, 16)
                for j in range(4):
                    split(u + 8 + j, i=i, per=8)

            gate_b(U_GB, 8)
            with act.Fori(0, 3) as i:
                gate_b(U_GB + 8, 9, i)
            act.wait_ge(gate_saved, 64)
            act.wait_ge(gate_used, 12)
            with act.Fori(0, 3) as i:
                group(U_S5, 5 + i, 4 * i, i)
            split(U_B2 + 4)
            b_token(7)
            split(U_B2 + 5)
            split(U_B2 + 6)
            decay_exp(7, 0)
            decay_exp(7, 1)
            state(7)
            y_hi(7, 12)
            split(U_B2 + 7)
            for n in range(1, 4):
                if n > 1:
                    transposed_hi(16, ht_hi, None, 0.5, range(2 * n - 4, 2 * n - 2))
                for j in range(4):
                    split(U_B2 + 4 * n + 4 + j)
            transposed_hi(16, ht_hi, None, 0.5, range(4, 8))

            with act.Fori(0, 2) as i:
                for n in range(2):
                    u = U_OUT + 4 * n
                    for j in range(4):
                        split(u + 4 + j, i=i, per=8)
                    act.wait_ge(unit_used, u + 4 + 8 * i)
                    for q in range(NT):
                        last = nc.scalar.activation(junk_o[:, 0:CH], bank[2 * n + q][:], ACT.Square, accum_out=stat[:, bass.ds(4 * q + n + 2 * i, 1)])
                        act.drain()
                    last.then_inc(mix_sq, 1)
            for q in range(NT):
                act.wait_ge(x1_ready, q + 1)
                nc.scalar.activation(junk_o[:], x1[:, q, :], ACT.Square, accum_out=stat[:, 12 + q:13 + q]).then_inc(x1_sq, 1)
                act.drain()
            transposed_hi(24, ht_hi, PRE_FFN)
            act.wait_ge(x1_out, 16)

            def tap(dst, b0, m, first_block):
                for b in range(4):
                    k = 4 * m + first_block + b
                    last = nc.scalar.activation(dst[:, b, :], bank[b0 + b // 2][:, (b % 2) * S:(b % 2 + 1) * S], ACT.Identity,
                                                scale=par[:, bass.ds(FFN_W + 4 * FB + k, 1)], bias=par[:, bass.ds(FFN_B + k, 1)])
                return last

            def up(u, m, kt, i):
                for j in range(4):
                    split(u + 4 + j, i=i, per=8)
                act.wait_ge(unit_used, u + 4 + 8 * i)
                tap(va, 0, m, 0).then_inc(a_tap, 1)
                split(u + 8, i=i, per=8)
                act.wait_ge(a_conv, m + 1)
                nc.scalar.activation(ta[:], va[:], ACT.Square, scale=GELU_CUBE ** 0.5).then_inc(a_sq, 1)
                split(u + 9, i=i, per=8)
                act.wait_ge(a_arg, m + 1)
                nc.scalar.activation(ta[:], ta[:], ACT.Tanh, scale=GELU_SCALE).then_inc(a_tanh, 1)
                split(u + 10, i=i, per=8)
                split(u + 11, i=i, per=8)
                act.wait_ge(unit_used, u + 8 + 8 * i)
                tap(vv, 2, m, FB).then_inc(v_tap, 1)
                act.wait_ge(f_ready, m + 1)
                nc.scalar.mul(ft_hi[:, bass.ds(kt, 4), :], tb[:], 0.5).then_inc(f_hi, 1)

            with act.Fori(0, UP0) as i:
                up(U_UP0, i, 4 * i, i)
            with act.Fori(0, 2) as i:
                for n in range(2):
                    u = U_DOWN0 + UP0 * n
                    for k in range(UP0):
                        split(u + 4 + k, i=i, per=2 * UP0)
                    act.wait_ge(unit_used, u + UP0 + 2 * UP0 * i)
                    for q in range(NT):
                        last = nc.scalar.copy(acc[:, q, bass.ds(1024 * i + 512 * n, CH)], bank[4 + 2 * n + q][:])
                    last.then_inc(evac[2 + n], 1)
            with act.Fori(0, UP1) as i:
                up(U_UP1, i + UP0, 4 * i, i)
            for n in range(4):
                for k in range(UP1):
                    if UP1 * n + k + 4 < U_END - U_DOWN1:
                        split(U_DOWN1 + UP1 * n + 4 + k)
                act.wait_ge(evac[2 + n % 2], (19 if n % 2 == 0 else 4) + n // 2)
                for q in range(NT):
                    last = nc.scalar.activation(junk_f[:], acc[:, q, 512 * n:512 * n + CH], ACT.Square, accum_out=stat[:, 4 * q + n:4 * q + n + 1])
                    act.drain()
                last.then_inc(down_sq, 1)

        @block.vector
        def _(dve):
            def split(u, width=2048, i=0, per=0):
                dve.wait_ge(hi_done, u + 1 + per * i)
                nc.vector.tensor_tensor(wlo[:, u % 4, 0:width], raw[:, u % 2, 0:width],
                                        whi[:, u % 4, 0:width].bitcast(F32), ALU.subtract).then_inc(lo_done, 1)

            def root(dst, src, n, scale, eps=EPS):
                v, g, w = scr[:, 0:n], scr[:, 8:8 + n], scr[:, 16:16 + n]
                nc.vector.tensor_scalar(v, src, scale, eps, ALU.mult, ALU.add)
                dve.drain()
                nc.vector.tensor_scalar(g.bitcast(I32), v.bitcast(I32), 1, None, ALU.logical_shift_right)
                dve.drain()
                nc.vector.tensor_scalar(dst.bitcast(I32), g.bitcast(I32), -1.0, float(0x5F3759DF), ALU.mult, ALU.add)
                dve.drain()
                for _ in range(3):
                    nc.vector.tensor_tensor(w, dst, dst, ALU.mult)
                    dve.drain()
                    nc.vector.scalar_tensor_tensor(w, w, -0.5, v, ALU.mult, ALU.mult)
                    dve.drain()
                    nc.vector.scalar_tensor_tensor(dst, w, 1.5, dst, ALU.add, ALU.mult)
                    dve.drain()

            def transposed_lo(n0, dst_hi, dst, gain, scale=1.0, groups=range(8)):
                for g in groups:
                    b = tp_bank(n0 + g)
                    dve.wait_ge(tp_hi, n0 + g + 1)
                    for k in range(2):
                        last = nc.vector.scalar_tensor_tensor(
                            dst[:, 2 * g + k, :], b[:, k * S:(k + 1) * S],
                            par[:, gain + 2 * g + k:gain + 2 * g + k + 1] if gain is not None else scale,
                            dst_hi[:, 2 * g + k, :].bitcast(F32), ALU.mult, ALU.subtract)
                    last.then_inc(tp_lo, 1)

            def mem_softmax(h):
                dve.wait_ge(ms_done, h + 1)
                nc.vector.tensor_reduce(stat[:, 0:2], bank[6][:].rearrange("p (q m) -> p q m", q=NT), AX_X, ALU.max)
                dve.drain()
                nc.vector.tensor_scalar(stat[:, 2:4], stat[:, 0:2], -MEM_SCALE, None, ALU.mult).then_inc(mnb, 1)
                dve.wait_ge(mexp, h + 1)
                nc.vector.reciprocal(stat[:, 6:8], stat[:, 4:6])
                dve.drain()
                for q in range(NT):
                    last = nc.vector.tensor_scalar(pmem[:, q, :], pmem[:, q, :], stat[:, 6 + q:7 + q], None, ALU.mult)
                last.then_inc(mprob, 1)

            def mem_probT(h):
                dve.wait_ge(mt_done, h + 1)
                nc.vector.tensor_copy(pmemT[:].rearrange("p a s -> p (a s)"), bank[7][:]).then_inc(mpT, 1)

            def mem_out_lo(h):
                dve.wait_ge(mo_hi, h + 1)
                for n in range(2):
                    last = nc.vector.tensor_tensor(ot_lo[:, bass.ds(4 * h + 2 * n, 2), :], bank[6 + n][:].rearrange("p (b s) -> p b s", b=2),
                                                   ot_hi[:, bass.ds(4 * h + 2 * n, 2), :].bitcast(F32), ALU.subtract)
                last.then_inc(mo_lo, 1)

            def mem_head(u, h, i=0, first=False):
                split(u + 4, i=i, per=12)
                if not first:
                    mem_softmax(h - 1)
                split(u + 5, i=i, per=12)
                split(u + 6, i=i, per=12)
                if not first:
                    mem_probT(h - 1)
                split(u + 7, i=i, per=12)
                dve.wait_ge(unit_used, u + 4 + 12 * i)
                nc.vector.tensor_copy(kmem[:, 2:4, :], bank[1][:].rearrange("p (b s) -> p b s", b=2)).then_inc(evac[0], 1)
                if first:
                    transposed_lo(8, ht_hi, ht_lo, PRE_MIX)
                for j in range(4):
                    split(u + 8 + j, i=i, per=12)
                    if j == 1 and not first:
                        mem_out_lo(h - 1)
                dve.wait_ge(unit_used, u + 8 + 12 * i)
                nc.vector.tensor_copy(vmem[:, 1, :], bank[3][:]).then_inc(evac[1], 1)
                for j in range(4):
                    split(u + 12 + j, i=i, per=12)
                dve.wait_ge(unit_used, u + 12 + 12 * i)
                nc.vector.tensor_copy(qmem[:, 2:4, :], bank[5][:].rearrange("p (b s) -> p b s", b=2)).then_inc(evac[2], 1)

            for n, src in enumerate((memin, xin)):
                dve.wait_ge(sq_done, n + 1)
                root(stat[:, 12 + 2 * n:14 + 2 * n], stat[:, 8 + 2 * n:10 + 2 * n], 2, 1.0 / D)
                for q in range(NT):
                    last = nc.vector.tensor_scalar(src[:, q, :], src[:, q, :], stat[:, 12 + 2 * n + q:13 + 2 * n + q], None, ALU.mult)
                last.then_inc(norm_done, 1)
            dve.wait_ge(par_done, 1)
            transposed_lo(0, memn_hi, memn_lo, MEM_G)
            for j in range(4):
                split(j)
            mem_head(0, 0, first=True)
            with dve.Fori(0, MEM_HEADS - 1) as i:
                mem_head(12, 1 + i, i)

            def gated(u, n, cc, i=0, fresh=False, side=(None, None, None, None)):
                for j in range(4):
                    split(u + 4 + j, i=i, per=8)
                    if side[j]:
                        side[j]()
                for j in range(4):
                    split(u + 8 + j, i=i, per=8)
                dve.wait_ge(evac[0], gates_from(n, i))
                dve.wait_ge(unit_used, u + 8 + 8 * i)
                for q in range(NT):
                    m = merged[:, q, bass.ds(cc, CH)]
                    if fresh:
                        last = nc.vector.scalar_tensor_tensor(m, tgate[:, q, :], 1.0, bank[2 + q][:], ALU.add, ALU.mult)
                    else:
                        last = nc.vector.scalar_tensor_tensor(tgate[:, q, :], tgate[:, q, :], 1.0, bank[2 + q][:], ALU.add, ALU.mult)
                last.then_inc(evac[1], 1)
                if fresh:
                    dve.drain().then_inc(gate_used, 1)
                else:
                    dve.drain()
                    for q in range(NT):
                        m = merged[:, q, bass.ds(cc, CH)]
                        last = nc.vector.tensor_tensor(m, m, tgate[:, q, :], ALU.add)
                    last.then_inc(gate_used, 1)

            gated(U_GC, 0, 0, fresh=True, side=(lambda: mem_softmax(3), None, lambda: mem_probT(3), lambda: mem_out_lo(3)))
            with dve.Fori(0, 3) as i:
                gated(U_GC + 8, 1, 512 + 512 * i, i, fresh=True)

            for j in range(4):
                split(U_CKV + j)
            dve.wait_ge(small_hi, 1)
            nc.vector.tensor_tensor(ki_lo[:], bank[0][:, 0:S], ki_hi[:].bitcast(F32), ALU.subtract)
            dve.wait_ge(evac[0], 13)
            nc.vector.tensor_scalar(widx[:], bank[1][:, 0:160].rearrange("p (q c) -> p q c", q=NT)[:, :, 0:16],
                                    IDX_W_SCALE, None, ALU.mult).then_inc(evac[0], 1)
            nc.vector.memset(score[:], 0.0)
            for j in range(4):
                split(U_QI + j)
            dve.wait_ge(ck_sq, 1)
            dve.wait_ge(kvg_in, 16)
            root(stat[:, 22:24], stat[:, 16:18], 2, 1.0 / RANK)
            for q in range(NT):
                last = nc.vector.scalar_tensor_tensor(ckv[:, q, :], bank[2 + q][:], stat[:, 22 + q:23 + q], kvg[:], ALU.mult, ALU.mult)
            last.then_inc(evac[1], 1)
            dve.wait_ge(ck_hi, 1)
            nc.vector.tensor_tensor(ckv_lo[:], ckv[:], ckv_hi[:].bitcast(F32), ALU.subtract).then_inc(ck_lo, 1)

            SEG = (slice(0, P), slice(P, 384))
            DIAG = (slice(0, P), slice(S, 384))

            def take_eight():
                for q in range(NT):
                    nc.vector.max(scr[:, 8 * q:8 * q + 8], score[:, SEG[q]])
                dve.drain()
                for q in range(NT):
                    nc.vector.match_replace(score[:, SEG[q]], scr[:, 8 * q:8 * q + 8], score[:, SEG[q]], MARK)
                dve.drain()

            def queries_lo(n):
                u = U_QI + 4 * n
                for j in range(4):
                    split(u + 4 + j, 1024 if n == 7 else 2048)
                    if n == 0 and j == 2:
                        dve.wait_ge(ckT_hi, 1)
                        for b in range(2):
                            last = nc.vector.tensor_tensor(ckvT_lo[:, 2 * b:2 * b + 2, :], bank[6 + b][:].rearrange("p (b s) -> p b s", b=2),
                                                           ckvT_hi[:, 2 * b:2 * b + 2, :].bitcast(F32), ALU.subtract)
                        last.then_inc(ckT_lo, 1)
                    if 1 <= n <= 4:
                        h = 4 * (n - 1) + j
                        dve.wait_ge(relu_done, h + 1)
                        dve.drain()
                        for q in range(NT):
                            last = nc.vector.scalar_tensor_tensor(score[:, SEG[q]], relu[:, h % 2, SEG[q]], widx[:, q, h:h + 1],
                                                                  score[:, SEG[q]], ALU.mult, ALU.add)
                        last.then_inc(relu_used, 1)
                    if n == 5:
                        if j == 0:
                            dve.drain()
                            for d in DIAG:
                                nc.vector.tensor_tensor(score[:, d], score[:, d], causneg[:], ALU.add)
                            dve.drain()
                        for _ in range(TOPK // 8 // 4):
                            take_eight()
                        if j == 3:
                            nc.vector.tensor_scalar(mask[:], score[:], TAKEN, MASKED, ALU.is_ge, ALU.mult)
                            dve.drain()
                            for d in DIAG:
                                nc.vector.tensor_tensor(mask[:, d], mask[:, d], causneg[:], ALU.add)
                            dve.drain()
                dve.wait_ge(q_hi, n + 1)
                for b in range(2):
                    k = slice(2 * b, 2 * b + 2) if n < 4 else slice(4 * (n - 4) + 2 * b, 4 * (n - 4) + 2 * b + 2)
                    hi, lo = (qi_hi[n % 2], qi_lo[n % 2]) if n < 4 else (ot_hi, ot_lo)
                    last = nc.vector.tensor_tensor(lo[:, k, :], bank[2 * (n % 2) + b][:].rearrange("p (b s) -> p b s", b=2),
                                                   hi[:, k, :].bitcast(F32), ALU.subtract)
                last.then_inc(evac[n % 2], 1)

            for n in range(8):
                queries_lo(n)

            def two_banks(hi, lo, n):
                for b in range(2):
                    last = nc.vector.tensor_tensor(lo[:, 2 * b:2 * b + 2, :], bank[n + b][:].rearrange("p (b s) -> p b s", b=2),
                                                   hi[:, 2 * b:2 * b + 2, :].bitcast(F32), ALU.subtract)
                return last

            def key_lo(h):
                dve.wait_ge(at_ql_hi, h + 1)
                two_banks(ql_hi, ql_lo, 0).then_inc(at_ql_lo, 1)

            def out_latent_lo(h):
                dve.wait_ge(at_ol_hi, h + 1)
                two_banks(ol_hi, ol_lo, 4).then_inc(at_ol_lo, 1)

            def out_lo(h):
                dve.wait_ge(at_o_hi, h + 1)
                nc.vector.tensor_tensor(ot_lo[:, bass.ds(h, 1), :].rearrange("p a s -> p (a s)"), bank[6][:, 0:S],
                                        ot_hi[:, bass.ds(h, 1), :].rearrange("p a s -> p (a s)").bitcast(F32), ALU.subtract).then_inc(at_o_lo, 1)

            def attention(h, first=False, last_head=False):
                dve.wait_ge(at_s, h + 1)
                nc.vector.scalar_tensor_tensor(prob[:], bank[2][:, 0:384], SCALE, mask[:], ALU.mult, ALU.add)
                dve.drain()
                for q in range(NT):
                    last = nc.vector.tensor_reduce(stat[:, 18 + q:19 + q], prob[:, SEG[q]], AX_X, ALU.max, negate=True)
                last.then_inc(at_nb, 1)
                if not first:
                    out_latent_lo(h - 1)
                dve.wait_ge(at_exp, h + 1)
                nc.vector.reciprocal(stat[:, 24:26], stat[:, 20:22])
                dve.drain()
                for q in range(NT):
                    last = nc.vector.tensor_scalar(prob[:, SEG[q]], prob[:, SEG[q]], stat[:, 24 + q:25 + q], None, ALU.mult)
                last.then_inc(at_p, 1)
                if not last_head:
                    key_lo(h + 1)
                dve.wait_ge(at_t_hi, h + 1)
                nc.vector.tensor_tensor(pT_lo[:], bank[3][:, 0:384], pT_hi[:].bitcast(F32), ALU.subtract).then_inc(at_t_lo, 1)
                if not first:
                    out_lo(h - 1)

            key_lo(0)
            attention(0, first=True)
            attention(1)
            with dve.Fori(0, 3) as i:
                for k in range(4):
                    attention(2 + k + 4 * i)
                    if k % 2 == 0:
                        split(U_ATT + 4 + k, 1024, i, 4)
                        split(U_ATT + 5 + k, 1024, i, 4)
            attention(14)
            for j in range(3):
                split(U_GA + j)
            attention(15, last_head=True)
            out_latent_lo(15)
            out_lo(15)
            split(U_GA + 3)

            gated(U_GA, 4, 0)
            with dve.Fori(0, 3) as i:
                gated(U_GA + 8, 5, 512 + 512 * i, i)

            def heads(row, g, width):
                return row[:, bass.ds(HPG * g, HPG)].unsqueeze(2).to_broadcast([P, HPG, width])

            def conv_taps(first_block, dst, banks, blocks, tap, done, g):
                dve.wait_ge(tap, g + 1)
                for s in range(1, 4):
                    for b in range(blocks):
                        src = banks[b // 2][:, (b % 2) * S:(b % 2 + 1) * S - s]
                        last = nc.vector.scalar_tensor_tensor(dst[:, b, s:S], src, par[:, bass.ds(CONV_W + (3 - s) * CONV_BLK + first_block[b], 1)],
                                                              dst[:, b, s:S], ALU.mult, ALU.add)
                    if s < 3:
                        dve.drain()
                last.then_inc(done, 1)

            def silu(dst, half, tanh, ready, g):
                dve.wait_ge(tanh, g + 1)
                nc.vector.scalar_tensor_tensor(dst[:], dst[:], 1.0, half[:], ALU.add, ALU.mult).then_inc(ready, 1)

            def core_inputs(g):
                dve.wait_ge(core_in, g + 1)
                for c in range(NT):
                    b = bank[5 + c][:].rearrange("p (h d) -> p h d", h=HPG)
                    nc.vector.tensor_tensor(xdt[:, c, :].rearrange("p (h d) -> p h d", h=HPG), b, heads(dt[:, c, :], g, SHD), ALU.mult)
                    last = nc.vector.tensor_tensor(y[:, c, :].rearrange("p (h d) -> p h d", h=HPG), b, heads(rows[:, 2, :], g, SHD), ALU.mult)
                last.then_inc(core_x, 1)
                dve.drain()
                nc.vector.tensor_tensor(xdd[:].rearrange("p (h d) -> p h d", h=HPG), xdt[:, 0, :].rearrange("p (h d) -> p h d", h=HPG),
                                        heads(edec, g, SHD), ALU.mult)
                dve.wait_ge(core_btok, g + 1)
                nc.vector.tensor_tensor(cb[:], bank[7][:, P:384].rearrange("p (c l) -> p c l", c=NT),
                                        tri[:].unsqueeze(1).to_broadcast([P, NT, P]), ALU.mult).then_inc(core_cb, 1)

            def segment(g, c):
                dve.wait_ge(cum_done, 2 * g + c + 1)
                for n in range(2):
                    nc.vector.tensor_tensor(dec[:, 4 * n:4 * n + 4, :], bank[5 + n][:].rearrange("p (h l) -> p h l", h=4),
                                            acum[:, c, bass.ds(HPG * g + 4 * n, 4)].unsqueeze(2).to_broadcast([P, 4, P]), ALU.subtract)
                dve.drain()
                nc.vector.tensor_scalar(dec[:], dec[:], 0.0, None, ALU.min).then_inc(seg_done, 1)

            def mixing(g, c):
                dve.wait_ge(dec_done, 2 * g + c + 1)
                nc.vector.tensor_tensor(dec[:], dec[:], cb[:, c, :].unsqueeze(1).to_broadcast([P, HPG, P]), ALU.mult).then_inc(m_ready, 1)

            def add_first(g):
                dve.wait_ge(yd_done, 2 * g + 1)
                nc.vector.tensor_tensor(y[:, 0, :], y[:, 0, :], bank[7][:], ALU.add).then_inc(y0_done, 1)

            def add_second(g):
                dve.wait_ge(yoff_done, g + 1)
                nc.vector.tensor_tensor(y[:, 1, :], y[:, 1, :], bank[5][:], ALU.add)
                nc.vector.tensor_tensor(xdd[:].rearrange("p (h d) -> p h d", h=HPG), bank[6][:].rearrange("p (h d) -> p h d", h=HPG),
                                        heads(eacum, g, SHD), ALU.mult)
                dve.drain()
                nc.vector.tensor_tensor(y[:, 1, :], y[:, 1, :], xdd[:], ALU.add)
                dve.drain()

            def gate_and_norm(g):
                nc.vector.tensor_tensor(y[:], y[:], zs[:], ALU.mult)
                dve.drain()
                for c in range(NT):
                    nc.vector.tensor_tensor_reduce(out=xdt[:, c, :], in0=y[:, c, :], in1=y[:, c, :], scale=1.0, scalar=0.0,
                                                   op0=ALU.mult, op1=ALU.add, accum_out=stat[:, 26 + c:27 + c])
                dve.drain()
                root(stat[:, 28:30], stat[:, 26:28], 2, 0.25 / CH)
                for c in range(NT):
                    last = nc.vector.tensor_scalar(y[:, c, :], y[:, c, :], stat[:, 28 + c:29 + c], 0.5, ALU.mult, ALU.mult)
                last.then_inc(y_ready, 1)

            def y_lo(g, kt):
                dve.wait_ge(yT_hi, g + 1)
                for b in range(4):
                    src = bank[7 if b < 2 else 5][:, (b % 2) * S:(b % 2 + 1) * S]
                    last = nc.vector.scalar_tensor_tensor(ot_lo[:, bass.ds(kt + b, 1), :].rearrange("p a s -> p (a s)"), src,
                                                          par[:, bass.ds(SSD_G + 4 * g + b, 1)],
                                                          ot_hi[:, bass.ds(kt + b, 1), :].rearrange("p a s -> p (a s)").bitcast(F32), ALU.mult, ALU.subtract)
                last.then_inc(yT_lo, 1)

            def group(u, g, kt, i=0, core=True):
                split(u + 4, 1024, i, 12)
                if core:
                    core_inputs(g - 1)
                split(u + 5, 1024, i, 12)
                if core:
                    segment(g - 1, 0)
                split(u + 6, 1024, i, 12)
                if core:
                    mixing(g - 1, 0)
                split(u + 7, 1024, i, 12)
                conv_taps([4 * g + b for b in range(4)], xv, bank[0:2], 4, x_tap, x_conv, g)
                dve.drain().then_inc(evac[0], 1)
                split(u + 8, 2048, i, 12)
                if core:
                    dve.wait_ge(yd_done, 2 * g - 1)
                    segment(g - 1, 1)
                silu(xT, xv, x_tanh, x_ready, g)
                if core:
                    add_first(g - 1)
                split(u + 9, 2048, i, 12)
                if core:
                    mixing(g - 1, 1)
                split(u + 10, 2048, i, 12)
                if core:
                    add_second(g - 1)
                split(u + 11, 2048, i, 12)
                conv_taps([XBLK + g, XBLK + GROUPS + g], bcv, bank[2:3], 2, bc_tap, bc_conv, g)
                dve.drain().then_inc(evac[1], 1)
                split(u + 12, 2048, i, 12)
                if core:
                    gate_and_norm(g - 1)
                split(u + 13, 2048, i, 12)
                silu(bcT, bcv, bc_tanh, bc_ready, g)
                split(u + 14, 2048, i, 12)
                if core:
                    y_lo(g - 1, kt)
                split(u + 15, 2048, i, 12)
                dve.wait_ge(z_tanh, g + 1)
                for q in range(NT):
                    last = nc.vector.scalar_tensor_tensor(zs[:, q, :], zs[:, q, :], 1.0, bank[3 + q][:], ALU.add, ALU.mult)
                last.then_inc(evac[2], 1)

            dve.wait_ge(row_in, 48)
            two = lambda ap: ap.rearrange("p (q h) -> p q h", q=NT)
            v, r, nv, e, w, ln, d1, eq = (tmp[:, k, :] for k in range(8))
            nc.vector.tensor_tensor(two(v), dt[:], rows[:, 0, :].unsqueeze(1).to_broadcast([P, NT, 64]), ALU.add)
            dve.drain()
            nc.vector.tensor_scalar(r, v, 0.0, None, ALU.max)
            dve.drain()
            nc.vector.scalar_tensor_tensor(nv, r, -2.0, v, ALU.mult, ALU.add).then_inc(pre_n, 1)
            dve.wait_ge(pre_u, 1)
            nc.vector.tensor_scalar(w, e, 1.0, None, ALU.add).then_inc(pre_w, 1)
            dve.drain()
            nc.vector.tensor_scalar(d1, w, -1.0, None, ALU.add)
            dve.drain()
            nc.vector.tensor_scalar(eq, d1, 0.0, None, ALU.is_equal)
            dve.drain()
            nc.vector.tensor_tensor(d1, d1, eq, ALU.add)
            nc.vector.tensor_tensor(eq, eq, e, ALU.mult)
            dve.drain()
            nc.vector.reciprocal(d1, d1)
            dve.drain()
            nc.vector.tensor_tensor(d1, d1, e, ALU.mult)
            dve.drain()
            dve.wait_ge(pre_ln, 1)
            nc.vector.tensor_tensor(ln, ln, d1, ALU.mult)
            nc.vector.tensor_tensor(r, r, eq, ALU.add)
            dve.drain()
            nc.vector.tensor_tensor(dt[:], two(r), two(ln), ALU.add)
            dve.drain()
            nc.vector.scalar_tensor_tensor(da[:], dt[:], -1.0, rows[:, 1, :].unsqueeze(1).to_broadcast([P, NT, 64]), ALU.mult, ALU.mult).then_inc(pre_da, 1)
            dve.wait_ge(pre_cum, 1)
            nc.vector.tensor_copy(acum[:].rearrange("p q h -> p (q h)"), bank[5][:, 0:P])
            dve.drain()
            nc.vector.tensor_tensor(edec[:], bank[6][:, 0:64], acum[:, 0, :], ALU.subtract).then_inc(pre_dec, 1)
            dve.wait_ge(pre_done, 1)

            group(U_S0, 0, 0, core=False)
            with dve.Fori(0, 4) as i:
                group(U_S0 + 12, 1 + i, 4 * i, i)

            def gate_b(u, n, cc, i=0):
                for j in range(8):
                    split(u + 4 + j, i=i, per=8)
                dve.wait_ge(evac[0], gates_from(n, i))
                dve.wait_ge(unit_used, u + 8 + 8 * i)
                add_gated(2, cc, evac[1])

            def add_gated(b, cc, done):
                for q in range(NT):
                    last = nc.vector.scalar_tensor_tensor(gprod[:, q, :], tgate_b[:, q, :], 1.0, bank[b + q][:], ALU.add, ALU.mult)
                last.then_inc(done, 1)
                dve.drain()
                for q in range(NT):
                    m = merged[:, q, bass.ds(cc, CH)]
                    last = nc.vector.tensor_tensor(m, m, gprod[:, q, :], ALU.add)
                last.then_inc(gate_used, 1)

            gate_b(U_GB, 8, 0)
            with dve.Fori(0, 3) as i:
                gate_b(U_GB + 8, 9, 512 + 512 * i, i)
            dve.drain()
            with dve.Fori(0, 3) as i:
                group(U_S5, 5 + i, 4 * i, i)
            split(U_B2 + 4)
            core_inputs(7)
            split(U_B2 + 5)
            segment(7, 0)
            split(U_B2 + 6)
            mixing(7, 0)
            dve.wait_ge(yd_done, 15)
            segment(7, 1)
            add_first(7)
            mixing(7, 1)
            add_second(7)
            gate_and_norm(7)
            y_lo(7, 12)
            split(U_B2 + 7)
            for n in range(4):
                if n > 1:
                    transposed_lo(16, ht_hi, ht_lo, None, 0.5, range(2 * n - 4, 2 * n - 2))
                if n:
                    for j in range(4):
                        split(U_B2 + 4 * n + 4 + j)
                dve.wait_ge(unit_used, U_B2 + 4 * n + 4)
                dve.wait_ge(gate_back, 16 * n + 16)
                add_gated(2 * (n % 2), 512 * n, evac[n % 2])
            transposed_lo(16, ht_hi, ht_lo, None, 0.5, range(4, 8))

            dve.wait_ge(late_in, 16)
            with dve.Fori(0, 2) as i:
                for n in range(2):
                    for j in range(4):
                        split(U_OUT + 4 * n + 4 + j, i=i, per=8)
                    dve.wait_ge(mix_sq, n + 1 + 2 * i)
                    c = bass.ds(512 * n + 1024 * i, CH)
                    for q in range(NT):
                        last = nc.vector.tensor_tensor(mix[:, q, c], bank[2 * n + q][:], grow[:, c], ALU.mult)
                    last.then_inc(evac[n], 1)
            nc.vector.tensor_reduce(stat[:, 8:10], stat[:, 0:8].rearrange("p (q n) -> p q n", q=NT), AX_X, ALU.add)
            dve.drain()
            root(stat[:, 10:12], stat[:, 8:10], 2, 1.0 / D)
            dve.wait_ge(x_again, 16)
            for q in range(NT):
                nc.vector.scalar_tensor_tensor(x1[:, q, :], mix[:, q, :], stat[:, 10 + q:11 + q], x1[:, q, :], ALU.mult, ALU.add).then_inc(x1_ready, 1)
            for q in range(NT):
                dve.wait_ge(x1_sq, q + 1)
                root(stat[:, 14 + q:15 + q], stat[:, 12 + q:13 + q], 1, 1.0 / D)
                nc.vector.tensor_scalar(diag[:, q, :], ident[:], stat[:, 14 + q:15 + q], None, ALU.mult).then_inc(diag_ready, 1)
            transposed_lo(24, ht_hi, ht_lo, PRE_FFN)
            dve.drain().then_inc(evac[3], 1)
            dve.wait_ge(x1_out, 16)

            def ffn_taps(dst, b0, m, first_block):
                for s in range(1, 3):
                    for b in range(4):
                        src = bank[b0 + b // 2][:, (b % 2) * S:(b % 2 + 1) * S - s]
                        w = FFN_W + (2 - s) * 2 * FB + 4 * m + first_block + b
                        last = nc.vector.scalar_tensor_tensor(dst[:, b, s:S], src, par[:, bass.ds(w, 1)], dst[:, b, s:S], ALU.mult, ALU.add)
                    if s < 2:
                        dve.drain()
                return last

            def up(u, m, kt, i):
                for j in range(4):
                    split(u + 4 + j, i=i, per=8)
                dve.wait_ge(a_tap, m + 1)
                ffn_taps(va, 0, m, 0).then_inc(a_conv, 1)
                dve.drain().then_inc(evac[0], 1)
                split(u + 8, i=i, per=8)
                dve.wait_ge(a_sq, m + 1)
                nc.vector.scalar_tensor_tensor(ta[:], ta[:], 1.0, va[:], ALU.add, ALU.mult).then_inc(a_arg, 1)
                split(u + 9, i=i, per=8)
                dve.wait_ge(a_tanh, m + 1)
                nc.vector.scalar_tensor_tensor(va[:], ta[:], 1.0, va[:], ALU.add, ALU.mult)
                split(u + 10, i=i, per=8)
                split(u + 11, i=i, per=8)
                dve.wait_ge(v_tap, m + 1)
                ffn_taps(vv, 2, m, FB).then_inc(evac[1], 1)
                dve.drain()
                nc.vector.tensor_tensor(tb[:], va[:], vv[:], ALU.mult).then_inc(f_ready, 1)
                dve.wait_ge(f_hi, m + 1)
                nc.vector.scalar_tensor_tensor(ft_lo[:, bass.ds(kt, 4), :], tb[:], 0.5, ft_hi[:, bass.ds(kt, 4), :].bitcast(F32),
                                               ALU.mult, ALU.subtract).then_inc(f_lo, 1)

            with dve.Fori(0, UP0) as i:
                up(U_UP0, i, 4 * i, i)
            with dve.Fori(0, 2) as i:
                for k in range(2 * UP0):
                    split(U_DOWN0 + 4 + k, i=i, per=2 * UP0)
            with dve.Fori(0, UP1) as i:
                up(U_UP1, i + UP0, 4 * i, i)
            for n in range(4):
                for k in range(UP1):
                    if UP1 * n + k + 4 < U_END - U_DOWN1:
                        split(U_DOWN1 + UP1 * n + 4 + k)
                dve.wait_ge(unit_used, U_DOWN1 + UP1 * n + UP1)
                c = slice(512 * n, 512 * n + CH)
                for q in range(NT):
                    last = nc.vector.tensor_tensor(acc[:, q, c], acc[:, q, c], bank[4 + 2 * (n % 2) + q][:], ALU.add)
                last.then_inc(evac[2 + n % 2], 1)
                if n == 0:
                    dve.wait_ge(x1_in, 32)
                dve.wait_ge(down_sq, n + 1)
                nc.vector.tensor_tensor(acc[:, :, c], acc[:, :, c], frow[:, c].unsqueeze(1).to_broadcast([P, NT, CH]), ALU.mult)
            nc.vector.tensor_reduce(stat[:, 8:10], stat[:, 0:8].rearrange("p (q n) -> p q n", q=NT), AX_X, ALU.add)
            dve.drain()
            root(stat[:, 10:12], stat[:, 8:10], 2, 1.0 / D)
            for n in range(4):
                c = slice(n % 2 * 1024, n % 2 * 1024 + 1024)
                nc.vector.scalar_tensor_tensor(acc[:, n // 2, c], acc[:, n // 2, c], stat[:, 10 + n // 2:11 + n // 2], x1b[:, n // 2, c],
                                               ALU.mult, ALU.add).then_inc(y_out, 1)

        @block.tensor
        def _(pe):
            def products_t(u, banks, mov_hi, mov_lo, kt, first, last, blocks=4, i=0, per=0, width=CH):
                pe.wait_ge(lo_done, u + 1 + per * i)
                hi = whi[:, u % 4, 0:4 * width].rearrange("p (k c) -> p k c", k=4)
                lo = wlo[:, u % 4, 0:4 * width].rearrange("p (k c) -> p k c", k=4)
                for k in range(4):
                    for b in range(blocks):
                        o = banks[b // 2][:, (b % 2) * S:(b % 2 + 1) * S]
                        c = slice(b * P, (b + 1) * P)
                        for n, (w, m) in enumerate(((hi, mov_hi), (hi, mov_lo), (lo, mov_hi))):
                            mm = nc.tensor.matmul(o, w[:, k, c], m[:, kt + k, :],
                                                  start=first and k == 0 and b % 2 == 0 and n == 0,
                                                  stop=last and k == 3 and n == 2, skip_group_check=True)
                mm.then_inc(unit_used, 1)

            def products(u, banks, sta_hi, sta_lo, kt, first, last, i=0, per=0):
                pe.wait_ge(lo_done, u + 1 + per * i)
                hi = whi[:, u % 4, :].rearrange("p (k c) -> p k c", k=4)
                lo = wlo[:, u % 4, :].rearrange("p (k c) -> p k c", k=4)
                for k in range(4):
                    for q in range(NT):
                        c = slice(q * P, (q + 1) * P)
                        for n, (s, w) in enumerate(((sta_hi, hi), (sta_hi, lo), (sta_lo, hi))):
                            mm = nc.tensor.matmul(banks[q][:, :], s[:, kt + k, c], w[:, k, :],
                                                  start=first and k == 0 and n == 0,
                                                  stop=last and k == 3 and n == 2, skip_group_check=True)
                mm.then_inc(unit_used, 1)

            def transposes(n0, src, waits, groups=range(8)):
                for g in groups:
                    if waits and g >= waits:
                        pe.wait_ge(tp_lo, n0 + g - waits + 1)
                    b = tp_bank(n0 + g)
                    for k in range(2):
                        for q in range(NT):
                            mm = nc.tensor.transpose(b[:, k * S + q * P:k * S + (q + 1) * P],
                                                     src[:, q, (2 * g + k) * P:(2 * g + k + 1) * P], ident[:])
                    mm.then_inc(tp_done, 1)

            def mem_scores(h, k):
                pe.wait_ge(evac[0], k)
                pe.wait_ge(evac[2], k)
                for q in range(NT):
                    for b in range(4):
                        mm = nc.tensor.matmul(bank[6][:, q * S:(q + 1) * S], qmem[:, b, q * P:(q + 1) * P], kmem[:, b, :],
                                              start=b == 0, stop=b == 3)
                mm.then_inc(ms_done, 1)

            def mem_transpose(h):
                pe.wait_ge(mprob, h + 1)
                for q in range(NT):
                    for m in range(NT):
                        mm = nc.tensor.transpose(bank[7][:, m * S + q * P:m * S + (q + 1) * P],
                                                 pmem[:, q, m * P:(m + 1) * P], ident[:])
                mm.then_inc(mt_done, 1)

            def mem_out(h, k):
                pe.wait_ge(mpT, h + 1)
                pe.wait_ge(evac[1], k)
                for b in range(4):
                    for m in range(NT):
                        mm = nc.tensor.matmul(bank[6 + b // 2][:, (b % 2) * S:(b % 2 + 1) * S],
                                              vmem[:, m, b * P:(b + 1) * P], pmemT[:, m, :], start=m == 0, stop=m == NT - 1)
                mm.then_inc(mo_done, 1)

            def mem_head(u, h, i=0, first=False):
                if not first:
                    pe.wait_ge(evac[0], 2 * h)
                for j in range(4):
                    products_t(u + j, bank[0:2], memn_hi, memn_lo, 4 * j, j == 0, j == 3, i=i, per=12)
                    if j == 0 and not first:
                        mem_scores(h - 1, 2 * h)
                    if j == 2 and not first:
                        mem_transpose(h - 1)
                if first:
                    pe.wait_ge(norm_done, 2)
                    transposes(8, xin, 6)
                    pe.wait_ge(tp_lo, 16)
                else:
                    pe.wait_ge(evac[1], 2 * h)
                for j in range(4):
                    products(u + 4 + j, bank[2:4], memn_hi, memn_lo, 4 * j, j == 0, j == 3, i=i, per=12)
                    if j == 0 and not first:
                        mem_out(h - 1, 2 * h)
                if not first:
                    pe.wait_ge(evac[2], 2 * h)
                    pe.wait_ge(mo_lo, h)
                for j in range(4):
                    products_t(u + 8 + j, bank[4:6], ht_hi, ht_lo, 4 * j, j == 0, j == 3, i=i, per=12)

            pe.wait_ge(consts, 1)
            pe.wait_ge(par_in, 176)
            for n, (r, c) in enumerate(((128, 0), (96, 128), (96, 224), (88, 0), (88, 88), (88, 176), (88, 264))):
                mm = nc.tensor.transpose(bank[n >= 3][:, c:c + r], stage[0:r, n, :], ident[0:r, 0:r])
            mm.then_inc(par_tp, 1)
            pe.wait_ge(norm_done, 1)
            pe.wait_ge(par_done, 1)
            transposes(0, memin, 0)
            pe.wait_ge(tp_lo, 8)
            mem_head(0, 0, first=True)
            with pe.Fori(0, MEM_HEADS - 1) as i:
                mem_head(12, 1 + i, i)

            def gated(u, e0, e1, sta_hi, sta_lo, kt, i=0, side=(None, None, None, None), ready=None):
                pe.wait_ge(evac[0], e0 + i)
                for j in range(4):
                    products(u + j, bank[0:2], ht_hi, ht_lo, 4 * j, j == 0, j == 3, i=i, per=8)
                    if side[j]:
                        side[j]()
                pe.wait_ge(evac[1], e1 + i)
                if ready:
                    ready()
                for j in range(4):
                    products(u + 4 + j, bank[2:4], sta_hi, sta_lo, kt + 4 * j, j == 0, j == 3, i=i, per=8)

            gated(U_GC, 8, 8, ot_hi, ot_lo, 0,
                  side=(lambda: mem_scores(3, 8), None, lambda: mem_transpose(3), lambda: mem_out(3, 8)),
                  ready=lambda: pe.wait_ge(mo_lo, 4))
            with pe.Fori(0, 3) as i:
                gated(U_GC + 8, 9, 9, ot_hi, ot_lo, 0, i)

            pe.wait_ge(evac[0], 12)
            for j in range(4):
                pe.wait_ge(lo_done, U_SMALL + j + 1)
                width = 144 if j < 2 else 64
                hi = whi[:, j, 0:8 * width].rearrange("p (k c) -> p k c", k=8)
                lo = wlo[:, j, 0:8 * width].rearrange("p (k c) -> p k c", k=8)
                for k in range(8):
                    kt = 8 * (j % 2) + k
                    first, last = kt == 0, kt == KT - 1
                    if j < 2:
                        for n, (w, m) in enumerate(((hi, ht_hi), (hi, ht_lo), (lo, ht_hi))):
                            nc.tensor.matmul(bank[0][:, 0:S], w[:, k, 0:P], m[:, kt, :], start=first and n == 0, stop=last and n == 2)
                    c, o = (slice(P, 144), 0) if j < 2 else (slice(0, 64), 16)
                    for q in range(NT):
                        for n, (x, w) in enumerate(((ht_hi, hi), (ht_hi, lo), (ht_lo, hi))):
                            mm = nc.tensor.matmul(bank[1][:, 80 * q + o:80 * q + o + c.stop - c.start], x[:, kt, q * P:(q + 1) * P], w[:, k, c],
                                                  start=j == 0 and first and n == 0 and q == 0, stop=last and n == 2, skip_group_check=True)
                mm.then_inc(unit_used, 1)
            pe.wait_ge(evac[1], 12)
            for j in range(4):
                products(U_CKV + j, bank[2:4], ht_hi, ht_lo, 4 * j, j == 0, j == 3)

            def latent_transpose():
                pe.wait_ge(evac[1], 13)
                for b in range(4):
                    for q in range(NT):
                        mm = nc.tensor.transpose(bank[6 + b // 2][:, (b % 2) * S + q * P:(b % 2) * S + (q + 1) * P],
                                                 ckv[:, q, b * P:(b + 1) * P], ident[:])
                mm.then_inc(ckT_done, 1)

            def index_logits(n, h):
                hi, lo = qi_hi[n % 2], qi_lo[n % 2]
                if h < 2:
                    pe.wait_ge(ckT_lo, 1)
                else:
                    pe.wait_ge(relu_done, h - 1)
                for q, o in enumerate((slice(0, P), slice(P, 384))):
                    for k, (a, b) in enumerate(((hi, ki_hi), (hi, ki_lo), (lo, ki_hi))):
                        mm = nc.tensor.matmul(bank[6 + h % 2][:, o], a[:, h % 4, q * P:(q + 1) * P], b[:, 0:(q + 1) * P],
                                              start=k == 0, stop=k == 2)
                mm.then_inc(idx_done, 1)

            for n in range(8):
                p = n % 2
                pe.wait_ge(evac[p], (14 if p == 0 else 13) + n // 2)
                for j in range(4):
                    products_t(U_QI + 4 * n + j, bank[2 * p:2 * p + 2], ht_hi, ht_lo, 4 * j, j == 0, j == 3)
                    if n == 0 and j == 2:
                        latent_transpose()
                    if 1 <= n <= 4:
                        if j == 0:
                            pe.wait_ge(evac[1 - p], (14 if p == 1 else 13) + (n - 1) // 2 + 1)
                        index_logits(n - 1, 4 * (n - 1) + j)

            def key_latent(h, hs, i=0):
                u = U_ATT + key_unit(hs // 2)
                pe.wait_ge(lo_done, u + 1 + 4 * i)
                c = 512 * (hs % 2)
                for b in range(4):
                    for n, (w, m) in enumerate(((whi, ot_hi), (whi, ot_lo), (wlo, ot_hi))):
                        mm = nc.tensor.matmul(bank[b // 2][:, (b % 2) * S:(b % 2 + 1) * S], w[:, u % 4, c + b * P:c + (b + 1) * P],
                                              m[:, bass.ds(h, 1), :].rearrange("p a s -> p (a s)"), start=n == 0, stop=n == 2)
                if hs % 2:
                    mm.then_inc(unit_used, 1)
                    pe.drain().then_inc(at_ql, 1)
                else:
                    mm.then_inc(at_ql, 1)

            def logits(h):
                pe.wait_ge(at_ql_lo, h + 1)
                for q, o in enumerate((slice(0, P), slice(P, 384))):
                    for b in range(4):
                        for n, (a, c) in enumerate(((ql_hi, ckvT_hi), (ql_hi, ckvT_lo), (ql_lo, ckvT_hi))):
                            mm = nc.tensor.matmul(bank[2][:, o], a[:, b, q * P:(q + 1) * P], c[:, b, 0:(q + 1) * P],
                                                  start=b == 0 and n == 0, stop=b == 3 and n == 2)
                mm.then_inc(at_s, 1)

            def out_latent(h):
                pe.wait_ge(at_t_lo, h + 1)
                for b in range(4):
                    o = bank[4 + b // 2][:, (b % 2) * S:(b % 2 + 1) * S]
                    for m in range(NT):
                        src = slice(0, S) if m == 0 else slice(S, 384)
                        for n, (c, x) in enumerate(((ckv_hi, pT_hi), (ckv_hi, pT_lo), (ckv_lo, pT_hi))):
                            mm = nc.tensor.matmul(o[:, m * P:S], c[:, m, b * P:(b + 1) * P], x[:, src],
                                                  start=m == 0 and n == 0, stop=m == 1 and n == 2, skip_group_check=True)
                mm.then_inc(at_ol, 1)

            def prob_transpose(h):
                pe.wait_ge(at_p, h + 1)
                for dst, src in ((0, 0), (P, P), (S, S)):
                    mm = nc.tensor.transpose(bank[3][:, dst:dst + P], prob[:, src:src + P], ident[:])
                mm.then_inc(at_t, 1)

            def head_out(h, hs, i=0, waits=True):
                u = U_ATT + value_unit(hs // 2)
                pe.wait_ge(lo_done, u + 1 + 4 * i)
                pe.wait_ge(at_ol_lo, h + 1)
                if waits:
                    pe.wait_ge(at_o_lo, h)
                for b in range(4):
                    c = 512 * (hs % 2) + b * P
                    for n, (w, m) in enumerate(((whi, ol_hi), (whi, ol_lo), (wlo, ol_hi))):
                        mm = nc.tensor.matmul(bank[6][:, 0:S], w[:, u % 4, c:c + P], m[:, b, :], start=b == 0 and n == 0, stop=b == 3 and n == 2)
                if hs % 2:
                    mm.then_inc(unit_used, 1)
                    pe.drain().then_inc(at_o, 1)
                else:
                    mm.then_inc(at_o, 1)

            def attention(h, hs, i=0, first=False, last_head=False):
                logits(h)
                if not first:
                    out_latent(h - 1)
                if not last_head:
                    key_latent(h + 1, hs + 1, i)
                prob_transpose(h)
                if not first:
                    head_out(h - 1, hs - 1, i, waits=hs >= 2)

            pe.wait_ge(evac[0], 18)
            pe.wait_ge(evac[1], 17)
            pe.wait_ge(ck_lo, 1)
            key_latent(0, 0)
            attention(0, 0, first=True)
            attention(1, 1)
            with pe.Fori(0, 3) as i:
                for k in range(4):
                    attention(2 + k + 4 * i, 2 + k, i)
            attention(14, 14)
            attention(15, 15, last_head=True)
            out_latent(15)
            head_out(15, 15)

            gated(U_GA, 18, 17, ot_hi, ot_lo, 0, ready=lambda: pe.wait_ge(at_o_lo, 16))
            with pe.Fori(0, 3) as i:
                gated(U_GA + 8, 19, 18, ot_hi, ot_lo, 0, i)

            def core_transposes(g):
                pe.wait_ge(x_ready, g + 1)
                pe.wait_ge(bc_ready, g + 1)
                for c in range(NT):
                    for b in range(4):
                        nc.tensor.transpose(bank[5 + c][:, b * P:(b + 1) * P], xT[:, b, c * P:(c + 1) * P], ident[:])
                nc.tensor.transpose(bank[7][:, 0:P], bcT[:, 0, 0:P], ident[:])
                for c in range(NT):
                    mm = nc.tensor.matmul(bank[7][:, P + c * P:2 * P + c * P], bcT[:, 0, c * P:(c + 1) * P], bcT[:, 1, c * P:(c + 1) * P],
                                          start=True, stop=True)
                mm.then_inc(core_in, 1)

            def running_sums(g, c):
                pe.wait_ge(atri_done, 2 * g + c + 1)
                if c == 0:
                    pe.wait_ge(core_x, g + 1)
                else:
                    pe.wait_ge(seg_done, 2 * g + 1)
                for n in range(2):
                    mm = nc.tensor.matmul(bank[5 + n][:], ones[:], atri[:, 4 * n:4 * n + 4, :], start=True, stop=True)
                mm.then_inc(cum_done, 1)

            def diagonal(g, c):
                pe.wait_ge(m_ready, 2 * g + c + 1)
                if c == 0:
                    pe.wait_ge(core_cb, g + 1)
                for h in range(HPG):
                    mm = nc.tensor.matmul(bank[7 if c == 0 else 5][:, h * SHD:(h + 1) * SHD], dec[:, h, :], xdt[:, c, h * SHD:(h + 1) * SHD],
                                          start=True, stop=True)
                mm.then_inc(yd_done, 1)

            def states(g):
                pe.wait_ge(y0_done, g + 1)
                nc.tensor.matmul(bank[7][:], btok[:], xdd[:], start=True, stop=True).then_inc(st_done, 1)

            def from_state(g):
                pe.wait_ge(st_ready, g + 1)
                nc.tensor.matmul(bank[6][:], bcT[:, 1, P:S], hst[:], start=True, stop=True).then_inc(yoff_done, 1)

            def y_transposes(g):
                pe.wait_ge(y_ready, g + 1)
                for b in range(4):
                    for c in range(NT):
                        mm = nc.tensor.transpose(bank[7 if b < 2 else 5][:, (b % 2) * S + c * P:(b % 2) * S + (c + 1) * P],
                                                 y[:, c, b * P:(b + 1) * P], ident[:])
                mm.then_inc(yT_done, 1)

            def group(u, g, e0, e1, e2, i=0, core=True):
                pe.wait_ge(evac[0], e0 + i)
                for j in range(4):
                    products_t(u + j, bank[0:2], ht_hi, ht_lo, 4 * j, j == 0, j == 3, i=i, per=12)
                    if core and j == 0:
                        core_transposes(g - 1)
                    if core and j == 1:
                        running_sums(g - 1, 0)
                if core:
                    diagonal(g - 1, 0)
                    running_sums(g - 1, 1)
                pe.wait_ge(evac[1], e1 + i)
                for j in range(4):
                    pe.wait_ge(lo_done, u + 5 + j + 12 * i)
                    hi = whi[:, j, 0:1024].rearrange("p (k c) -> p k c", k=8)
                    lo = wlo[:, j, 0:1024].rearrange("p (k c) -> p k c", k=8)
                    for k in range(8):
                        kt = 8 * (j % 2) + k
                        for n, (w, m) in enumerate(((hi, ht_hi), (hi, ht_lo), (lo, ht_hi))):
                            mm = nc.tensor.matmul(bank[2][:, (j // 2) * S:(j // 2 + 1) * S], w[:, k, :], m[:, kt, :],
                                                  start=kt == 0 and n == 0, stop=kt == KT - 1 and n == 2)
                    mm.then_inc(unit_used, 1)
                    if core and j == 1:
                        states(g - 1)
                        diagonal(g - 1, 1)
                    if core and j == 2:
                        from_state(g - 1)
                pe.wait_ge(evac[2], e2 + i)
                for j in range(4):
                    products(u + 8 + j, bank[3:5], ht_hi, ht_lo, 4 * j, j == 0, j == 3, i=i, per=12)
                    if core and j == 1:
                        y_transposes(g - 1)
                if core:
                    pe.wait_ge(yT_lo, g)

            pe.wait_ge(pre_da, 1)
            for c in range(NT):
                nc.tensor.matmul(bank[5][:, 64 * c:64 * c + 64], tri[:], da[:, c, :], start=True, stop=True)
            nc.tensor.matmul(bank[6][:, 0:64], ones[:], da[:, 0, :], start=True, stop=True).then_inc(pre_cum, 1)
            group(U_S0, 0, 22, 21, 8, core=False)
            with pe.Fori(0, 4) as i:
                group(U_S0 + 12, 1 + i, 23, 22, 9, i)
            pe.wait_ge(evac[2], 13)
            gated(U_GB, 27, 26, ot_hi, ot_lo, 0, ready=lambda: pe.wait_ge(yT_lo, 4))
            with pe.Fori(0, 3) as i:
                gated(U_GB + 8, 28, 27, ot_hi, ot_lo, 0, i)
            with pe.Fori(0, 3) as i:
                group(U_S5, 5 + i, 31, 30, 13, i)
            pe.wait_ge(evac[0], 34)
            for j in range(4):
                if j == 3:
                    diagonal(7, 0)
                    running_sums(7, 1)
                    states(7)
                    diagonal(7, 1)
                    from_state(7)
                    y_transposes(7)
                    pe.wait_ge(yT_lo, 8)
                products(U_B2 + j, bank[0:2], ot_hi, ot_lo, 4 * j, j == 0, j == 3)
                if j == 0:
                    core_transposes(7)
                if j == 1:
                    running_sums(7, 0)
            for n in range(1, 4):
                pe.wait_ge(evac[n % 2], (33, 35, 34)[n - 1])
                if n == 1:
                    pe.wait_ge(evac[2], 16)
                for j in range(4):
                    products(U_B2 + 4 * n + j, bank[2 * (n % 2):2 * (n % 2) + 2], ot_hi, ot_lo, 4 * j, j == 0, j == 3)
                pe.wait_ge(gate_used, 12 + n)
                transposes(16, merged, 4, range(2 * n - 2, 2 * n))
            pe.wait_ge(evac[0], 36)
            for j in range(4):
                pe.wait_ge(tp_lo, 18 + 2 * j)
                products(U_OUT + j, bank[0:2], ht_hi, ht_lo, 4 * j, j == 0, j == 3)
                if j == 1:
                    pe.wait_ge(gate_used, 16)
                    transposes(16, merged, 4, range(6, 8))
            for n in range(1, 4):
                pe.wait_ge(evac[n % 2], (35, 37, 36)[n - 1])
                for j in range(4):
                    products(U_OUT + 4 * n + j, bank[2 * (n % 2):2 * (n % 2) + 2], ht_hi, ht_lo, 4 * j, j == 0, j == 3)
            pe.wait_ge(evac[0], 38)
            pe.wait_ge(evac[1], 37)
            for q in range(NT):
                pe.wait_ge(diag_ready, q + 1)
                for g in range(8):
                    for k in range(2):
                        mm = nc.tensor.matmul(tp_bank(24 + g)[:, k * S + q * P:k * S + (q + 1) * P], x1[:, q, (2 * g + k) * P:(2 * g + k + 1) * P],
                                              diag[:, q, :], start=True, stop=True)
                    if q == 1:
                        mm.then_inc(tp_done, 1)
            pe.wait_ge(tp_lo, 32)

            def up(u, e0, e1, i):
                for n in range(2):
                    pe.wait_ge(evac[n], (e0, e1)[n] + i)
                    for j in range(4):
                        products_t(u + 4 * n + j, bank[2 * n:2 * n + 2], ht_hi, ht_lo, 4 * j, j == 0, j == 3, i=i, per=8)

            with pe.Fori(0, UP0) as i:
                up(U_UP0, 38, 37, i)
            with pe.Fori(0, 2) as i:
                for n in range(2):
                    pe.wait_ge(f_lo, UP0 - 1)
                    pe.wait_ge(evac[2 + n], (16, 1)[n] + i)
                    for k in range(UP0):
                        if k == UP0 - 1:
                            pe.wait_ge(f_lo, UP0)
                        products(U_DOWN0 + UP0 * n + k, bank[4 + 2 * n:6 + 2 * n], ft_hi, ft_lo, 4 * k, k == 0, k == UP0 - 1, i=i, per=2 * UP0)
            with pe.Fori(0, UP1) as i:
                up(U_UP1, 38 + UP0, 37 + UP0, i)
            for n in range(4):
                pe.wait_ge(f_lo, UP0 + UP1 - 1)
                pe.wait_ge(evac[2 + n % 2], (18 if n % 2 == 0 else 3) + n // 2)
                for k in range(UP1):
                    if k == UP1 - 1:
                        pe.wait_ge(f_lo, UP0 + UP1)
                    products(U_DOWN1 + UP1 * n + k, bank[4 + 2 * (n % 2):6 + 2 * (n % 2)], ft_hi, ft_lo, 4 * k, k == 0, k == UP1 - 1)


_INS = ['x', 'mem', 'pre_mix_g', 'w_in', 'kv_norm_g', 'w_uk', 'w_uv', 'ssd_conv_w', 'ssd_conv_b', 'dt_bias', 'a_log',
        'd_skip', 'ssd_norm_g', 'mem_norm_g', 'w_mem_k', 'w_mem_v', 'w_br_a', 'w_br_b', 'w_br_c', 'w_out',
        'post_mix_g', 'pre_ffn_g', 'w_up', 'ffn_conv_w', 'ffn_conv_b', 'w_down', 'post_ffn_g']


def kernel(**inputs):
    import numpy as _np
    import concourse.bacc as _bacc
    from concourse.bass_utils import run_bass_kernel_spmd as _run

    nc = _bacc.Bacc("TRN2", target_bir_lowering=False, num_devices=1)
    arrays, aps = {}, {}
    for name in _INS:
        a = _np.ascontiguousarray(inputs[name])
        arrays[f"in_{name}"] = a
        aps[name] = nc.dram_tensor(f"in_{name}", a.shape, F32, kind="ExternalInput").ap()
    out = nc.dram_tensor("out_x", (1, S, D), F32, kind="ExternalOutput").ap()
    hybrid_layer(nc, aps, out)
    r = _run(nc, [arrays], core_ids=[0])
    return r.results[0]["out_x"]
```

```python
from contextlib import ExitStack

import concourse.bass as bass
from concourse import mybir

F32 = mybir.dt.float32
F32R = mybir.dt.float32r
I32 = mybir.dt.int32
ALU = mybir.AluOpType
ACT = mybir.ActivationFunctionType
AX_X = mybir.AxisListType.X

P = 128
S = 256
D = 2048
NT = S // P
KT = D // P
CH = 512
EPS = 1e-6
GELU_CUBE, GELU_SCALE = 0.044715, (2 / 3.141592653589793) ** 0.5

HEADS, HD, RANK = 16, 128, 512
TOPK = S // 4
SCALE = HD ** -0.5
IDX_SCALE, IDX_W_SCALE = HD ** -0.5, 16 ** -0.5
MEM_HEADS, MEM_HD = 4, 512
MEM_SCALE = MEM_HD ** -0.5
GROUPS, STATE, SSD_HEADS, SHD = 8, 128, 64, 64
INNER = 4096
HPG = SSD_HEADS // GROUPS
FFN = 5632
FB = FFN // P
XBLK = INNER // P
UP0, UP1 = 6, 5
CONV_BLK = 48

Q_A = 0
C_KV = Q_A + 2048
Q_I = C_KV + 512
K_I = Q_I + 2048
W_I = K_I + 128
Z = W_I + 16
XBC = Z + 4096
DT_C = XBC + 6144
Q_M = DT_C + 64
GATE = Q_M + 2048

NEG = -3.0e38
MARK = -3.4e38
TAKEN = -3.2e38
MASKED = -1.0e30


def hybrid_layer(nc, t, out):
    ctx = ExitStack()
    with ctx:
        def sem(name):
            return ctx.enter_context(nc.semaphore(name))

        BASE = 16512
        RAW_AT = BASE
        WHI_AT = RAW_AT + 2 * 8192
        WLO_AT = WHI_AT + 4 * 8192
        HT_AT = WLO_AT + 4 * 8192
        OT_AT = HT_AT + 32768
        MERGED_AT = OT_AT + 32768
        PAR_AT = MERGED_AT + 16384
        WORK_AT = PAR_AT + 8192
        END = 229368

        def at(name, shape, dtype, offset):
            return nc.alloc_sbuf_tensor_at(name, [P] + shape, dtype, offset=offset)

        raw = at("raw", [2, 2048], F32, RAW_AT)
        whi = at("whi", [4, 2048], F32R, WHI_AT)
        wlo = at("wlo", [4, 2048], F32R, WLO_AT)
        ht_hi = at("ht_hi", [KT, S], F32R, HT_AT)
        ht_lo = at("ht_lo", [KT, S], F32R, HT_AT + 16384)
        ot_hi = at("ot_hi", [KT, S], F32R, OT_AT)
        ot_lo = at("ot_lo", [KT, S], F32R, OT_AT + 16384)
        merged = at("merged", [NT, D], F32, MERGED_AT)

        par = at("par", [672], F32, PAR_AT)
        ident = at("ident", [P], F32, PAR_AT + 2688)
        ones = at("ones", [P], F32, PAR_AT + 3200)
        tri = at("tri", [P], F32, PAR_AT + 3712)
        causneg = at("causneg", [P], F32, PAR_AT + 4224)
        rows = at("rows", [3, 64], F32, PAR_AT + 4736)
        dt = at("dt", [NT, 64], F32, PAR_AT + 5504)
        da = at("da", [NT, 64], F32, PAR_AT + 6016)
        acum = at("acum", [NT, 64], F32, PAR_AT + 6528)
        eacum = at("eacum", [64], F32, PAR_AT + 7040)
        edec = at("edec", [64], F32, PAR_AT + 7296)
        stat = at("stat", [32], F32, PAR_AT + 7552)
        widx = at("widx", [NT, 16], F32, PAR_AT + 7680)
        scr = at("scr", [32], F32, PAR_AT + 7808)
        PRE_MIX, MEM_G, PRE_FFN, SSD_G, CONV_B, CONV_W, FFN_W, FFN_B = 0, 16, 32, 48, 80, 128, 320, 584

        xin = at("xin", [NT, D], F32, OT_AT)
        memin = at("memin", [NT, D], F32, OT_AT + 16384)
        stage = at("stage", [7, P], F32, WORK_AT + 16384)
        mdiag = at("mdiag", [NT, P], F32, WORK_AT + 20480)
        junk_a = at("junk_a", [D], F32, WORK_AT + 24576)
        memn_hi = at("memn_hi", [KT, S], F32R, MERGED_AT)
        memn_lo = at("memn_lo", [KT, S], F32R, WORK_AT)

        kmem = at("kmem", [4, S], F32, WORK_AT + 16384)
        vmem = at("vmem", [NT, CH], F32, WORK_AT + 20480)
        qmem = at("qmem", [4, S], F32, WORK_AT + 24576)
        pmem = at("pmem", [NT, S], F32, WORK_AT + 28672)
        pmemT = at("pmemT", [NT, S], F32, WORK_AT + 30720)
        tgate = at("tgate", [NT, CH], F32, WORK_AT + 32768)

        kvg = at("kvg", [RANK], F32, WORK_AT)
        mask = at("mask", [384], F32, WORK_AT)
        ckv_hi = at("ckv_hi", [NT, RANK], F32R, WORK_AT + 2048)
        ckv_lo = at("ckv_lo", [NT, RANK], F32R, WORK_AT + 6144)
        ckvT_hi = at("ckvT_hi", [4, S], F32R, WORK_AT + 10240)
        ckvT_lo = at("ckvT_lo", [4, S], F32R, WORK_AT + 14336)
        ql_hi = at("ql_hi", [4, S], F32R, WORK_AT + 18432)
        ql_lo = at("ql_lo", [4, S], F32R, WORK_AT + 22528)
        ol_hi = at("ol_hi", [4, S], F32R, WORK_AT + 26624)
        ol_lo = at("ol_lo", [4, S], F32R, WORK_AT + 30720)
        pT_hi = at("pT_hi", [384], F32R, WORK_AT + 34816)
        pT_lo = at("pT_lo", [384], F32R, WORK_AT + 36352)
        prob = at("prob", [384], F32, WORK_AT + 37888)
        qi_hi = [ql_hi, ol_hi]
        qi_lo = [ql_lo, ol_lo]
        ckv = at("ckv", [NT, RANK], F32, WORK_AT + 26624)
        junk_q = at("junk_q", [RANK], F32, OT_AT + 12 * 1024)
        relu = at("relu", [2, 384], F32, OT_AT + 12 * 1024)
        ki_hi = at("ki_hi", [S], F32R, OT_AT + 16384 + 12 * 1024)
        ki_lo = at("ki_lo", [S], F32R, OT_AT + 16384 + 13 * 1024)
        smallT = at("smallT", [2, S], F32, OT_AT)
        score = at("score", [384], F32, OT_AT + 16384 + 14 * 1024)

        xv = at("xv", [4, S], F32, WORK_AT)
        xT = at("xT", [4, S], F32, WORK_AT + 4096)
        bcv = at("bcv", [2, S], F32, WORK_AT + 8192)
        bcT = at("bcT", [2, S], F32, WORK_AT + 10240)
        xdt = at("xdt", [NT, CH], F32, WORK_AT + 12288)
        y = at("y", [NT, CH], F32, WORK_AT + 16384)
        xdd = at("xdd", [CH], F32, WORK_AT + 20480)
        atri = at("atri", [HPG, P], F32, WORK_AT + 22528)
        dec = at("dec", [HPG, P], F32, WORK_AT + 26624)
        cb = at("cb", [NT, P], F32, WORK_AT + 30720)
        btok = at("btok", [P], F32, WORK_AT + 31744)
        hst = at("hst", [CH], F32, WORK_AT + 32256)
        zs = at("zs", [NT, CH], F32, WORK_AT + 34304)
        assert WORK_AT + 34304 + 4096 <= END

        tmp = at("tmp", [8, P], F32, WORK_AT + 12288)
        tgate_b = at("tgate_b", [NT, CH], F32, WORK_AT)
        gprod = at("gprod", [NT, CH], F32, WORK_AT + 12288)

        mix = at("mix", [NT, D], F32, WORK_AT)
        grow = at("grow", [D], F32, WORK_AT + 16384)
        diag = at("diag", [NT, P], F32, WORK_AT + 24576)
        junk_o = at("junk_o", [D], F32, OT_AT)
        x1 = at("x1", [NT, D], F32, MERGED_AT)

        ft_hi = at("ft_hi", [24, S], F32R, OT_AT)
        ft_lo = at("ft_lo", [24, S], F32R, OT_AT + 24576)
        acc = at("acc", [NT, D], F32, WORK_AT)
        va = at("va", [4, S], F32, WORK_AT + 16384)
        ta = at("ta", [4, S], F32, WORK_AT + 20480)
        vv = at("vv", [4, S], F32, WORK_AT + 24576)
        tb = at("tb", [4, S], F32, WORK_AT + 28672)
        x1b = at("x1b", [NT, D], F32, HT_AT)
        frow = at("frow", [D], F32, HT_AT + 16384)
        junk_f = at("junk_f", [CH], F32, HT_AT + 24576)

        x1_dram = nc.dram_tensor("x1_scratch", (S, D), F32, kind="Internal").ap()

        gate_dram = nc.dram_tensor("gate_scratch", (4, P, NT * CH), F32, kind="Internal").ap()

        bank = [ctx.enter_context(nc.psum_tensor(f"bank{i}", [P, CH], F32)) for i in range(8)]

        def sems(names):
            return (sem(n) for n in names.split())

        raw_in = [sem(f"raw_in{n}") for n in range(4)]
        hi_done, lo_done = sems("hi_done lo_done")
        unit_used = sem("unit_used")
        evac = [sem("evac0"), sem("evac1"), sem("evac2"), sem("evac3")]
        mem_in = [sem("mem_in0"), sem("mem_in1")]
        x_in, par_in, late_par_in, row_in, kvg_in = sems("x_in par_in late_par_in row_in kvg_in")
        gate_saved, gate_back = sems("gate_saved gate_back")
        grow_in, x_again, x1_out, x1_in, out_done = sems("grow_in x_again x1_out x1_in out_done")
        consts = sem("consts")
        par_tp, par_done, late_par_tp, late_par_done = sems("par_tp par_done late_par_tp late_par_done")
        sq_done, norm_done = sems("sq_done norm_done")
        tp_done, tp_hi, tp_lo = sems("tp_done tp_hi tp_lo")
        ms_done, mnb, mexp, mprob, mt_done, mpT, mo_done, mo_hi, mo_lo = sems("ms_done mnb mexp mprob mt_done mpT mo_done mo_hi mo_lo")
        gate_used = sem("gate_used")
        small_hi, small_T, small_tok, dt_read = sems("small_hi small_T small_tok dt_read")
        ck_sq, ck_hi, ck_lo, ckT_done, ckT_hi, ckT_lo = sems("ck_sq ck_hi ck_lo ckT_done ckT_hi ckT_lo")
        q_hi = sem("q_hi")
        idx_done, relu_done, relu_used = sems("idx_done relu_done relu_used")
        at_ql, at_ql_hi, at_ql_lo, at_s, at_nb, at_exp, at_p, at_t = sems("at_ql at_ql_hi at_ql_lo at_s at_nb at_exp at_p at_t")
        at_t_hi, at_t_lo, at_ol, at_ol_hi, at_ol_lo, at_o, at_o_hi, at_o_lo = sems("at_t_hi at_t_lo at_ol at_ol_hi at_ol_lo at_o at_o_hi at_o_lo")
        pre_n, pre_u, pre_w, pre_ln, pre_da, pre_cum, pre_dec, pre_done = sems("pre_n pre_u pre_w pre_ln pre_da pre_cum pre_dec pre_done")
        x_tap, x_conv, x_tanh, x_ready, bc_tap, bc_conv, bc_tanh, bc_ready = sems("x_tap x_conv x_tanh x_ready bc_tap bc_conv bc_tanh bc_ready")
        z_tanh = sem("z_tanh")
        core_in, core_btok, core_x, core_cb = sems("core_in core_btok core_x core_cb")
        atri_done, cum_done, seg_done, dec_done, m_ready, yd_done = sems("atri_done cum_done seg_done dec_done m_ready yd_done")
        y0_done, st_done, st_ready, yoff_done, y_ready, yT_done, yT_hi, yT_lo = sems("y0_done st_done st_ready yoff_done y_ready yT_done yT_hi yT_lo")
        mix_sq, x1_ready, x1_sq, diag_ready = sems("mix_sq x1_ready x1_sq diag_ready")
        a_tap, a_conv, a_sq, a_arg, a_tanh, v_tap, f_ready, f_hi, f_lo = sems("a_tap a_conv a_sq a_arg a_tanh v_tap f_ready f_hi f_lo")
        down_sq, y_out = sems("down_sq y_out")

        U_MEM = 0
        U_GC = U_MEM + 12 * MEM_HEADS
        U_SMALL = U_GC + 32
        U_CKV = U_SMALL + 4
        U_QI = U_CKV + 4
        U_QA = U_QI + 16
        U_ATT = U_QA + 16
        U_GA = U_ATT + 16
        U_S0 = U_GA + 32
        U_GB = U_S0 + 5 * 12
        U_S5 = U_GB + 32
        U_B2 = U_S5 + 3 * 12
        U_OUT = U_B2 + 16
        U_UP0 = U_OUT + 16
        U_DOWN0 = U_UP0 + 8 * UP0
        U_UP1 = U_DOWN0 + 4 * UP0
        U_DOWN1 = U_UP1 + 8 * UP1
        U_END = U_DOWN1 + 4 * UP1

        w_in = t["w_in"][0]

        def cols(w, j, c0, n):
            return w[j * 512:(j + 1) * 512, c0:c0 + n].rearrange("(k p) c -> p k c", p=P)

        def dcols(w, j, c0, n):
            return w[j * 512:(j + 1) * 512, bass.ds(c0, n)].rearrange("(k p) c -> p k c", p=P)

        def gates_from(n, i):
            return E0_GATE[n] + i

        def tp_bank(n):
            return bank[2 + n % 6] if n < 8 else bank[4 + n % 4] if n < 24 else bank[n - 24]

        E0_GATE = {0: 9, 1: 10, 4: 19, 5: 20, 8: 28, 9: 29}

        X_GROUPS = [range(0, 2), range(2, 5), range(5, 8)]

        def key_unit(pair):
            return max(2 * pair - 1, 0)

        B2_ORDER = [(0, 0), (0, 1), (0, 2), (1, 0), (1, 1), (1, 2), (0, 3), (1, 3)] + [(c, j) for c in (2, 3) for j in range(4)]

        def value_unit(pair):
            return 2 * pair + 2 if pair < HEADS // 2 - 1 else 2 * pair + 1

        block = ctx.enter_context(nc.Block())

        @block.sync
        def _(sp):
            for name, r0, k in (("pre_mix_g", 0, 16), ("mem_norm_g", 16, 16), ("pre_ffn_g", 32, 16), ("ssd_norm_g", 48, 32), ("ssd_conv_b", 80, 48)):
                sp.dma_start(stage[r0:r0 + k, 0, :], t[name][0].rearrange("(b c) -> b c", c=P)).then_inc(par_in, 16)
            for q in range(NT):
                sp.dma_start(memin[:, q, :], t["mem"][0][q * P:(q + 1) * P]).then_inc(mem_in[q], 16)

            def load(u, src, i=0, per=0):
                n = src.shape[1] // 2
                for h in range(2):
                    if not isinstance(i, int) or u >= 2:
                        sp.wait_ge(lo_done, 2 * u - 3 + h + 2 * per * i)
                    sp.dma_start(raw[:, u % 2, 1024 * h:1024 * h + n * src.shape[2]].rearrange("p (k c) -> p k c", k=n),
                                 src[:, h * n:(h + 1) * n]).then_inc(raw_in[2 * (u % 2) + h], 16)

            wk, wv = t["w_mem_k"][0], t["w_mem_v"][0]

            def mem_head(u, c0, i=0):
                for n, (w, off) in enumerate(((wk, 0), (wv, 0), (w_in, Q_M))):
                    for j in range(4):
                        load(u + 4 * n + j, dcols(w, j, c0 + off, CH), i, 12)
                        if isinstance(i, int) and n == 0 and j == 1:
                            sp.dma_start(xin[:], t["x"][0].rearrange("(a p) d -> p a d", p=P)).then_inc(x_in, 16)

            mem_head(0, 0)
            with sp.Fori(0, MEM_HEADS - 1) as i:
                mem_head(12, 512 + 512 * i, i)

            def gated(u, branch, w, j0, c0, i=0):
                for j in range(4):
                    load(u + j, dcols(w_in, j, GATE + branch * D + c0, CH), i, 8)
                for j in range(4):
                    load(u + 4 + j, dcols(w, j0 + j, c0, CH), i, 8)

            gated(U_GC, 2, t["w_br_c"][0], 0, 0)
            with sp.Fori(0, 3) as i:
                gated(U_GC + 8, 2, t["w_br_c"][0], 0, 512 + 512 * i, i)

            sp.wait_ge(unit_used, U_GC)
            sp.dma_start(kvg[:], t["kv_norm_g"].to_broadcast([P, RANK])).then_inc(kvg_in, 16)
            for j in range(4):
                c0, n = (K_I, 144) if j < 2 else (DT_C, 64)
                r = 1024 * (j % 2)
                load(U_SMALL + j, w_in[r:r + 1024, c0:c0 + n].rearrange("(k p) c -> p k c", p=P))
            for j in range(4):
                load(U_CKV + j, cols(w_in, j, C_KV, CH))
            for u, c0 in ((U_QI, Q_I), (U_QA, Q_A)):
                for j in range(4):
                    load(u + j, cols(w_in, j, c0, CH))
                with sp.Fori(0, 3) as i:
                    for j in range(4):
                        load(u + 4 + j, dcols(w_in, j, c0 + 512 + 512 * i, CH), i, 4)
            uk = t["w_uk"][0].rearrange("(g h) d r -> g d h r", h=2)
            uv = t["w_uv"][0].rearrange("h r d -> (h r) d").rearrange("(g x p) d -> g p x d", p=P, x=8)
            for n in range(16):
                if n == 0 or n % 2 and n < 15:
                    load(U_ATT + n, uk[(n + 1) // 2])
                else:
                    load(U_ATT + n, uv[7 if n == 15 else n // 2 - 1])
            gated(U_GA, 0, t["w_br_a"][0], 0, 0)
            with sp.Fori(0, 3) as i:
                gated(U_GA + 8, 0, t["w_br_a"][0], 0, 512 + 512 * i, i)

            def group(u, g, i=0):
                for j in range(4):
                    load(u + j, dcols(w_in, j, XBC + CH * g, CH), i, 12)
                for j in range(4):
                    c0 = XBC + INNER + 1024 * (j // 2) + P * g
                    r = 1024 * (j % 2)
                    load(u + 4 + j, w_in[r:r + 1024, bass.ds(c0, P)].rearrange("(k p) c -> p k c", p=P), i, 12)
                for j in range(4):
                    load(u + 8 + j, dcols(w_in, j, Z + CH * g, CH), i, 12)

            group(U_S0, 0)
            with sp.Fori(0, 4) as i:
                group(U_S0 + 12, 1 + i, i)
            gated(U_GB, 1, t["w_br_b"][0], 0, 0)
            with sp.Fori(0, 3) as i:
                gated(U_GB + 8, 1, t["w_br_b"][0], 0, 512 + 512 * i, i)
            with sp.Fori(0, 3) as i:
                group(U_S5, 5 + i, i)
            for n, (c, j) in enumerate(B2_ORDER):
                load(U_B2 + n, cols(t["w_br_b"][0], 4 + j, 512 * c, CH))
            with sp.Fori(0, 4) as i:
                for j in range(4):
                    load(U_OUT + j, dcols(t["w_out"][0], j, 512 * i, CH), i, 4)

            def up(u, c0, chunks):
                with sp.Fori(0, chunks) as i:
                    for n in range(2):
                        for j in range(4):
                            load(u + 4 * n + j, dcols(t["w_up"][0], j, c0 + n * FFN + 512 * i, CH), i, 8)

            up(U_UP0, 0, UP0)
            with sp.Fori(0, 2) as i:
                for n in range(2):
                    for k in range(UP0):
                        load(U_DOWN0 + UP0 * n + k, dcols(t["w_down"][0], k, 1024 * i + 512 * n, CH), i, 2 * UP0)
            up(U_UP1, 512 * UP0, UP1)
            for n in range(4):
                for k in range(UP1):
                    load(U_DOWN1 + UP1 * n + k, cols(t["w_down"][0], UP0 + k, 512 * n, CH))
            y = out[0].rearrange("(q p) d -> q p d", p=P)
            for n in range(4):
                sp.wait_ge(y_out, n + 1)
                c = slice(n % 2 * 1024, n % 2 * 1024 + 1024)
                sp.dma_start(y[n // 2][:, c], acc[:, n // 2, c]).then_inc(out_done, 16)
            sp.wait_ge(out_done, 64)

        @block.gpsimd
        def _(pool):
            nc.gpsimd.memset(ones[:], 1.0)
            nc.gpsimd.memset(ident[:], 0.0)
            nc.gpsimd.memset(causneg[:], 0.0)
            pool.drain()
            nc.gpsimd.affine_select(out=ident[:], in_=ident[:], compare_op=ALU.not_equal, fill=1.0, base=0,
                                    pattern=[[-1, P]], channel_multiplier=1)
            nc.gpsimd.affine_select(out=tri[:], in_=ones[:], compare_op=ALU.is_ge, fill=0.0, base=0,
                                    pattern=[[1, P]], channel_multiplier=-1)
            nc.gpsimd.affine_select(out=causneg[:], in_=causneg[:], compare_op=ALU.is_ge, fill=NEG, base=0,
                                    pattern=[[-1, P]], channel_multiplier=1).then_inc(consts, 1)

            pool.wait_ge(pre_da, 1)

            def running(g, c):
                nc.gpsimd.tensor_tensor(atri[:], tri[:].unsqueeze(1).to_broadcast([P, HPG, P]),
                                        da[:, c, bass.ds(HPG * g, HPG)].unsqueeze(2).to_broadcast([P, HPG, P]), ALU.mult).then_inc(atri_done, 1)
                pool.wait_ge(cum_done, 2 * g + c + 1)

            with pool.Fori(0, GROUPS) as g:
                for c in range(NT):
                    running(g, c)
            pool.wait_ge(gate_saved, 64)
            pool.wait_ge(x_ready, GROUPS)
            for n in range(4):
                if n:
                    pool.wait_ge(gate_used, 12 + n)
                nc.gpsimd.dma_start(tgate_b[:].rearrange("p a c -> p (a c)"), gate_dram[n]).then_inc(gate_back, 16)
            nc.gpsimd.dma_start(grow[:], t["post_mix_g"].to_broadcast([P, D])).then_inc(grow_in, 16)
            pool.wait_ge(tp_done, 24)
            nc.gpsimd.dma_start(x1[:], t["x"][0].rearrange("(a p) d -> p a d", p=P)).then_inc(x_again, 16)
            pool.wait_ge(x1_ready, 2)
            nc.gpsimd.dma_start(x1_dram.rearrange("(a p) d -> p a d", p=P), x1[:]).then_inc(x1_out, 16)
            pool.wait_ge(x1_out, 16)
            pool.wait_ge(unit_used, U_DOWN1)
            nc.gpsimd.dma_start(x1b[:], x1_dram.rearrange("(a p) d -> p a d", p=P)).then_inc(x1_in, 16)
            nc.gpsimd.dma_start(frow[:], t["post_ffn_g"].to_broadcast([P, D])).then_inc(x1_in, 16)

        @block.scalar
        def _(act):
            def load_parameters():
                cw = t["ssd_conv_w"][0].rearrange("k (b c) -> (k b) c", c=P)
                fw = t["ffn_conv_w"][0].rearrange("k (b c) -> (k b) c", c=P)
                for n in range(2):
                    act.dma_start(stage[0:96, 1 + n, :], cw[96 * n:96 * n + 96]).then_inc(late_par_in, 16)
                for n in range(3):
                    act.dma_start(stage[0:88, 3 + n, :], fw[88 * n:88 * n + 88]).then_inc(late_par_in, 16)
                act.dma_start(stage[0:88, 6, :], t["ffn_conv_b"][0].rearrange("(b c) -> b c", c=P)).then_inc(late_par_in, 16)
                for n, name in enumerate(("dt_bias", "a_log", "d_skip")):
                    act.dma_start(rows[:, n, :], t[name].to_broadcast([P, 64])).then_inc(row_in, 16)

            def split(u, width=2048, i=0, per=0):
                w = width // 2
                for h in range(2):
                    act.wait_ge(raw_in[2 * (u % 2) + h], 16 * (u // 2 + 1) + 8 * per * i)
                    if h == 0 and (not isinstance(i, int) or u >= 4):
                        act.wait_ge(unit_used, u - 3 + per * i)
                    nc.scalar.copy(whi[:, u % 4, h * w:(h + 1) * w], raw[:, u % 2, 1024 * h:1024 * h + w]).then_inc(hi_done, 1)

            def transposed_hi(n0, dst, gain, scale=1.0, groups=range(8)):
                for g in groups:
                    b = tp_bank(n0 + g)
                    act.wait_ge(tp_done, n0 + g + 1)
                    for k in range(2):
                        last = nc.scalar.activation(dst[:, 2 * g + k, :], b[:, k * S:(k + 1) * S], ACT.Copy,
                                                    scale=par[:, gain + 2 * g + k:gain + 2 * g + k + 1] if gain is not None else scale)
                    last.then_inc(tp_hi, 1)

            def squares(n, src, ready):
                for q in range(NT):
                    act.wait_ge(ready[q], 16)
                    last = nc.scalar.activation(junk_a[:], src[:, q, :], ACT.Square, accum_out=stat[:, 8 + 2 * n + q:9 + 2 * n + q])
                    act.drain()
                last.then_inc(sq_done, 1)

            def mem_exp(h):
                act.wait_ge(mnb, h + 1)
                for q in range(NT):
                    last = nc.scalar.activation(pmem[:, q, :], bank[6][:, q * S:(q + 1) * S], ACT.Exp, scale=MEM_SCALE,
                                                bias=stat[:, 2 + q:3 + q], accum_out=stat[:, 4 + q:5 + q])
                last.then_inc(mexp, 1)

            def mem_out_hi(h):
                act.wait_ge(mo_done, h + 1)
                for n in range(2):
                    last = nc.scalar.copy(ot_hi[:, bass.ds(4 * h + 2 * n, 2), :], bank[6 + n][:].rearrange("p (b s) -> p b s", b=2))
                last.then_inc(mo_hi, 1)

            def mem_head(u, h, i=0, first=False):
                for j in range(4):
                    split(u + 4 + j, i=i, per=12)
                    if first and j == 1:
                        squares(1, xin, (x_in, x_in))
                    if first and j == 2:
                        act.wait_ge(late_par_tp, 1)
                        nc.scalar.mul(par[:, 128:320], bank[2][:, 0:192], 0.5)
                        nc.scalar.copy(par[:, 320:672], bank[3][:, 0:352]).then_inc(late_par_done, 1)
                    elif not first and j == 0:
                        mem_exp(h - 1)
                act.wait_ge(unit_used, u + 4 + 12 * i)
                nc.scalar.copy(kmem[:, 0:2, :], bank[0][:].rearrange("p (b s) -> p b s", b=2)).then_inc(evac[0], 1)
                for j in range(4):
                    split(u + 8 + j, i=i, per=12)
                    if first and j < 3:
                        transposed_hi(8, ht_hi, PRE_MIX, groups=X_GROUPS[j])
                    if j == 1 and not first:
                        mem_out_hi(h - 1)
                act.wait_ge(unit_used, u + 8 + 12 * i)
                nc.scalar.copy(vmem[:, 0, :], bank[2][:]).then_inc(evac[1], 1)
                for j in range(4):
                    split(u + 12 + j, i=i, per=12)
                act.wait_ge(unit_used, u + 12 + 12 * i)
                nc.scalar.copy(qmem[:, 0:2, :], bank[4][:].rearrange("p (b s) -> p b s", b=2)).then_inc(evac[2], 1)

            squares(0, memin, mem_in)
            act.wait_ge(par_tp, 1)
            nc.scalar.copy(par[:, 0:80], bank[0][:, 0:80])
            nc.scalar.mul(par[:, 80:128], bank[0][:, 80:128], 0.5).then_inc(par_done, 1)
            act.drain()
            for j in range(4):
                transposed_hi(0, memn_hi, MEM_G, groups=range(2 * j, 2 * j + 2))
                split(j)
            load_parameters()
            mem_head(0, 0, first=True)
            with act.Fori(0, MEM_HEADS - 1) as i:
                mem_head(12, 1 + i, i)

            def gate_tanh(u, n, i=0):
                act.wait_ge(unit_used, u + 4 + 8 * i)
                if n > 0:
                    act.wait_ge(gate_used, n + i)
                for q in range(NT):
                    last = nc.scalar.activation(tgate[:, q, :], bank[q][:], ACT.Tanh, scale=0.5)
                last.then_inc(evac[0], 1)

            def gated(u, n, i=0, side=(None, None, None, None)):
                for j in range(4):
                    split(u + 4 + j, i=i, per=8)
                    if side[j]:
                        side[j]()
                gate_tanh(u, n, i)
                for j in range(4):
                    split(u + 8 + j, i=i, per=8)

            gated(U_GC, 0, side=(lambda: mem_exp(3), None, None, lambda: mem_out_hi(3)))
            with act.Fori(0, 3) as i:
                gated(U_GC + 8, 1, i)

            for j in range(4):
                split(U_CKV + j)
            act.wait_ge(unit_used, U_SMALL + 4)
            nc.scalar.copy(ki_hi[:], bank[0][:, 0:S]).then_inc(small_hi, 1)
            nc.scalar.copy(smallT[0:16, 0, :], bank[4][0:16, 0:S])
            nc.scalar.copy(smallT[0:64, 1, :], bank[5][0:64, 0:S]).then_inc(small_T, 1)
            for j in range(4):
                split(U_QI + j)
            act.wait_ge(small_tok, 1)
            nc.scalar.copy(dt[:], bank[4][:, 0:160].rearrange("p (q c) -> p q c", q=NT)[:, :, 16:80]).then_inc(dt_read, 1)
            act.wait_ge(unit_used, U_CKV + 4)
            for q in range(NT):
                last = nc.scalar.activation(junk_q[:], bank[2 + q][:], ACT.Square, accum_out=stat[:, 16 + q:17 + q])
                act.drain()
            last.then_inc(ck_sq, 1)
            act.wait_ge(evac[1], 13)
            nc.scalar.copy(ckv_hi[:], ckv[:]).then_inc(ck_hi, 1)

            def queries_hi(n):
                u = U_QI + 4 * n
                for j in range(3 if n == 7 else 4):
                    split(u + 4 + j, 1024 if n == 7 else 2048)
                    if n == 0 and j == 2:
                        act.wait_ge(ckT_done, 1)
                        for b in range(2):
                            last = nc.scalar.copy(ckvT_hi[:, 2 * b:2 * b + 2, :], bank[6 + b][:].rearrange("p (b s) -> p b s", b=2))
                        last.then_inc(ckT_hi, 1)
                    if 1 <= n <= 4:
                        h = 4 * (n - 1) + j
                        act.wait_ge(idx_done, h + 1)
                        if h >= 2:
                            act.wait_ge(relu_used, h - 1)
                        nc.scalar.activation(relu[:, h % 2, :], bank[6 + h % 2][:, 0:384], ACT.Relu, scale=IDX_SCALE).then_inc(relu_done, 1)
                if n == 7:
                    key_hi(0)
                act.wait_ge(unit_used, u + 4)
                for b in range(2):
                    dst = qi_hi[n % 2][:, 2 * b:2 * b + 2, :] if n < 4 else ot_hi[:, 4 * (n - 4) + 2 * b:4 * (n - 4) + 2 * b + 2, :]
                    last = nc.scalar.copy(dst, bank[2 * (n % 2) + b][:].rearrange("p (b s) -> p b s", b=2))
                last.then_inc(q_hi, 1)
                if n == 7:
                    split(u + 7, 1024)

            def two_banks(dst, n):
                for b in range(2):
                    last = nc.scalar.copy(dst[:, 2 * b:2 * b + 2, :], bank[n + b][:].rearrange("p (b s) -> p b s", b=2))
                return last

            def key_hi(h):
                act.wait_ge(at_ql, h + 1)
                two_banks(ql_hi, 0).then_inc(at_ql_hi, 1)

            def out_latent_hi(h):
                act.wait_ge(at_ol, h + 1)
                two_banks(ol_hi, 4).then_inc(at_ol_hi, 1)

            def out_hi(h):
                act.wait_ge(at_o, h + 1)
                nc.scalar.copy(ot_hi[:, bass.ds(h, 1), :].rearrange("p a s -> p (a s)"), bank[6][:, 0:S]).then_inc(at_o_hi, 1)

            def attention(h, outs=2, last_head=False):
                if not last_head:
                    key_hi(h + 1)
                act.wait_ge(at_nb, h + 1)
                nc.scalar.activation(prob[:, 0:P], prob[:, 0:P], ACT.Exp, bias=stat[:, 18:19], accum_out=stat[:, 20:21])
                nc.scalar.activation(prob[:, P:384], prob[:, P:384], ACT.Exp, bias=stat[:, 19:20], accum_out=stat[:, 21:22]).then_inc(at_exp, 1)
                if outs == 2:
                    out_hi(h - 2)
                if outs >= 1:
                    out_latent_hi(h - 1)
                act.wait_ge(at_t, h + 1)
                nc.scalar.copy(pT_hi[:], bank[3][:, 0:384]).then_inc(at_t_hi, 1)

            for n in range(8):
                queries_hi(n)
            attention(0, 0)
            attention(1, 1)
            with act.Fori(0, 3) as i:
                for k in range(4):
                    attention(2 + k + 4 * i)
                    if k % 2 == 0:
                        split(U_ATT + 4 + k, 1024, i, 4)
                        split(U_ATT + 5 + k, 1024, i, 4)
            attention(14)
            split(U_GA)
            attention(15, last_head=True)
            split(U_GA + 1)
            out_hi(14)
            out_latent_hi(15)
            split(U_GA + 2)
            act.wait_ge(at_o, 16)
            split(U_GA + 3)
            out_hi(15)

            gated(U_GA, 4)
            with act.Fori(0, 3) as i:
                gated(U_GA + 8, 5, i)

            def conv_tap(first_block, dst, banks, blocks, done, u, i):
                act.wait_ge(unit_used, u + 12 * i)
                for b in range(blocks):
                    k = first_block[b]
                    last = nc.scalar.activation(dst[:, b, :], banks[b // 2][:, (b % 2) * S:(b % 2 + 1) * S], ACT.Identity,
                                                scale=par[:, bass.ds(CONV_W + 3 * CONV_BLK + k, 1)], bias=par[:, bass.ds(CONV_B + k, 1)])
                last.then_inc(done, 1)

            def decay_exp(g, c):
                act.wait_ge(seg_done, 2 * g + c + 1)
                nc.scalar.activation(dec[:], dec[:], ACT.Exp).then_inc(dec_done, 1)

            def b_token(g):
                act.wait_ge(core_in, g + 1)
                nc.scalar.copy(btok[:], bank[7][:, 0:P]).then_inc(core_btok, 1)

            def state(g):
                act.wait_ge(st_done, g + 1)
                nc.scalar.copy(hst[:], bank[7][:]).then_inc(st_ready, 1)

            def y_hi(g, kt):
                act.wait_ge(yT_done, g + 1)
                for b in range(4):
                    src = bank[7 if b < 2 else 5][:, (b % 2) * S:(b % 2 + 1) * S]
                    last = nc.scalar.activation(ot_hi[:, bass.ds(kt + b, 1), :].rearrange("p a s -> p (a s)"), src, ACT.Copy,
                                                scale=par[:, bass.ds(SSD_G + 4 * g + b, 1)])
                last.then_inc(yT_hi, 1)

            def group(u, g, kt, i=0, core=True):
                split(u + 4, 1024, i, 12)
                split(u + 5, 1024, i, 12)
                if core:
                    b_token(g - 1)
                split(u + 6, 1024, i, 12)
                split(u + 7, 1024, i, 12)
                if core:
                    decay_exp(g - 1, 0)
                split(u + 8, 2048, i, 12)
                conv_tap([4 * g + b for b in range(4)], xv, bank[0:2], 4, x_tap, u + 4, i)
                split(u + 9, 2048, i, 12)
                if core:
                    decay_exp(g - 1, 1)
                split(u + 10, 2048, i, 12)
                split(u + 11, 2048, i, 12)
                if core:
                    state(g - 1)
                act.wait_ge(x_conv, g + 1)
                nc.scalar.activation(xT[:], xv[:], ACT.Tanh).then_inc(x_tanh, 1)
                split(u + 12, 2048, i, 12)
                conv_tap([XBLK + g, XBLK + GROUPS + g], bcv, bank[2:3], 2, bc_tap, u + 8, i)
                split(u + 13, 2048, i, 12)
                split(u + 14, 2048, i, 12)
                act.wait_ge(bc_conv, g + 1)
                nc.scalar.activation(bcT[:], bcv[:], ACT.Tanh).then_inc(bc_tanh, 1)
                split(u + 15, 2048, i, 12)
                act.wait_ge(unit_used, u + 12 + 12 * i)
                if core:
                    y_hi(g - 1, kt)
                    act.wait_ge(y_ready, g)
                for q in range(NT):
                    last = nc.scalar.activation(zs[:, q, :], bank[3 + q][:], ACT.Tanh, scale=0.5)
                last.then_inc(z_tanh, 1)

            act.wait_ge(row_in, 48)
            nc.scalar.activation(rows[:, 1, :], rows[:, 1, :], ACT.Exp)
            act.wait_ge(pre_n, 1)
            nc.scalar.activation(tmp[:, 3, :], tmp[:, 2, :], ACT.Exp).then_inc(pre_u, 1)
            act.wait_ge(pre_w, 1)
            nc.scalar.activation(tmp[:, 5, :], tmp[:, 4, :], ACT.Ln).then_inc(pre_ln, 1)
            act.wait_ge(pre_dec, 1)
            nc.scalar.activation(eacum[:], acum[:, 1, :], ACT.Exp)
            nc.scalar.activation(edec[:], edec[:], ACT.Exp).then_inc(pre_done, 1)

            group(U_S0, 0, 0, core=False)
            with act.Fori(0, 4) as i:
                group(U_S0 + 12, 1 + i, 4 * i, i)

            def gate_b(u, n, i=0):
                for j in range(4):
                    split(u + 4 + j, i=i, per=8)
                act.wait_ge(unit_used, u + 4 + 8 * i)
                if n > 8:
                    act.wait_ge(gate_used, n + i)
                    act.wait_ge(gate_saved, 16 * (n - 8) + 16 * i)
                for q in range(NT):
                    last = nc.scalar.activation(tgate_b[:, q, :], bank[q][:], ACT.Tanh, scale=0.5)
                last.then_inc(evac[0], 1)
                act.wait_ge(evac[0], gates_from(n, i))
                act.dma_start(gate_dram[bass.ds(n - 8 + i, 1), :, :].rearrange("a p c -> (a p) c"), tgate_b[:].rearrange("p a c -> p (a c)")).then_inc(gate_saved, 16)
                for j in range(4):
                    split(u + 8 + j, i=i, per=8)

            gate_b(U_GB, 8)
            with act.Fori(0, 3) as i:
                gate_b(U_GB + 8, 9, i)
            act.wait_ge(gate_saved, 64)
            act.wait_ge(gate_used, 12)
            with act.Fori(0, 3) as i:
                group(U_S5, 5 + i, 4 * i, i)
            split(U_B2 + 4)
            split(U_B2 + 5)
            b_token(7)
            split(U_B2 + 6)
            decay_exp(7, 0)
            split(U_B2 + 7)
            decay_exp(7, 1)
            state(7)
            split(U_B2 + 8)
            split(U_B2 + 9)
            y_hi(7, 12)
            split(U_B2 + 10)
            split(U_B2 + 11)
            for n in range(2, 4):
                if n == 3:
                    transposed_hi(16, ht_hi, None, 0.5, range(0, 4))
                for j in range(3 if n == 3 else 4):
                    split(U_B2 + 4 * n + 4 + j)
            transposed_hi(16, ht_hi, None, 0.5, range(4, 8))

            with act.Fori(0, 2) as i:
                for n in range(2):
                    u = U_OUT + 4 * n
                    for j in range(4):
                        split(u + 3 + j, i=i, per=8)
                    act.wait_ge(unit_used, u + 4 + 8 * i)
                    for q in range(NT):
                        last = nc.scalar.activation(junk_o[:, 0:CH], bank[2 * n + q][:], ACT.Square, accum_out=stat[:, bass.ds(4 * q + n + 2 * i, 1)])
                        act.drain()
                    last.then_inc(mix_sq, 1)
            split(U_UP0 + 3)
            for q in range(NT):
                act.wait_ge(x1_ready, q + 1)
                nc.scalar.activation(junk_o[:], x1[:, q, :], ACT.Square, accum_out=stat[:, 12 + q:13 + q]).then_inc(x1_sq, 1)
                act.drain()
            transposed_hi(24, ht_hi, PRE_FFN)
            act.wait_ge(x1_out, 16)

            def tap(dst, b0, m, first_block):
                for b in range(4):
                    k = 4 * m + first_block + b
                    last = nc.scalar.activation(dst[:, b, :], bank[b0 + b // 2][:, (b % 2) * S:(b % 2 + 1) * S], ACT.Identity,
                                                scale=par[:, bass.ds(FFN_W + 4 * FB + k, 1)], bias=par[:, bass.ds(FFN_B + k, 1)])
                return last

            def up(u, m, kt, i):
                for j in range(4):
                    split(u + 4 + j, i=i, per=8)
                act.wait_ge(unit_used, u + 4 + 8 * i)
                tap(va, 0, m, 0).then_inc(a_tap, 1)
                split(u + 8, i=i, per=8)
                act.wait_ge(a_conv, m + 1)
                nc.scalar.activation(ta[:], va[:], ACT.Square, scale=GELU_CUBE ** 0.5).then_inc(a_sq, 1)
                split(u + 9, i=i, per=8)
                act.wait_ge(a_arg, m + 1)
                nc.scalar.activation(ta[:], ta[:], ACT.Tanh, scale=GELU_SCALE).then_inc(a_tanh, 1)
                split(u + 10, i=i, per=8)
                split(u + 11, i=i, per=8)
                act.wait_ge(unit_used, u + 8 + 8 * i)
                tap(vv, 2, m, FB).then_inc(v_tap, 1)
                act.wait_ge(f_ready, m + 1)
                nc.scalar.mul(ft_hi[:, bass.ds(kt, 4), :], tb[:], 0.5).then_inc(f_hi, 1)

            with act.Fori(0, UP0) as i:
                up(U_UP0, i, 4 * i, i)
            with act.Fori(0, 2) as i:
                for n in range(2):
                    u = U_DOWN0 + UP0 * n
                    for k in range(UP0):
                        split(u + 4 + k, i=i, per=2 * UP0)
                    act.wait_ge(unit_used, u + UP0 + 2 * UP0 * i)
                    for q in range(NT):
                        last = nc.scalar.copy(acc[:, q, bass.ds(1024 * i + 512 * n, CH)], bank[4 + 2 * n + q][:])
                    last.then_inc(evac[2 + n], 1)
            with act.Fori(0, UP1) as i:
                up(U_UP1, i + UP0, 4 * i, i)
            for n in range(4):
                for k in range(UP1):
                    if UP1 * n + k + 4 < U_END - U_DOWN1:
                        split(U_DOWN1 + UP1 * n + 4 + k)
                act.wait_ge(evac[2 + n % 2], (19 if n % 2 == 0 else 4) + n // 2)
                for q in range(NT):
                    last = nc.scalar.activation(junk_f[:], acc[:, q, 512 * n:512 * n + CH], ACT.Square, accum_out=stat[:, 4 * q + n:4 * q + n + 1])
                    act.drain()
                last.then_inc(down_sq, 1)

        @block.vector
        def _(dve):
            def split(u, width=2048, i=0, per=0):
                w = width // 2
                for h in range(2):
                    dve.wait_ge(hi_done, 2 * u + 1 + h + 2 * per * i)
                    nc.vector.tensor_tensor(wlo[:, u % 4, h * w:(h + 1) * w], raw[:, u % 2, 1024 * h:1024 * h + w],
                                            whi[:, u % 4, h * w:(h + 1) * w].bitcast(F32), ALU.subtract).then_inc(lo_done, 1)

            def root(dst, src, n, scale, eps=EPS):
                v, g, w = scr[:, 0:n], scr[:, 8:8 + n], scr[:, 16:16 + n]
                nc.vector.tensor_scalar(v, src, scale, eps, ALU.mult, ALU.add)
                dve.drain()
                nc.vector.tensor_scalar(g.bitcast(I32), v.bitcast(I32), 1, None, ALU.logical_shift_right)
                dve.drain()
                nc.vector.tensor_scalar(dst.bitcast(I32), g.bitcast(I32), -1.0, float(0x5F3759DF), ALU.mult, ALU.add)
                dve.drain()
                for _ in range(3):
                    nc.vector.tensor_tensor(w, dst, dst, ALU.mult)
                    dve.drain()
                    nc.vector.scalar_tensor_tensor(w, w, -0.5, v, ALU.mult, ALU.mult)
                    dve.drain()
                    nc.vector.scalar_tensor_tensor(dst, w, 1.5, dst, ALU.add, ALU.mult)
                    dve.drain()

            def transposed_lo(n0, dst_hi, dst, gain, scale=1.0, groups=range(8)):
                for g in groups:
                    b = tp_bank(n0 + g)
                    dve.wait_ge(tp_hi, n0 + g + 1)
                    for k in range(2):
                        last = nc.vector.scalar_tensor_tensor(
                            dst[:, 2 * g + k, :], b[:, k * S:(k + 1) * S],
                            par[:, gain + 2 * g + k:gain + 2 * g + k + 1] if gain is not None else scale,
                            dst_hi[:, 2 * g + k, :].bitcast(F32), ALU.mult, ALU.subtract)
                    last.then_inc(tp_lo, 1)

            def mem_softmax(h):
                dve.wait_ge(ms_done, h + 1)
                nc.vector.tensor_reduce(stat[:, 0:2], bank[6][:].rearrange("p (q m) -> p q m", q=NT), AX_X, ALU.max)
                dve.drain()
                nc.vector.tensor_scalar(stat[:, 2:4], stat[:, 0:2], -MEM_SCALE, None, ALU.mult).then_inc(mnb, 1)
                dve.wait_ge(mexp, h + 1)
                nc.vector.reciprocal(stat[:, 6:8], stat[:, 4:6])
                dve.drain()
                for q in range(NT):
                    last = nc.vector.tensor_scalar(pmem[:, q, :], pmem[:, q, :], stat[:, 6 + q:7 + q], None, ALU.mult)
                last.then_inc(mprob, 1)

            def mem_probT(h):
                dve.wait_ge(mt_done, h + 1)
                nc.vector.tensor_copy(pmemT[:].rearrange("p a s -> p (a s)"), bank[7][:]).then_inc(mpT, 1)

            def mem_out_lo(h):
                dve.wait_ge(mo_hi, h + 1)
                for n in range(2):
                    last = nc.vector.tensor_tensor(ot_lo[:, bass.ds(4 * h + 2 * n, 2), :], bank[6 + n][:].rearrange("p (b s) -> p b s", b=2),
                                                   ot_hi[:, bass.ds(4 * h + 2 * n, 2), :].bitcast(F32), ALU.subtract)
                last.then_inc(mo_lo, 1)

            def mem_head(u, h, i=0, first=False):
                for j in range(4):
                    split(u + 4 + j, i=i, per=12)
                    if first and j == 1:
                        dve.wait_ge(sq_done, 2)
                        root(stat[:, 14:16], stat[:, 10:12], 2, 1.0 / D)
                        for q in range(NT):
                            last = nc.vector.tensor_scalar(xin[:, q, :], xin[:, q, :], stat[:, 14 + q:15 + q], None, ALU.mult)
                        last.then_inc(norm_done, 1)
                    if not first and j == 0:
                        mem_softmax(h - 1)
                    if not first and j == 2:
                        mem_probT(h - 1)
                dve.wait_ge(unit_used, u + 4 + 12 * i)
                nc.vector.tensor_copy(kmem[:, 2:4, :], bank[1][:].rearrange("p (b s) -> p b s", b=2)).then_inc(evac[0], 1)
                for j in range(4):
                    split(u + 8 + j, i=i, per=12)
                    if first and j < 3:
                        transposed_lo(8, ht_hi, ht_lo, PRE_MIX, groups=X_GROUPS[j])
                    if j == 1 and not first:
                        mem_out_lo(h - 1)
                dve.wait_ge(unit_used, u + 8 + 12 * i)
                nc.vector.tensor_copy(vmem[:, 1, :], bank[3][:]).then_inc(evac[1], 1)
                for j in range(4):
                    split(u + 12 + j, i=i, per=12)
                dve.wait_ge(unit_used, u + 12 + 12 * i)
                nc.vector.tensor_copy(qmem[:, 2:4, :], bank[5][:].rearrange("p (b s) -> p b s", b=2)).then_inc(evac[2], 1)

            dve.wait_ge(consts, 1)
            dve.wait_ge(sq_done, 1)
            root(stat[:, 12:14], stat[:, 8:10], 2, 1.0 / D)
            for q in range(NT):
                last = nc.vector.tensor_scalar(mdiag[:, q, :], ident[:], stat[:, 12 + q:13 + q], None, ALU.mult)
            last.then_inc(norm_done, 1)
            dve.wait_ge(par_done, 1)
            for j in range(4):
                transposed_lo(0, memn_hi, memn_lo, MEM_G, groups=range(2 * j, 2 * j + 2))
                split(j)
            mem_head(0, 0, first=True)
            with dve.Fori(0, MEM_HEADS - 1) as i:
                mem_head(12, 1 + i, i)

            def gated(u, n, cc, i=0, fresh=False, side=(None, None, None, None)):
                for j in range(4):
                    split(u + 4 + j, i=i, per=8)
                    if side[j]:
                        side[j]()
                for j in range(4):
                    split(u + 8 + j, i=i, per=8)
                dve.wait_ge(evac[0], gates_from(n, i))
                dve.wait_ge(unit_used, u + 8 + 8 * i)
                for q in range(NT):
                    m = merged[:, q, bass.ds(cc, CH)]
                    if fresh:
                        last = nc.vector.scalar_tensor_tensor(m, tgate[:, q, :], 1.0, bank[2 + q][:], ALU.add, ALU.mult)
                    else:
                        last = nc.vector.scalar_tensor_tensor(tgate[:, q, :], tgate[:, q, :], 1.0, bank[2 + q][:], ALU.add, ALU.mult)
                last.then_inc(evac[1], 1)
                if fresh:
                    dve.drain().then_inc(gate_used, 1)
                else:
                    dve.drain()
                    for q in range(NT):
                        m = merged[:, q, bass.ds(cc, CH)]
                        last = nc.vector.tensor_tensor(m, m, tgate[:, q, :], ALU.add)
                    last.then_inc(gate_used, 1)

            gated(U_GC, 0, 0, fresh=True, side=(lambda: mem_softmax(3), None, lambda: mem_probT(3), lambda: mem_out_lo(3)))
            with dve.Fori(0, 3) as i:
                gated(U_GC + 8, 1, 512 + 512 * i, i, fresh=True)

            for j in range(4):
                split(U_CKV + j)
            dve.wait_ge(small_hi, 1)
            nc.vector.tensor_tensor(ki_lo[:], bank[0][:, 0:S], ki_hi[:].bitcast(F32), ALU.subtract).then_inc(evac[0], 1)
            nc.vector.memset(score[:], 0.0)
            for j in range(4):
                split(U_QI + j)
            dve.wait_ge(dt_read, 1)
            nc.vector.tensor_scalar(widx[:], bank[4][:, 0:160].rearrange("p (q c) -> p q c", q=NT)[:, :, 0:16],
                                    IDX_W_SCALE, None, ALU.mult).then_inc(evac[0], 1)
            dve.wait_ge(ck_sq, 1)
            dve.wait_ge(kvg_in, 16)
            root(stat[:, 22:24], stat[:, 16:18], 2, 1.0 / RANK)
            for q in range(NT):
                last = nc.vector.scalar_tensor_tensor(ckv[:, q, :], bank[2 + q][:], stat[:, 22 + q:23 + q], kvg[:], ALU.mult, ALU.mult)
            last.then_inc(evac[1], 1)
            dve.wait_ge(ck_hi, 1)
            nc.vector.tensor_tensor(ckv_lo[:], ckv[:], ckv_hi[:].bitcast(F32), ALU.subtract).then_inc(ck_lo, 1)

            SEG = (slice(0, P), slice(P, 384))
            DIAG = (slice(0, P), slice(S, 384))

            def take_eight():
                for q in range(NT):
                    nc.vector.max(scr[:, 8 * q:8 * q + 8], score[:, SEG[q]])
                dve.drain()
                for q in range(NT):
                    nc.vector.match_replace(score[:, SEG[q]], scr[:, 8 * q:8 * q + 8], score[:, SEG[q]], MARK)
                dve.drain()

            def queries_lo(n):
                u = U_QI + 4 * n
                for j in range(3 if n == 7 else 4):
                    split(u + 4 + j, 1024 if n == 7 else 2048)
                    if n == 0 and j == 2:
                        dve.wait_ge(ckT_hi, 1)
                        for b in range(2):
                            last = nc.vector.tensor_tensor(ckvT_lo[:, 2 * b:2 * b + 2, :], bank[6 + b][:].rearrange("p (b s) -> p b s", b=2),
                                                           ckvT_hi[:, 2 * b:2 * b + 2, :].bitcast(F32), ALU.subtract)
                        last.then_inc(ckT_lo, 1)
                    if 1 <= n <= 4:
                        h = 4 * (n - 1) + j
                        dve.wait_ge(relu_done, h + 1)
                        dve.drain()
                        for q in range(NT):
                            last = nc.vector.scalar_tensor_tensor(score[:, SEG[q]], relu[:, h % 2, SEG[q]], widx[:, q, h:h + 1],
                                                                  score[:, SEG[q]], ALU.mult, ALU.add)
                        last.then_inc(relu_used, 1)
                    if n == 5:
                        if j == 0:
                            dve.drain()
                            for d in DIAG:
                                nc.vector.tensor_tensor(score[:, d], score[:, d], causneg[:], ALU.add)
                            dve.drain()
                        for _ in range(TOPK // 8 // 4):
                            take_eight()
                        if j == 3:
                            nc.vector.tensor_scalar(mask[:], score[:], TAKEN, MASKED, ALU.is_ge, ALU.mult)
                            dve.drain()
                            for d in DIAG:
                                nc.vector.tensor_tensor(mask[:, d], mask[:, d], causneg[:], ALU.add)
                            dve.drain()
                if n == 7:
                    key_lo(0)
                dve.wait_ge(q_hi, n + 1)
                for b in range(2):
                    k = slice(2 * b, 2 * b + 2) if n < 4 else slice(4 * (n - 4) + 2 * b, 4 * (n - 4) + 2 * b + 2)
                    hi, lo = (qi_hi[n % 2], qi_lo[n % 2]) if n < 4 else (ot_hi, ot_lo)
                    last = nc.vector.tensor_tensor(lo[:, k, :], bank[2 * (n % 2) + b][:].rearrange("p (b s) -> p b s", b=2),
                                                   hi[:, k, :].bitcast(F32), ALU.subtract)
                last.then_inc(evac[n % 2], 1)
                if n == 7:
                    split(u + 7, 1024)

            def two_banks(hi, lo, n):
                for b in range(2):
                    last = nc.vector.tensor_tensor(lo[:, 2 * b:2 * b + 2, :], bank[n + b][:].rearrange("p (b s) -> p b s", b=2),
                                                   hi[:, 2 * b:2 * b + 2, :].bitcast(F32), ALU.subtract)
                return last

            def key_lo(h):
                dve.wait_ge(at_ql_hi, h + 1)
                two_banks(ql_hi, ql_lo, 0).then_inc(at_ql_lo, 1)

            def out_latent_lo(h):
                dve.wait_ge(at_ol_hi, h + 1)
                two_banks(ol_hi, ol_lo, 4).then_inc(at_ol_lo, 1)

            def out_lo(h):
                dve.wait_ge(at_o_hi, h + 1)
                nc.vector.tensor_tensor(ot_lo[:, bass.ds(h, 1), :].rearrange("p a s -> p (a s)"), bank[6][:, 0:S],
                                        ot_hi[:, bass.ds(h, 1), :].rearrange("p a s -> p (a s)").bitcast(F32), ALU.subtract).then_inc(at_o_lo, 1)

            def attention(h, outs=2, last_head=False):
                dve.wait_ge(at_s, h + 1)
                nc.vector.scalar_tensor_tensor(prob[:], bank[2][:, 0:384], SCALE, mask[:], ALU.mult, ALU.add)
                dve.drain()
                for q in range(NT):
                    last = nc.vector.tensor_reduce(stat[:, 18 + q:19 + q], prob[:, SEG[q]], AX_X, ALU.max, negate=True)
                last.then_inc(at_nb, 1)
                if not last_head:
                    key_lo(h + 1)
                dve.wait_ge(at_exp, h + 1)
                nc.vector.reciprocal(stat[:, 24:26], stat[:, 20:22])
                dve.drain()
                for q in range(NT):
                    last = nc.vector.tensor_scalar(prob[:, SEG[q]], prob[:, SEG[q]], stat[:, 24 + q:25 + q], None, ALU.mult)
                last.then_inc(at_p, 1)
                if outs == 2:
                    out_lo(h - 2)
                if outs >= 1:
                    out_latent_lo(h - 1)
                dve.wait_ge(at_t_hi, h + 1)
                nc.vector.tensor_tensor(pT_lo[:], bank[3][:, 0:384], pT_hi[:].bitcast(F32), ALU.subtract).then_inc(at_t_lo, 1)

            for n in range(8):
                queries_lo(n)
            attention(0, 0)
            attention(1, 1)
            with dve.Fori(0, 3) as i:
                for k in range(4):
                    attention(2 + k + 4 * i)
                    if k % 2 == 0:
                        split(U_ATT + 4 + k, 1024, i, 4)
                        split(U_ATT + 5 + k, 1024, i, 4)
            attention(14)
            split(U_GA)
            attention(15, last_head=True)
            split(U_GA + 1)
            out_lo(14)
            out_latent_lo(15)
            split(U_GA + 2)
            split(U_GA + 3)
            out_lo(15)

            gated(U_GA, 4, 0)
            with dve.Fori(0, 3) as i:
                gated(U_GA + 8, 5, 512 + 512 * i, i)

            def heads(row, g, width):
                return row[:, bass.ds(HPG * g, HPG)].unsqueeze(2).to_broadcast([P, HPG, width])

            def conv_taps(first_block, dst, banks, blocks, tap, done, g):
                dve.wait_ge(tap, g + 1)
                for s in range(1, 4):
                    for b in range(blocks):
                        src = banks[b // 2][:, (b % 2) * S:(b % 2 + 1) * S - s]
                        last = nc.vector.scalar_tensor_tensor(dst[:, b, s:S], src, par[:, bass.ds(CONV_W + (3 - s) * CONV_BLK + first_block[b], 1)],
                                                              dst[:, b, s:S], ALU.mult, ALU.add)
                    if s < 3:
                        dve.drain()
                last.then_inc(done, 1)

            def silu(dst, half, tanh, ready, g):
                dve.wait_ge(tanh, g + 1)
                nc.vector.scalar_tensor_tensor(dst[:], dst[:], 1.0, half[:], ALU.add, ALU.mult).then_inc(ready, 1)

            def core_inputs(g):
                dve.wait_ge(core_in, g + 1)
                for c in range(NT):
                    b = bank[5 + c][:].rearrange("p (h d) -> p h d", h=HPG)
                    nc.vector.tensor_tensor(xdt[:, c, :].rearrange("p (h d) -> p h d", h=HPG), b, heads(dt[:, c, :], g, SHD), ALU.mult)
                    last = nc.vector.tensor_tensor(y[:, c, :].rearrange("p (h d) -> p h d", h=HPG), b, heads(rows[:, 2, :], g, SHD), ALU.mult)
                last.then_inc(core_x, 1)
                dve.drain()
                nc.vector.tensor_tensor(xdd[:].rearrange("p (h d) -> p h d", h=HPG), xdt[:, 0, :].rearrange("p (h d) -> p h d", h=HPG),
                                        heads(edec, g, SHD), ALU.mult)
                dve.wait_ge(core_btok, g + 1)
                nc.vector.tensor_tensor(cb[:], bank[7][:, P:384].rearrange("p (c l) -> p c l", c=NT),
                                        tri[:].unsqueeze(1).to_broadcast([P, NT, P]), ALU.mult).then_inc(core_cb, 1)

            def segment(g, c):
                dve.wait_ge(cum_done, 2 * g + c + 1)
                for n in range(2):
                    nc.vector.tensor_tensor(dec[:, 4 * n:4 * n + 4, :], bank[5 + n][:].rearrange("p (h l) -> p h l", h=4),
                                            acum[:, c, bass.ds(HPG * g + 4 * n, 4)].unsqueeze(2).to_broadcast([P, 4, P]), ALU.subtract)
                dve.drain()
                nc.vector.tensor_scalar(dec[:], dec[:], 0.0, None, ALU.min).then_inc(seg_done, 1)

            def mixing(g, c):
                dve.wait_ge(dec_done, 2 * g + c + 1)
                nc.vector.tensor_tensor(dec[:], dec[:], cb[:, c, :].unsqueeze(1).to_broadcast([P, HPG, P]), ALU.mult).then_inc(m_ready, 1)

            def add_first(g):
                dve.wait_ge(yd_done, 2 * g + 1)
                nc.vector.tensor_tensor(y[:, 0, :], y[:, 0, :], bank[7][:], ALU.add).then_inc(y0_done, 1)

            def add_second(g):
                dve.wait_ge(yoff_done, g + 1)
                nc.vector.tensor_tensor(y[:, 1, :], y[:, 1, :], bank[5][:], ALU.add)
                nc.vector.tensor_tensor(xdd[:].rearrange("p (h d) -> p h d", h=HPG), bank[6][:].rearrange("p (h d) -> p h d", h=HPG),
                                        heads(eacum, g, SHD), ALU.mult)
                dve.drain()
                nc.vector.tensor_tensor(y[:, 1, :], y[:, 1, :], xdd[:], ALU.add)
                dve.drain()

            def gate_and_norm(g):
                nc.vector.tensor_tensor(y[:], y[:], zs[:], ALU.mult)
                dve.drain()
                for c in range(NT):
                    nc.vector.tensor_tensor_reduce(out=xdt[:, c, :], in0=y[:, c, :], in1=y[:, c, :], scale=1.0, scalar=0.0,
                                                   op0=ALU.mult, op1=ALU.add, accum_out=stat[:, 26 + c:27 + c])
                dve.drain()
                root(stat[:, 28:30], stat[:, 26:28], 2, 0.25 / CH)
                for c in range(NT):
                    last = nc.vector.tensor_scalar(y[:, c, :], y[:, c, :], stat[:, 28 + c:29 + c], 0.5, ALU.mult, ALU.mult)
                last.then_inc(y_ready, 1)

            def y_lo(g, kt):
                dve.wait_ge(yT_hi, g + 1)
                for b in range(4):
                    src = bank[7 if b < 2 else 5][:, (b % 2) * S:(b % 2 + 1) * S]
                    last = nc.vector.scalar_tensor_tensor(ot_lo[:, bass.ds(kt + b, 1), :].rearrange("p a s -> p (a s)"), src,
                                                          par[:, bass.ds(SSD_G + 4 * g + b, 1)],
                                                          ot_hi[:, bass.ds(kt + b, 1), :].rearrange("p a s -> p (a s)").bitcast(F32), ALU.mult, ALU.subtract)
                last.then_inc(yT_lo, 1)

            def group(u, g, kt, i=0, core=True):
                split(u + 4, 1024, i, 12)
                split(u + 5, 1024, i, 12)
                if core:
                    core_inputs(g - 1)
                split(u + 6, 1024, i, 12)
                split(u + 7, 1024, i, 12)
                if core:
                    segment(g - 1, 0)
                    mixing(g - 1, 0)
                split(u + 8, 2048, i, 12)
                split(u + 9, 2048, i, 12)
                if core:
                    add_first(g - 1)
                    segment(g - 1, 1)
                    mixing(g - 1, 1)
                split(u + 10, 2048, i, 12)
                split(u + 11, 2048, i, 12)
                conv_taps([4 * g + b for b in range(4)], xv, bank[0:2], 4, x_tap, x_conv, g)
                dve.drain().then_inc(evac[0], 1)
                split(u + 12, 2048, i, 12)
                if core:
                    add_second(g - 1)
                    gate_and_norm(g - 1)
                split(u + 13, 2048, i, 12)
                conv_taps([XBLK + g, XBLK + GROUPS + g], bcv, bank[2:3], 2, bc_tap, bc_conv, g)
                dve.drain().then_inc(evac[1], 1)
                split(u + 14, 2048, i, 12)
                silu(xT, xv, x_tanh, x_ready, g)
                silu(bcT, bcv, bc_tanh, bc_ready, g)
                split(u + 15, 2048, i, 12)
                if core:
                    y_lo(g - 1, kt)
                dve.wait_ge(z_tanh, g + 1)
                for q in range(NT):
                    last = nc.vector.scalar_tensor_tensor(zs[:, q, :], zs[:, q, :], 1.0, bank[3 + q][:], ALU.add, ALU.mult)
                last.then_inc(evac[2], 1)

            dve.wait_ge(row_in, 48)
            two = lambda ap: ap.rearrange("p (q h) -> p q h", q=NT)
            v, r, nv, e, w, ln, d1, eq = (tmp[:, k, :] for k in range(8))
            nc.vector.tensor_tensor(two(v), dt[:], rows[:, 0, :].unsqueeze(1).to_broadcast([P, NT, 64]), ALU.add)
            dve.drain()
            nc.vector.tensor_scalar(r, v, 0.0, None, ALU.max)
            dve.drain()
            nc.vector.scalar_tensor_tensor(nv, r, -2.0, v, ALU.mult, ALU.add).then_inc(pre_n, 1)
            dve.wait_ge(pre_u, 1)
            nc.vector.tensor_scalar(w, e, 1.0, None, ALU.add).then_inc(pre_w, 1)
            dve.drain()
            nc.vector.tensor_scalar(d1, w, -1.0, None, ALU.add)
            dve.drain()
            nc.vector.tensor_scalar(eq, d1, 0.0, None, ALU.is_equal)
            dve.drain()
            nc.vector.tensor_tensor(d1, d1, eq, ALU.add)
            nc.vector.tensor_tensor(eq, eq, e, ALU.mult)
            dve.drain()
            nc.vector.reciprocal(d1, d1)
            dve.drain()
            nc.vector.tensor_tensor(d1, d1, e, ALU.mult)
            dve.drain()
            dve.wait_ge(pre_ln, 1)
            nc.vector.tensor_tensor(ln, ln, d1, ALU.mult)
            nc.vector.tensor_tensor(r, r, eq, ALU.add)
            dve.drain()
            nc.vector.tensor_tensor(dt[:], two(r), two(ln), ALU.add)
            dve.drain()
            nc.vector.scalar_tensor_tensor(da[:], dt[:], -1.0, rows[:, 1, :].unsqueeze(1).to_broadcast([P, NT, 64]), ALU.mult, ALU.mult).then_inc(pre_da, 1)
            dve.wait_ge(pre_cum, 1)
            nc.vector.tensor_copy(acum[:].rearrange("p q h -> p (q h)"), bank[5][:, 0:P])
            dve.drain()
            nc.vector.tensor_tensor(edec[:], bank[6][:, 0:64], acum[:, 0, :], ALU.subtract).then_inc(pre_dec, 1)
            dve.drain().then_inc(yT_lo, 1)
            dve.wait_ge(pre_done, 1)

            group(U_S0, 0, 0, core=False)
            with dve.Fori(0, 4) as i:
                group(U_S0 + 12, 1 + i, 4 * i, i)

            def gate_b(u, n, cc, i=0):
                for j in range(8):
                    split(u + 4 + j, i=i, per=8)
                dve.wait_ge(evac[0], gates_from(n, i))
                dve.wait_ge(unit_used, u + 8 + 8 * i)
                add_gated(2, cc, evac[1])

            def add_gated(b, cc, done):
                for q in range(NT):
                    last = nc.vector.scalar_tensor_tensor(gprod[:, q, :], tgate_b[:, q, :], 1.0, bank[b + q][:], ALU.add, ALU.mult)
                last.then_inc(done, 1)
                dve.drain()
                for q in range(NT):
                    m = merged[:, q, bass.ds(cc, CH)]
                    last = nc.vector.tensor_tensor(m, m, gprod[:, q, :], ALU.add)
                last.then_inc(gate_used, 1)

            gate_b(U_GB, 8, 0)
            with dve.Fori(0, 3) as i:
                gate_b(U_GB + 8, 9, 512 + 512 * i, i)
            dve.drain()
            with dve.Fori(0, 3) as i:
                group(U_S5, 5 + i, 4 * i, i)
            split(U_B2 + 4)
            split(U_B2 + 5)
            core_inputs(7)
            split(U_B2 + 6)
            segment(7, 0)
            mixing(7, 0)
            split(U_B2 + 7)
            add_first(7)
            segment(7, 1)
            mixing(7, 1)
            split(U_B2 + 8)
            add_second(7)
            gate_and_norm(7)
            split(U_B2 + 9)
            y_lo(7, 12)
            for n in range(4):
                if n < 2:
                    split(U_B2 + 10 + n)
                if n == 3:
                    transposed_lo(16, ht_hi, ht_lo, None, 0.5, range(0, 4))
                if n >= 2:
                    for j in range(3 if n == 3 else 4):
                        split(U_B2 + 4 * n + 4 + j)
                dve.wait_ge(unit_used, U_B2 + (7, 8, 12, 16)[n])
                dve.wait_ge(gate_back, 16 * n + 16)
                add_gated(2 * (n % 2), 512 * n, evac[n % 2])
            transposed_lo(16, ht_hi, ht_lo, None, 0.5, range(4, 8))

            dve.wait_ge(grow_in, 16)
            with dve.Fori(0, 2) as i:
                for n in range(2):
                    for j in range(4):
                        split(U_OUT + 4 * n + 3 + j, i=i, per=8)
                    dve.wait_ge(mix_sq, n + 1 + 2 * i)
                    c = bass.ds(512 * n + 1024 * i, CH)
                    for q in range(NT):
                        last = nc.vector.tensor_tensor(mix[:, q, c], bank[2 * n + q][:], grow[:, c], ALU.mult)
                    last.then_inc(evac[n], 1)
            nc.vector.tensor_reduce(stat[:, 8:10], stat[:, 0:8].rearrange("p (q n) -> p q n", q=NT), AX_X, ALU.add)
            dve.drain()
            root(stat[:, 10:12], stat[:, 8:10], 2, 1.0 / D)
            dve.wait_ge(x_again, 16)
            for q in range(NT):
                nc.vector.scalar_tensor_tensor(x1[:, q, :], mix[:, q, :], stat[:, 10 + q:11 + q], x1[:, q, :], ALU.mult, ALU.add).then_inc(x1_ready, 1)
            for q in range(NT):
                dve.wait_ge(x1_sq, q + 1)
                root(stat[:, 14 + q:15 + q], stat[:, 12 + q:13 + q], 1, 1.0 / D)
                nc.vector.tensor_scalar(diag[:, q, :], ident[:], stat[:, 14 + q:15 + q], None, ALU.mult).then_inc(diag_ready, 1)
            split(U_UP0 + 3)
            transposed_lo(24, ht_hi, ht_lo, PRE_FFN)
            dve.drain().then_inc(evac[3], 1)
            dve.wait_ge(x1_out, 16)

            def ffn_taps(dst, b0, m, first_block):
                for s in range(1, 3):
                    for b in range(4):
                        src = bank[b0 + b // 2][:, (b % 2) * S:(b % 2 + 1) * S - s]
                        w = FFN_W + (2 - s) * 2 * FB + 4 * m + first_block + b
                        last = nc.vector.scalar_tensor_tensor(dst[:, b, s:S], src, par[:, bass.ds(w, 1)], dst[:, b, s:S], ALU.mult, ALU.add)
                    if s < 2:
                        dve.drain()
                return last

            def up(u, m, kt, i):
                for j in range(4):
                    split(u + 4 + j, i=i, per=8)
                dve.wait_ge(a_tap, m + 1)
                ffn_taps(va, 0, m, 0).then_inc(a_conv, 1)
                dve.drain().then_inc(evac[0], 1)
                split(u + 8, i=i, per=8)
                dve.wait_ge(a_sq, m + 1)
                nc.vector.scalar_tensor_tensor(ta[:], ta[:], 1.0, va[:], ALU.add, ALU.mult).then_inc(a_arg, 1)
                split(u + 9, i=i, per=8)
                dve.wait_ge(a_tanh, m + 1)
                nc.vector.scalar_tensor_tensor(va[:], ta[:], 1.0, va[:], ALU.add, ALU.mult)
                split(u + 10, i=i, per=8)
                split(u + 11, i=i, per=8)
                dve.wait_ge(v_tap, m + 1)
                ffn_taps(vv, 2, m, FB).then_inc(evac[1], 1)
                dve.drain()
                nc.vector.tensor_tensor(tb[:], va[:], vv[:], ALU.mult).then_inc(f_ready, 1)
                dve.wait_ge(f_hi, m + 1)
                nc.vector.scalar_tensor_tensor(ft_lo[:, bass.ds(kt, 4), :], tb[:], 0.5, ft_hi[:, bass.ds(kt, 4), :].bitcast(F32),
                                               ALU.mult, ALU.subtract).then_inc(f_lo, 1)

            with dve.Fori(0, UP0) as i:
                up(U_UP0, i, 4 * i, i)
            with dve.Fori(0, 2) as i:
                for k in range(2 * UP0):
                    split(U_DOWN0 + 4 + k, i=i, per=2 * UP0)
            with dve.Fori(0, UP1) as i:
                up(U_UP1, i + UP0, 4 * i, i)
            for n in range(4):
                for k in range(UP1):
                    if UP1 * n + k + 4 < U_END - U_DOWN1:
                        split(U_DOWN1 + UP1 * n + 4 + k)
                dve.wait_ge(unit_used, U_DOWN1 + UP1 * n + UP1)
                c = slice(512 * n, 512 * n + CH)
                for q in range(NT):
                    last = nc.vector.tensor_tensor(acc[:, q, c], acc[:, q, c], bank[4 + 2 * (n % 2) + q][:], ALU.add)
                last.then_inc(evac[2 + n % 2], 1)
                if n == 0:
                    dve.wait_ge(x1_in, 32)
                dve.wait_ge(down_sq, n + 1)
                nc.vector.tensor_tensor(acc[:, :, c], acc[:, :, c], frow[:, c].unsqueeze(1).to_broadcast([P, NT, CH]), ALU.mult)
            nc.vector.tensor_reduce(stat[:, 8:10], stat[:, 0:8].rearrange("p (q n) -> p q n", q=NT), AX_X, ALU.add)
            dve.drain()
            root(stat[:, 10:12], stat[:, 8:10], 2, 1.0 / D)
            for n in range(4):
                c = slice(n % 2 * 1024, n % 2 * 1024 + 1024)
                nc.vector.scalar_tensor_tensor(acc[:, n // 2, c], acc[:, n // 2, c], stat[:, 10 + n // 2:11 + n // 2], x1b[:, n // 2, c],
                                               ALU.mult, ALU.add).then_inc(y_out, 1)

        @block.tensor
        def _(pe):
            def products_t(u, banks, mov_hi, mov_lo, kt, first, last, blocks=4, i=0, per=0, width=CH):
                hi = whi[:, u % 4, 0:4 * width].rearrange("p (k c) -> p k c", k=4)
                lo = wlo[:, u % 4, 0:4 * width].rearrange("p (k c) -> p k c", k=4)
                for k in range(4):
                    if k % 2 == 0:
                        pe.wait_ge(lo_done, 2 * u + 1 + k // 2 + 2 * per * i)
                    for b in range(blocks):
                        o = banks[b // 2][:, (b % 2) * S:(b % 2 + 1) * S]
                        c = slice(b * P, (b + 1) * P)
                        for n, (w, m) in enumerate(((hi, mov_hi), (hi, mov_lo), (lo, mov_hi))):
                            mm = nc.tensor.matmul(o, w[:, k, c], m[:, kt + k, :],
                                                  start=first and k == 0 and b % 2 == 0 and n == 0,
                                                  stop=last and k == 3 and n == 2, skip_group_check=True)
                mm.then_inc(unit_used, 1)

            def products(u, banks, sta_hi, sta_lo, kt, first, last, i=0, per=0):
                hi = whi[:, u % 4, :].rearrange("p (k c) -> p k c", k=4)
                lo = wlo[:, u % 4, :].rearrange("p (k c) -> p k c", k=4)
                for k in range(4):
                    if k % 2 == 0:
                        pe.wait_ge(lo_done, 2 * u + 1 + k // 2 + 2 * per * i)
                    for q in range(NT):
                        c = slice(q * P, (q + 1) * P)
                        for n, (s, w) in enumerate(((sta_hi, hi), (sta_hi, lo), (sta_lo, hi))):
                            mm = nc.tensor.matmul(banks[q][:, :], s[:, kt + k, c], w[:, k, :],
                                                  start=first and k == 0 and n == 0,
                                                  stop=last and k == 3 and n == 2, skip_group_check=True)
                mm.then_inc(unit_used, 1)

            def transposes(n0, src, waits, groups=range(8), scale=None):
                for g in groups:
                    if waits and g >= waits:
                        pe.wait_ge(tp_lo, n0 + g - waits + 1)
                    b = tp_bank(n0 + g)
                    for k in range(2):
                        for q in range(NT):
                            o, x = b[:, k * S + q * P:k * S + (q + 1) * P], src[:, q, (2 * g + k) * P:(2 * g + k + 1) * P]
                            if scale is None:
                                mm = nc.tensor.transpose(o, x, ident[:])
                            else:
                                mm = nc.tensor.matmul(o, x, scale[:, q, :], start=True, stop=True)
                    mm.then_inc(tp_done, 1)

            def mem_scores(h, k):
                pe.wait_ge(evac[0], k)
                pe.wait_ge(evac[2], k)
                for q in range(NT):
                    for b in range(4):
                        mm = nc.tensor.matmul(bank[6][:, q * S:(q + 1) * S], qmem[:, b, q * P:(q + 1) * P], kmem[:, b, :],
                                              start=b == 0, stop=b == 3)
                mm.then_inc(ms_done, 1)

            def mem_transpose(h):
                pe.wait_ge(mprob, h + 1)
                for q in range(NT):
                    for m in range(NT):
                        mm = nc.tensor.transpose(bank[7][:, m * S + q * P:m * S + (q + 1) * P],
                                                 pmem[:, q, m * P:(m + 1) * P], ident[:])
                mm.then_inc(mt_done, 1)

            def mem_out(h, k):
                pe.wait_ge(mpT, h + 1)
                pe.wait_ge(evac[1], k)
                for b in range(4):
                    for m in range(NT):
                        mm = nc.tensor.matmul(bank[6 + b // 2][:, (b % 2) * S:(b % 2 + 1) * S],
                                              vmem[:, m, b * P:(b + 1) * P], pmemT[:, m, :], start=m == 0, stop=m == NT - 1)
                mm.then_inc(mo_done, 1)

            def mem_head(u, h, i=0, first=False):
                if not first:
                    pe.wait_ge(evac[0], 2 * h)
                for j in range(4):
                    if first:
                        pe.wait_ge(tp_lo, 2 * j + 2)
                    products_t(u + j, bank[0:2], memn_hi, memn_lo, 4 * j, j == 0, j == 3, i=i, per=12)
                    if first and j == 2:
                        pe.wait_ge(late_par_in, 96)
                        pe.wait_ge(tp_lo, 8)
                        for n, (r, b, c) in enumerate(((96, 2, 0), (96, 2, 96), (88, 3, 0), (88, 3, 88), (88, 3, 176), (88, 3, 264))):
                            mm = nc.tensor.transpose(bank[b][:, c:c + r], stage[0:r, 1 + n, :], ident[0:r, 0:r])
                        mm.then_inc(late_par_tp, 1)
                    if j == 0 and not first:
                        mem_scores(h - 1, 2 * h)
                    if j == 2 and not first:
                        mem_transpose(h - 1)
                if first:
                    pe.wait_ge(late_par_done, 1)
                else:
                    pe.wait_ge(evac[1], 2 * h)
                for j in range(4):
                    products(u + 4 + j, bank[2:4], memn_hi, memn_lo, 4 * j, j == 0, j == 3, i=i, per=12)
                    if j == 0 and first:
                        pe.wait_ge(norm_done, 2)
                    if j < 3 and first:
                        transposes(8, xin, 4, X_GROUPS[j])
                    if j == 0 and not first:
                        mem_out(h - 1, 2 * h)
                if first:
                    pe.wait_ge(tp_lo, 16)
                else:
                    pe.wait_ge(evac[2], 2 * h)
                    pe.wait_ge(mo_lo, h)
                for j in range(4):
                    products_t(u + 8 + j, bank[4:6], ht_hi, ht_lo, 4 * j, j == 0, j == 3, i=i, per=12)

            pe.wait_ge(consts, 1)
            pe.wait_ge(par_in, 80)
            nc.tensor.transpose(bank[0][:, 0:P], stage[:, 0, :], ident[:]).then_inc(par_tp, 1)
            pe.wait_ge(norm_done, 1)
            transposes(0, memin, 6, scale=mdiag)
            pe.wait_ge(par_done, 1)
            mem_head(0, 0, first=True)
            with pe.Fori(0, MEM_HEADS - 1) as i:
                mem_head(12, 1 + i, i)

            def gated(u, e0, e1, sta_hi, sta_lo, kt, i=0, side=(None, None, None, None), ready=None):
                pe.wait_ge(evac[0], e0 + i)
                for j in range(4):
                    products(u + j, bank[0:2], ht_hi, ht_lo, 4 * j, j == 0, j == 3, i=i, per=8)
                    if side[j]:
                        side[j]()
                pe.wait_ge(evac[1], e1 + i)
                if ready:
                    ready()
                for j in range(4):
                    products(u + 4 + j, bank[2:4], sta_hi, sta_lo, kt + 4 * j, j == 0, j == 3, i=i, per=8)

            gated(U_GC, 8, 8, ot_hi, ot_lo, 0,
                  side=(lambda: mem_scores(3, 8), None, lambda: mem_transpose(3), lambda: mem_out(3, 8)),
                  ready=lambda: pe.wait_ge(mo_lo, 4))
            with pe.Fori(0, 3) as i:
                gated(U_GC + 8, 9, 9, ot_hi, ot_lo, 0, i)

            pe.wait_ge(evac[0], 12)
            for j in range(4):
                pe.wait_ge(lo_done, 2 * (U_SMALL + j + 1))
                width = 144 if j < 2 else 64
                for k in range(8):
                    at_k = 1024 * (k // 4) + width * (k % 4)
                    hi, lo = whi[:, j, at_k:at_k + width], wlo[:, j, at_k:at_k + width]
                    kt = 8 * (j % 2) + k
                    first, last = kt == 0, kt == KT - 1
                    for o, c in (((bank[0][:, 0:S], slice(0, P)), (bank[4][0:16, 0:S], slice(P, 144))) if j < 2 else
                                 ((bank[5][0:64, 0:S], slice(0, 64)),)):
                        for n, (w, m) in enumerate(((hi, ht_hi), (hi, ht_lo), (lo, ht_hi))):
                            mm = nc.tensor.matmul(o, w[:, c], m[:, kt, :], start=first and n == 0, stop=last and n == 2)
                mm.then_inc(unit_used, 1)
            pe.wait_ge(evac[1], 12)
            for j in range(4):
                products(U_CKV + j, bank[2:4], ht_hi, ht_lo, 4 * j, j == 0, j == 3)
            pe.wait_ge(small_T, 1)
            for q in range(NT):
                c = slice(q * P, (q + 1) * P)
                nc.tensor.transpose(bank[4][:, 80 * q:80 * q + 16], smallT[0:16, 0, c], ident[0:16, 0:16])
                mm = nc.tensor.transpose(bank[4][:, 80 * q + 16:80 * q + 80], smallT[0:64, 1, c], ident[0:64, 0:64])
            mm.then_inc(small_tok, 1)

            def latent_transpose():
                pe.wait_ge(evac[1], 13)
                for b in range(4):
                    for q in range(NT):
                        mm = nc.tensor.transpose(bank[6 + b // 2][:, (b % 2) * S + q * P:(b % 2) * S + (q + 1) * P],
                                                 ckv[:, q, b * P:(b + 1) * P], ident[:])
                mm.then_inc(ckT_done, 1)

            def index_logits(n, h):
                hi, lo = qi_hi[n % 2], qi_lo[n % 2]
                if h < 2:
                    pe.wait_ge(ckT_lo, 1)
                else:
                    pe.wait_ge(relu_done, h - 1)
                for q, o in enumerate((slice(0, P), slice(P, 384))):
                    for k, (a, b) in enumerate(((hi, ki_hi), (hi, ki_lo), (lo, ki_hi))):
                        mm = nc.tensor.matmul(bank[6 + h % 2][:, o], a[:, h % 4, q * P:(q + 1) * P], b[:, 0:(q + 1) * P],
                                              start=k == 0, stop=k == 2)
                mm.then_inc(idx_done, 1)

            def key_latent(h, hs, i=0):
                u = U_ATT + key_unit(hs // 2)
                pe.wait_ge(lo_done, 2 * (u + 1) + 8 * i)
                c = 512 * (hs % 2)
                for b in range(4):
                    for n, (w, m) in enumerate(((whi, ot_hi), (whi, ot_lo), (wlo, ot_hi))):
                        mm = nc.tensor.matmul(bank[b // 2][:, (b % 2) * S:(b % 2 + 1) * S], w[:, u % 4, c + b * P:c + (b + 1) * P],
                                              m[:, bass.ds(h, 1), :].rearrange("p a s -> p (a s)"), start=n == 0, stop=n == 2)
                if hs % 2:
                    mm.then_inc(unit_used, 1)
                    pe.drain().then_inc(at_ql, 1)
                else:
                    mm.then_inc(at_ql, 1)

            for n in range(8):
                p = n % 2
                pe.wait_ge(evac[p], (14 if p == 0 and n else 13) + n // 2)
                for j in range(4):
                    products_t(U_QI + 4 * n + j, bank[2 * p:2 * p + 2], ht_hi, ht_lo, 4 * j, j == 0, j == 3)
                    if n == 0 and j == 2:
                        latent_transpose()
                    if 1 <= n <= 4:
                        if j == 0:
                            pe.wait_ge(evac[1 - p], (14 if p == 1 else 13) + (n - 1) // 2 + 1)
                        index_logits(n - 1, 4 * (n - 1) + j)
                    if n == 7 and j == 2:
                        pe.wait_ge(evac[0], 18)
                        key_latent(0, 0)

            def logits(h):
                pe.wait_ge(at_ql_lo, h + 1)
                for q, o in enumerate((slice(0, P), slice(P, 384))):
                    for b in range(4):
                        for n, (a, c) in enumerate(((ql_hi, ckvT_hi), (ql_hi, ckvT_lo), (ql_lo, ckvT_hi))):
                            mm = nc.tensor.matmul(bank[2][:, o], a[:, b, q * P:(q + 1) * P], c[:, b, 0:(q + 1) * P],
                                                  start=b == 0 and n == 0, stop=b == 3 and n == 2)
                mm.then_inc(at_s, 1)

            def out_latent(h):
                pe.wait_ge(at_t_lo, h + 1)
                for b in range(4):
                    o = bank[4 + b // 2][:, (b % 2) * S:(b % 2 + 1) * S]
                    for m in range(NT):
                        src = slice(0, S) if m == 0 else slice(S, 384)
                        for n, (c, x) in enumerate(((ckv_hi, pT_hi), (ckv_hi, pT_lo), (ckv_lo, pT_hi))):
                            mm = nc.tensor.matmul(o[:, m * P:S], c[:, m, b * P:(b + 1) * P], x[:, src],
                                                  start=m == 0 and n == 0, stop=m == 1 and n == 2, skip_group_check=True)
                mm.then_inc(at_ol, 1)

            def prob_transpose(h):
                pe.wait_ge(at_p, h + 1)
                for dst, src in ((0, 0), (P, P), (S, S)):
                    mm = nc.tensor.transpose(bank[3][:, dst:dst + P], prob[:, src:src + P], ident[:])
                mm.then_inc(at_t, 1)

            def head_out(h, hs, i=0):
                u = U_ATT + value_unit(hs // 2)
                pe.wait_ge(lo_done, 2 * (u + 1) + 8 * i)
                pe.wait_ge(at_ol_lo, h + 1)
                for b in range(4):
                    c = 512 * (hs % 2) + b * P
                    for n, (w, m) in enumerate(((whi, ol_hi), (whi, ol_lo), (wlo, ol_hi))):
                        mm = nc.tensor.matmul(bank[6][:, 0:S], w[:, u % 4, c:c + P], m[:, b, :], start=b == 0 and n == 0, stop=b == 3 and n == 2)
                if hs % 2:
                    mm.then_inc(unit_used, 1)
                    pe.drain().then_inc(at_o, 1)
                else:
                    mm.then_inc(at_o, 1)

            def attention(h, hs, i=0, outs=2, last_head=False):
                logits(h)
                if not last_head:
                    key_latent(h + 1, hs + 1, i)
                if outs == 2:
                    head_out(h - 2, hs - 2, i)
                if outs >= 1:
                    out_latent(h - 1)
                prob_transpose(h)
                if outs == 2:
                    pe.wait_ge(at_o_lo, h - 1)

            pe.wait_ge(evac[1], 17)
            pe.wait_ge(ck_lo, 1)
            attention(0, 0, outs=0)
            attention(1, 1, outs=1)
            with pe.Fori(0, 3) as i:
                for k in range(4):
                    attention(2 + k + 4 * i, 2 + k, i)
            attention(14, 14)
            attention(15, 15, last_head=True)

            def last_latent():
                head_out(14, 14)
                out_latent(15)

            def last_out():
                pe.wait_ge(at_o_lo, 15)
                head_out(15, 15)

            gated(U_GA, 18, 17, ot_hi, ot_lo, 0, side=(last_latent, last_out, None, None),
                  ready=lambda: pe.wait_ge(at_o_lo, 16))
            with pe.Fori(0, 3) as i:
                gated(U_GA + 8, 19, 18, ot_hi, ot_lo, 0, i)

            def core_transposes(g):
                pe.wait_ge(x_ready, g + 1)
                pe.wait_ge(bc_ready, g + 1)
                pe.wait_ge(yT_lo, g + 1)
                for c in range(NT):
                    for b in range(4):
                        nc.tensor.transpose(bank[5 + c][:, b * P:(b + 1) * P], xT[:, b, c * P:(c + 1) * P], ident[:])
                nc.tensor.transpose(bank[7][:, 0:P], bcT[:, 0, 0:P], ident[:])
                for c in range(NT):
                    mm = nc.tensor.matmul(bank[7][:, P + c * P:2 * P + c * P], bcT[:, 0, c * P:(c + 1) * P], bcT[:, 1, c * P:(c + 1) * P],
                                          start=True, stop=True)
                mm.then_inc(core_in, 1)

            def running_sums(g, c):
                pe.wait_ge(atri_done, 2 * g + c + 1)
                if c == 0:
                    pe.wait_ge(core_x, g + 1)
                else:
                    pe.wait_ge(seg_done, 2 * g + 1)
                for n in range(2):
                    mm = nc.tensor.matmul(bank[5 + n][:], ones[:], atri[:, 4 * n:4 * n + 4, :], start=True, stop=True)
                mm.then_inc(cum_done, 1)

            def diagonal(g, c):
                pe.wait_ge(m_ready, 2 * g + c + 1)
                if c == 0:
                    pe.wait_ge(core_cb, g + 1)
                for h in range(HPG):
                    mm = nc.tensor.matmul(bank[7 if c == 0 else 5][:, h * SHD:(h + 1) * SHD], dec[:, h, :], xdt[:, c, h * SHD:(h + 1) * SHD],
                                          start=True, stop=True)
                mm.then_inc(yd_done, 1)

            def states(g):
                pe.wait_ge(y0_done, g + 1)
                nc.tensor.matmul(bank[7][:], btok[:], xdd[:], start=True, stop=True).then_inc(st_done, 1)

            def from_state(g):
                pe.wait_ge(st_ready, g + 1)
                nc.tensor.matmul(bank[6][:], bcT[:, 1, P:S], hst[:], start=True, stop=True).then_inc(yoff_done, 1)

            def y_transposes(g):
                pe.wait_ge(y_ready, g + 1)
                for b in range(4):
                    for c in range(NT):
                        mm = nc.tensor.transpose(bank[7 if b < 2 else 5][:, (b % 2) * S + c * P:(b % 2) * S + (c + 1) * P],
                                                 y[:, c, b * P:(b + 1) * P], ident[:])
                mm.then_inc(yT_done, 1)

            def group(u, g, e0, e1, e2, i=0, core=True):
                pe.wait_ge(evac[0], e0 + i)
                for j in range(4):
                    products_t(u + j, bank[0:2], ht_hi, ht_lo, 4 * j, j == 0, j == 3, i=i, per=12)
                    if core and j == 1:
                        core_transposes(g - 1)
                    if not core and j == 1:
                        all_sums()
                if core:
                    running_sums(g - 1, 0)
                pe.wait_ge(evac[1], e1 + i)
                for j in range(4):
                    pe.wait_ge(lo_done, 2 * (u + 5 + j) + 24 * i)
                    hi = whi[:, j, 0:1024].rearrange("p (k c) -> p k c", k=8)
                    lo = wlo[:, j, 0:1024].rearrange("p (k c) -> p k c", k=8)
                    for k in range(8):
                        kt = 8 * (j % 2) + k
                        for n, (w, m) in enumerate(((hi, ht_hi), (hi, ht_lo), (lo, ht_hi))):
                            mm = nc.tensor.matmul(bank[2][:, (j // 2) * S:(j // 2 + 1) * S], w[:, k, :], m[:, kt, :],
                                                  start=kt == 0 and n == 0, stop=kt == KT - 1 and n == 2)
                    mm.then_inc(unit_used, 1)
                    if core and j == 2:
                        diagonal(g - 1, 0)
                        running_sums(g - 1, 1)
                if core:
                    states(g - 1)
                pe.wait_ge(evac[2], e2 + i)
                for j in range(4):
                    products(u + 8 + j, bank[3:5], ht_hi, ht_lo, 4 * j, j == 0, j == 3, i=i, per=12)
                    if core and j == 0:
                        diagonal(g - 1, 1)
                        from_state(g - 1)
                if core:
                    y_transposes(g - 1)

            def all_sums():
                pe.wait_ge(pre_da, 1)
                for c in range(NT):
                    nc.tensor.matmul(bank[5][:, 64 * c:64 * c + 64], tri[:], da[:, c, :], start=True, stop=True)
                nc.tensor.matmul(bank[6][:, 0:64], ones[:], da[:, 0, :], start=True, stop=True).then_inc(pre_cum, 1)

            group(U_S0, 0, 22, 21, 8, core=False)
            with pe.Fori(0, 4) as i:
                group(U_S0 + 12, 1 + i, 23, 22, 9, i)

            def halves_ready():
                pe.wait_ge(evac[2], 13)
                pe.wait_ge(yT_lo, 5)

            gated(U_GB, 27, 26, ot_hi, ot_lo, 0, ready=halves_ready)
            with pe.Fori(0, 3) as i:
                gated(U_GB + 8, 28, 27, ot_hi, ot_lo, 0, i)
            with pe.Fori(0, 3) as i:
                group(U_S5, 5 + i, 31, 30, 13, i)
            side = {1: (lambda: core_transposes(7),), 2: (lambda: running_sums(7, 0),),
                    3: (lambda: diagonal(7, 0), lambda: running_sums(7, 1)),
                    4: (lambda: states(7), lambda: diagonal(7, 1), lambda: from_state(7)), 5: (lambda: y_transposes(7),)}
            for n, (c, j) in enumerate(B2_ORDER):
                if j == 0:
                    pe.wait_ge(evac[c % 2], (34, 33, 35, 34)[c])
                    if c == 1:
                        pe.wait_ge(evac[2], 16)
                if n == 6:
                    pe.wait_ge(yT_lo, 9)
                products(U_B2 + n, bank[2 * (c % 2):2 * (c % 2) + 2], ot_hi, ot_lo, 4 * j, j == 0, j == 3)
                for step in side.get(n, ()):
                    step()
                if n in (11, 15):
                    pe.wait_ge(gate_used, 14 if n == 11 else 15)
                    transposes(16, merged, 4, range(0, 4) if n == 11 else range(4, 6))
            pe.wait_ge(evac[0], 36)
            for j in range(4):
                pe.wait_ge(tp_lo, 18 + 2 * j)
                products(U_OUT + j, bank[0:2], ht_hi, ht_lo, 4 * j, j == 0, j == 3)
                if j == 1:
                    pe.wait_ge(gate_used, 16)
                    transposes(16, merged, 4, range(6, 8))
            for n in range(1, 4):
                pe.wait_ge(evac[n % 2], (35, 37, 36)[n - 1])
                for j in range(4):
                    products(U_OUT + 4 * n + j, bank[2 * (n % 2):2 * (n % 2) + 2], ht_hi, ht_lo, 4 * j, j == 0, j == 3)
            pe.wait_ge(evac[0], 38)
            pe.wait_ge(evac[1], 37)
            for q in range(NT):
                pe.wait_ge(diag_ready, q + 1)
                for g in range(8):
                    for k in range(2):
                        mm = nc.tensor.matmul(tp_bank(24 + g)[:, k * S + q * P:k * S + (q + 1) * P], x1[:, q, (2 * g + k) * P:(2 * g + k + 1) * P],
                                              diag[:, q, :], start=True, stop=True)
                    if q == 1:
                        mm.then_inc(tp_done, 1)

            def up(u, e0, e1, i):
                for n in range(2):
                    pe.wait_ge(evac[n], (e0, e1)[n] + i)
                    for j in range(4):
                        if n == 0:
                            pe.wait_ge(tp_lo, 26 + 2 * j)
                        products_t(u + 4 * n + j, bank[2 * n:2 * n + 2], ht_hi, ht_lo, 4 * j, j == 0, j == 3, i=i, per=8)

            with pe.Fori(0, UP0) as i:
                up(U_UP0, 38, 37, i)
            with pe.Fori(0, 2) as i:
                for n in range(2):
                    pe.wait_ge(f_lo, UP0 - 1)
                    pe.wait_ge(evac[2 + n], (16, 1)[n] + i)
                    for k in range(UP0):
                        if k == UP0 - 1:
                            pe.wait_ge(f_lo, UP0)
                        products(U_DOWN0 + UP0 * n + k, bank[4 + 2 * n:6 + 2 * n], ft_hi, ft_lo, 4 * k, k == 0, k == UP0 - 1, i=i, per=2 * UP0)
            with pe.Fori(0, UP1) as i:
                up(U_UP1, 38 + UP0, 37 + UP0, i)
            for n in range(4):
                pe.wait_ge(f_lo, UP0 + UP1 - 1)
                pe.wait_ge(evac[2 + n % 2], (18 if n % 2 == 0 else 3) + n // 2)
                for k in range(UP1):
                    if k == UP1 - 1:
                        pe.wait_ge(f_lo, UP0 + UP1)
                    products(U_DOWN1 + UP1 * n + k, bank[4 + 2 * (n % 2):6 + 2 * (n % 2)], ft_hi, ft_lo, 4 * k, k == 0, k == UP1 - 1)


_INS = ['x', 'mem', 'pre_mix_g', 'w_in', 'kv_norm_g', 'w_uk', 'w_uv', 'ssd_conv_w', 'ssd_conv_b', 'dt_bias', 'a_log',
        'd_skip', 'ssd_norm_g', 'mem_norm_g', 'w_mem_k', 'w_mem_v', 'w_br_a', 'w_br_b', 'w_br_c', 'w_out',
        'post_mix_g', 'pre_ffn_g', 'w_up', 'ffn_conv_w', 'ffn_conv_b', 'w_down', 'post_ffn_g']


def kernel(**inputs):
    import numpy as _np
    import concourse.bacc as _bacc
    from concourse.bass_utils import run_bass_kernel_spmd as _run

    nc = _bacc.Bacc("TRN2", target_bir_lowering=False, num_devices=1)
    arrays, aps = {}, {}
    for name in _INS:
        a = _np.ascontiguousarray(inputs[name])
        arrays[f"in_{name}"] = a
        aps[name] = nc.dram_tensor(f"in_{name}", a.shape, F32, kind="ExternalInput").ap()
    out = nc.dram_tensor("out_x", (1, S, D), F32, kind="ExternalOutput").ap()
    hybrid_layer(nc, aps, out)
    r = _run(nc, [arrays], core_ids=[0])
    return r.results[0]["out_x"]
```
